# Optimizing a Trainium2 kernel written in Bass

```python
import math
import jax
import jax.numpy as jnp
from jax import lax
import numpy as np

D_MODEL = 1024
BATCH = 1
SEQ = 512
DEPTH = 2

QB = 128
NEG_INF = -1e30
BIG = 1e9
NORM_EPS = 1e-6

DIFF_HEADS = 4
DIFF_DH = 64
MLA_HEADS = 4
MLA_NOPE = 128
MLA_ROPE = 64
MLA_VDIM = 128
MLA_Q_LORA = 256
MLA_KV_LORA = 256
ROPE_THETA = 10000.0
FOX_HEADS = 4
FOX_DH = 128
NSA_HEADS = 8
NSA_GROUPS = 2
NSA_HPG = NSA_HEADS // NSA_GROUPS
NSA_DH = 64
CMP_STRIDE = 16
CMP_LEN = 2 * CMP_STRIDE
CMP_HIDDEN = 128
SLC_LEN = 64
SLC_TOPK = 8
WINDOW = 256
N_BRANCH = 4
BRANCH_WIDTH = 512
D_FF = 2816
CONV_WIDTH = 3

IN_WIDTHS = (
    DIFF_HEADS * 2 * DIFF_DH,
    DIFF_HEADS * 2 * DIFF_DH,
    DIFF_HEADS * 2 * DIFF_DH,
    MLA_Q_LORA,
    MLA_KV_LORA,
    MLA_ROPE,
    FOX_HEADS * FOX_DH,
    FOX_HEADS * FOX_DH,
    FOX_HEADS * FOX_DH,
    FOX_HEADS,
    NSA_HEADS * NSA_DH,
    3 * 2 * NSA_GROUPS * NSA_DH,
    3 * NSA_HEADS,
    N_BRANCH * D_MODEL,
)
N_IN = sum(IN_WIDTHS)

kernel_name = 'hybrid_gated_four_mixer_trunk'

def rms_norm(t, g):
    tf = t.astype(jnp.float32)
    y = tf * lax.rsqrt(jnp.mean(tf * tf, axis=-1, keepdims=True) + NORM_EPS)
    return (y * g.astype(jnp.float32)).astype(t.dtype)

def masked_softmax(s, mask):
    p = jax.nn.softmax(jnp.where(mask, s, NEG_INF), axis=-1)
    return jnp.where(mask, p, 0.0)

def alibi_slopes(n):
    return jnp.asarray(np.exp2(-8.0 * np.arange(1, n + 1) / n), dtype=jnp.float32)

def rope(t, pos):
    d = t.shape[-1]
    inv_freq = ROPE_THETA ** (-jnp.arange(0, d, 2, dtype=jnp.float32) / d)
    ang = pos.astype(jnp.float32)[:, None] * inv_freq[None, :]
    cos, sin = jnp.cos(ang), jnp.sin(ang)
    tf = t.astype(jnp.float32)
    t1, t2 = tf[..., : d // 2], tf[..., d // 2:]
    return jnp.concatenate([t1 * cos - t2 * sin, t2 * cos + t1 * sin], axis=-1).astype(t.dtype)

def to_blocks(a, seq_axis):
    seq_axis = seq_axis % a.ndim
    s = a.shape[seq_axis]
    a = a.reshape(a.shape[:seq_axis] + (s // QB, QB) + a.shape[seq_axis + 1:])
    return jnp.moveaxis(a, seq_axis, 0)

def from_blocks(o):
    o = jnp.moveaxis(o, 0, -3)
    return o.reshape(o.shape[:-3] + (o.shape[-3] * o.shape[-2], o.shape[-1]))

def merge_heads(t):
    t = jnp.moveaxis(t, -2, 1)
    return t.reshape(t.shape[0], t.shape[1], -1)

def diff_attention(q, k, v, lam, lam_init, subln_g):
    s, d = q.shape[-2], q.shape[-1]
    slopes = alibi_slopes(q.shape[1])[None, :, None, None, None]
    k_pos = jnp.arange(s)

    def block(args):
        i, qb = args
        q_pos = i * QB + jnp.arange(QB)
        dist = q_pos[:, None] - k_pos[None, :]
        sc = jnp.einsum('bhcqd,bhcsd->bhcqs', qb, k, preferred_element_type=jnp.float32) * d ** -0.5
        sc = sc - slopes * dist.astype(jnp.float32)
        p = masked_softmax(sc, dist >= 0)
        a = p[:, :, 0] - lam * p[:, :, 1]
        return jnp.einsum('bhqs,bhsd->bhqd', a.astype(v.dtype), v)

    o = from_blocks(lax.map(block, (jnp.arange(s // QB), to_blocks(q, -2))))
    return rms_norm(o, subln_g) * (1.0 - lam_init)

def mla_attention(c_q, c_kv, k_rope_in, norm_q, w_uq, norm_kv, w_ukv):
    b, s, _ = c_q.shape
    pos = jnp.arange(s)
    q = (rms_norm(c_q, norm_q) @ w_uq).reshape(b, s, MLA_HEADS, MLA_NOPE + MLA_ROPE).transpose(0, 2, 1, 3)
    q_nope, q_pe = q[..., :MLA_NOPE], rope(q[..., MLA_NOPE:], pos)
    kv = (rms_norm(c_kv, norm_kv) @ w_ukv).reshape(b, s, MLA_HEADS, MLA_NOPE + MLA_VDIM).transpose(0, 2, 1, 3)
    k_nope, v = kv[..., :MLA_NOPE], kv[..., MLA_NOPE:]
    k_pe = rope(k_rope_in, pos)
    scale = (MLA_NOPE + MLA_ROPE) ** -0.5

    def block(args):
        i, qn, qr = args
        q_pos = i * QB + jnp.arange(QB)
        mask = pos[None, :] <= q_pos[:, None]
        sc = (jnp.einsum('bhqd,bhsd->bhqs', qn, k_nope, preferred_element_type=jnp.float32)
              + jnp.einsum('bhqd,bsd->bhqs', qr, k_pe, preferred_element_type=jnp.float32)) * scale
        p = masked_softmax(sc, mask)
        return jnp.einsum('bhqs,bhsd->bhqd', p.astype(v.dtype), v)

    return from_blocks(lax.map(block, (jnp.arange(s // QB), to_blocks(q_nope, -2), to_blocks(q_pe, -2))))

def forgetting_attention(q, k, v, log_f):
    s, d = q.shape[-2], q.shape[-1]
    c = lax.cumsum(log_f, axis=2)
    k_pos = jnp.arange(s)

    def block(args):
        i, qb, cq = args
        q_pos = i * QB + jnp.arange(QB)
        mask = k_pos[None, :] <= q_pos[:, None]
        sc = jnp.einsum('bhqd,bhsd->bhqs', qb, k, preferred_element_type=jnp.float32) * d ** -0.5
        sc = sc + (cq[..., :, None] - c[..., None, :])
        p = masked_softmax(sc, mask)
        return jnp.einsum('bhqs,bhsd->bhqd', p.astype(v.dtype), v)

    return from_blocks(lax.map(block, (jnp.arange(s // QB), to_blocks(q, -2), to_blocks(c, -1))))

def compress(kx, pe, w1, w2):
    b, g, s, d = kx.shape
    ch = kx.reshape(b, g, s // CMP_STRIDE, CMP_STRIDE, d)
    blocks = jnp.concatenate([ch[:, :, :-1], ch[:, :, 1:]], axis=3) + pe
    return jax.nn.gelu(blocks.reshape(b, g, -1, CMP_LEN * d) @ w1) @ w2

def nsa_attention(q, gates, kv, cmp_pe, cmp_w1, cmp_w2):
    b, g, hg, s, d = q.shape
    scale = d ** -0.5
    slopes = alibi_slopes(NSA_HEADS).reshape(g, hg)[None, :, :, None, None]
    k_c = compress(kv[0, 0], cmp_pe[0], cmp_w1[0], cmp_w2[0])
    v_c = compress(kv[0, 1], cmp_pe[1], cmp_w1[1], cmp_w2[1])
    n_c = k_c.shape[2]
    cmp_start = jnp.arange(n_c) * CMP_STRIDE
    cmp_end = cmp_start + CMP_LEN - 1
    n_sel = s // SLC_LEN
    n_topk = min(SLC_TOPK, n_sel)
    sel_start = jnp.arange(n_sel) * SLC_LEN
    overlap = jnp.maximum(
        jnp.minimum(cmp_start[:, None] + CMP_LEN, sel_start[None, :] + SLC_LEN)
        - jnp.maximum(cmp_start[:, None], sel_start[None, :]), 0).astype(jnp.float32) / CMP_LEN
    k_s = kv[1, 0].reshape(b, g, n_sel, SLC_LEN, d)
    v_s = kv[1, 1].reshape(b, g, n_sel, SLC_LEN, d)
    pad = ((0, 0), (0, 0), (WINDOW, 0), (0, 0))
    k_w = jnp.pad(kv[2, 0], pad)
    v_w = jnp.pad(kv[2, 1], pad)
    gather = jax.vmap(jax.vmap(lambda blk, ix: blk[ix]))

    def block(args):
        i, qb, gb = args
        q_pos = i * QB + jnp.arange(QB)
        dist_c = q_pos[:, None] - cmp_end[None, :]
        sc = jnp.einsum('bghqd,bgcd->bghqc', qb, k_c, preferred_element_type=jnp.float32) * scale
        p_c = masked_softmax(sc - slopes * dist_c.astype(jnp.float32), dist_c >= 0)
        o_c = jnp.einsum('bghqc,bgcd->bghqd', p_c.astype(v_c.dtype), v_c)
        imp = jnp.einsum('bghqc,cj->bgqj', p_c, overlap)
        blk = (q_pos // SLC_LEN)[:, None]
        j = jnp.arange(n_sel)[None, :]
        forced = (j == 0) | (j == blk) | (j == blk - 1)
        imp = jnp.where(j > blk, NEG_INF, jnp.where(forced, BIG, imp))
        _, idx = lax.top_k(imp, n_topk)
        k_g = gather(k_s, idx)
        v_g = gather(v_s, idx)
        key_pos = idx[..., None] * SLC_LEN + jnp.arange(SLC_LEN)
        dist_s = (q_pos[:, None, None] - key_pos)[:, :, None]
        sc = jnp.einsum('bghqd,bgqkld->bghqkl', qb, k_g, preferred_element_type=jnp.float32) * scale
        sc = sc - slopes[..., None] * dist_s.astype(jnp.float32)
        p_s = masked_softmax(sc.reshape(b, g, hg, QB, n_topk * SLC_LEN),
                             (dist_s >= 0).reshape(b, g, 1, QB, n_topk * SLC_LEN))
        o_s = jnp.einsum('bghqn,bgqnd->bghqd', p_s.astype(v_g.dtype),
                         v_g.reshape(b, g, QB, n_topk * SLC_LEN, d))
        k_wb = lax.dynamic_slice_in_dim(k_w, i * QB, WINDOW + QB, axis=2)
        v_wb = lax.dynamic_slice_in_dim(v_w, i * QB, WINDOW + QB, axis=2)
        key_pos_w = i * QB - WINDOW + jnp.arange(WINDOW + QB)
        dist_w = q_pos[:, None] - key_pos_w[None, :]
        mask_w = (dist_w >= 0) & (dist_w < WINDOW) & (key_pos_w[None, :] >= 0)
        sc = jnp.einsum('bghqd,bgkd->bghqk', qb, k_wb, preferred_element_type=jnp.float32) * scale
        p_w = masked_softmax(sc - slopes * dist_w.astype(jnp.float32), mask_w)
        o_w = jnp.einsum('bghqk,bgkd->bghqd', p_w.astype(v_wb.dtype), v_wb)
        return gb[..., 0:1] * o_c + gb[..., 1:2] * o_s + gb[..., 2:3] * o_w

    return from_blocks(lax.map(block, (jnp.arange(s // QB), to_blocks(q, -2), to_blocks(gates, -2))))

def token_mixers(h, layer_idx, w_in, diff_lambda, diff_subln, mla_norm_q, mla_w_uq, mla_norm_kv,
                 mla_w_ukv, fox_b_f, nsa_cmp_pe, nsa_cmp_w1, nsa_cmp_w2, w_branch, w_out):
    b, s, _ = h.shape
    proj = h @ w_in
    (a_q, a_k, a_v, b_cq, b_ckv, b_kr, c_q, c_k, c_v, c_f,
     d_q, d_kv, d_g, gate) = jnp.split(proj, np.cumsum(IN_WIDTHS)[:-1].tolist(), axis=-1)

    lam_init = 0.8 - 0.6 * math.exp(-0.3 * layer_idx)
    lf = diff_lambda.astype(jnp.float32)
    lam = jnp.exp(jnp.sum(lf[0] * lf[1])) - jnp.exp(jnp.sum(lf[2] * lf[3])) + lam_init
    qa = a_q.reshape(b, s, DIFF_HEADS, 2, DIFF_DH).transpose(0, 2, 3, 1, 4)
    ka = a_k.reshape(b, s, DIFF_HEADS, 2, DIFF_DH).transpose(0, 2, 3, 1, 4)
    va = a_v.reshape(b, s, DIFF_HEADS, 2 * DIFF_DH).transpose(0, 2, 1, 3)
    y_a = merge_heads(diff_attention(qa, ka, va, lam, lam_init, diff_subln))

    y_b = merge_heads(mla_attention(b_cq, b_ckv, b_kr, mla_norm_q, mla_w_uq, mla_norm_kv, mla_w_ukv))

    def heads(t):
        return t.reshape(b, s, FOX_HEADS, FOX_DH).transpose(0, 2, 1, 3)
    log_f = jax.nn.log_sigmoid((c_f + fox_b_f).astype(jnp.float32)).transpose(0, 2, 1)
    y_c = merge_heads(forgetting_attention(heads(c_q), heads(c_k), heads(c_v), log_f))

    qd = d_q.reshape(b, s, NSA_GROUPS, NSA_HPG, NSA_DH).transpose(0, 2, 3, 1, 4)
    gd = jax.nn.sigmoid(d_g.reshape(b, s, NSA_GROUPS, NSA_HPG, 3)).transpose(0, 2, 3, 1, 4)
    kvd = d_kv.reshape(b, s, 3, 2, NSA_GROUPS, NSA_DH).transpose(2, 3, 0, 4, 1, 5)
    y_d = merge_heads(nsa_attention(qd, gd, kvd, nsa_cmp_pe, nsa_cmp_w1, nsa_cmp_w2))

    ys = jnp.stack([y_a, y_b, y_c, y_d], axis=2)
    branch_out = jnp.einsum('bsnc,ncd->bsnd', ys, w_branch)
    gates = jax.nn.sigmoid(gate.reshape(b, s, N_BRANCH, D_MODEL))
    merged = jnp.einsum('bsnd,bsnd->bsd', gates, branch_out)
    return merged @ w_out

def conv_glu_mlp(h, w_up, conv_w, conv_b, w_down):
    s = h.shape[1]
    u = h @ w_up
    up = jnp.pad(u, ((0, 0), (CONV_WIDTH - 1, 0), (0, 0)))
    u = conv_b + sum(conv_w[k] * up[:, k:k + s] for k in range(CONV_WIDTH))
    a, g = jnp.split(u, 2, axis=-1)
    return (jax.nn.silu(a) * g) @ w_down

def setup_inputs(seed: int = 0) -> dict:
    key = jax.random.key(seed)
    ks = iter(jax.random.split(key, 32))
    L = DEPTH

    def nrm(shape, fan_in):
        return jax.random.normal(next(ks), shape, jnp.float32) * fan_in ** -0.5

    def gain(shape):
        return 1.0 + 0.02 * jax.random.normal(next(ks), shape, jnp.float32)

    def small(shape, scale):
        return scale * jax.random.normal(next(ks), shape, jnp.float32)

    return {
        'x': jax.random.normal(next(ks), (BATCH, SEQ, D_MODEL), jnp.float32),
        'norm_mix': gain((L, D_MODEL)),
        'w_in': nrm((L, D_MODEL, N_IN), D_MODEL),
        'diff_lambda': small((L, 4, DIFF_DH), 0.1),
        'diff_subln': gain((L, 2 * DIFF_DH)),
        'mla_norm_q': gain((L, MLA_Q_LORA)),
        'mla_w_uq': nrm((L, MLA_Q_LORA, MLA_HEADS * (MLA_NOPE + MLA_ROPE)), MLA_Q_LORA),
        'mla_norm_kv': gain((L, MLA_KV_LORA)),
        'mla_w_ukv': nrm((L, MLA_KV_LORA, MLA_HEADS * (MLA_NOPE + MLA_VDIM)), MLA_KV_LORA),
        'fox_b_f': 3.0 + small((L, FOX_HEADS), 0.5),
        'nsa_cmp_pe': small((L, 2, CMP_LEN, NSA_DH), 0.02),
        'nsa_cmp_w1': nrm((L, 2, CMP_LEN * NSA_DH, CMP_HIDDEN), CMP_LEN * NSA_DH),
        'nsa_cmp_w2': nrm((L, 2, CMP_HIDDEN, NSA_DH), CMP_HIDDEN),
        'w_branch': nrm((L, N_BRANCH, BRANCH_WIDTH, D_MODEL), BRANCH_WIDTH),
        'w_out': nrm((L, D_MODEL, D_MODEL), D_MODEL),
        'norm_ffn': gain((L, D_MODEL)),
        'w_up': nrm((L, D_MODEL, 2 * D_FF), D_MODEL),
        'conv_w': nrm((L, CONV_WIDTH, 2 * D_FF), CONV_WIDTH),
        'conv_b': small((L, 2 * D_FF), 0.02),
        'w_down': nrm((L, D_FF, D_MODEL), D_FF),
        'norm_final': gain((D_MODEL,)),
    }

def reference(x, norm_mix, w_in, diff_lambda, diff_subln, mla_norm_q, mla_w_uq, mla_norm_kv, mla_w_ukv,
              fox_b_f, nsa_cmp_pe, nsa_cmp_w1, nsa_cmp_w2, w_branch, w_out, norm_ffn, w_up, conv_w,
              conv_b, w_down, norm_final):
    for l in range(DEPTH):
        h = rms_norm(x, norm_mix[l])
        x = x + token_mixers(h, l, w_in[l], diff_lambda[l], diff_subln[l], mla_norm_q[l], mla_w_uq[l],
                             mla_norm_kv[l], mla_w_ukv[l], fox_b_f[l], nsa_cmp_pe[l], nsa_cmp_w1[l],
                             nsa_cmp_w2[l], w_branch[l], w_out[l])
        h = rms_norm(x, norm_ffn[l])
        x = x + conv_glu_mlp(h, w_up[l], conv_w[l], conv_b[l], w_down[l])
    return rms_norm(x, norm_final)


_drawn_inputs = setup_inputs


def setup_inputs(seed=0):
    import zlib

    import numpy as np

    out = dict(_drawn_inputs(seed))
    spreads = {}
    factors = {'diff_subln': 4.993,
     'mla_norm_q': 8.0,
     'mla_norm_kv': 8.0,
     'nsa_cmp_pe': 8.0,
     'norm_ffn': 2.763,
     'conv_b': 2.866,
     'norm_final': 2.949}
    for name, (base, spread) in spreads.items():
        noise = np.random.default_rng([zlib.crc32(name.encode()), seed]).standard_normal(out[name].shape)
        drawn = base * np.exp(spread * noise) if base else spread * noise
        out[name] = jnp.asarray(drawn.astype(out[name].dtype))
    for name, factor in factors.items():
        out[name] = (out[name] * factor).astype(out[name].dtype)
    return out
```

```python
import math
from contextlib import ExitStack, contextmanager

import numpy as np

import concourse.bass as bass
from concourse import mybir

F32 = mybir.dt.float32
F32R = mybir.dt.float32r
ALU = mybir.AluOpType
ACT = mybir.ActivationFunctionType
AX = mybir.AxisListType

P = 128
S, D, L = 512, 1024, 2
NT = S // P
KD = D // P
TILES = 16
BLK = TILES * P
EPS = 1e-6
NEG = -1e30
BR_A, BR_B, BR_C, BR_D = range(4)
HEADS = 4
NSA_H, NSA_G, NSA_D = 8, 2, 64
NCMP = S // 16 - 1
WIN = 256
FFC = 2816 // P
HALVES = ((0, 12), (12, FFC - 12))
B_A, B_C, B_B, B_D = 0, 6, 12, 16
B_GATE = B_D + 7
B_OUT = B_GATE + 24
B_MLP = B_OUT + 4
NBLK = B_MLP + FFC + 8 * FFC // TILES
STEPS = 8
V_NM, V_NF, V_NQ, V_NKV, V_CONV = 0, 8, 16, 18, 20
V_SW = V_CONV + 4 * 2 * FFC
ROPE = 64
SWC = ROPE + 28
V_W2 = V_SW + KD * SWC
V_PE = V_W2 + P
V_SUB = V_PE + 2 * 16
V_BF = V_SUB + P
NV = V_BF + HEADS
C_ID = 0
C_TRI = C_ID + P
C_ND = C_TRI + S
C_CM = C_ND + S
C_NDW = C_CM + S
C_NDC = C_NDW + 3 * P
C_COS = C_NDC + NT * NCMP
C_SIN = C_COS + S
C_ROT = C_SIN + S
C_ROW = C_ROT + P
C_LAM = C_ROW + NT
NCONST = C_LAM + L


def attention_units():
    units = {b: [] for b in range(4)}
    maps = 0
    for br, heads, parts in ((BR_A, HEADS, 2), (BR_C, HEADS, 1), (BR_B, HEADS, 1), (BR_D, NSA_H, 3)):
        for h in range(heads):
            for part in range(parts):
                blocks = [0] if (br == BR_D and part == 2) else range(NT)
                units[br] += [(br, h, part, i, maps) for i in blocks]
                maps += 1
    return units


class Counts:

    def __init__(self, known=None):
        self.known = known
        self.now, self.base, self.stride, self.total, self.start = {}, {}, {}, {}, {}
        self.loop = None

    def tick(self, name, key=None, by=1):
        self.now[name] = self.now.get(name, 0) + by
        self.base[name, key] = (self.now[name], self.loop)
        return by


class Engine:

    def __init__(self, counts):
        self.c, self.layer, self.turn, self.loop = counts, None, None, None

    def tick(self, name, key=None, by=1):
        return self.c.tick(name, key, by)

    def _value(self, name, n, loop, last=None):
        known = self.c.known
        if known is None:
            return 1
        if loop is not None:
            step = known.stride.get((loop, name), 0)
            if self.loop == loop:
                n = self.turn * step + n if step else n
            else:
                n += step * (known.trips[loop] - 1)
        if self.layer is not None:
            n = self.layer * known.total.get(name, 0) + n
        return n

    def at(self, name, key, off=0):
        if self.c.known is None:
            return 1
        n, loop = self.c.known.base[name, key]
        return self._value(name, n + off, loop)

    def mine(self, name):
        return self._value(name, self.c.now[name], self.loop)

    @contextmanager
    def layers(self, e):
        before = dict(self.c.now)
        with e.Fori(0, L) as i:
            self.layer = i
            yield
        for name, n in self.c.now.items():
            per = n - before.get(name, 0)
            if per:
                self.c.total[name] = per
                self.c.now[name] = n + per * (L - 1)
        self.layer = None

    @contextmanager
    def turns(self, e, loop, trips):
        before = dict(self.c.now)
        self.c.loop = self.loop = loop
        with e.Fori(0, trips) as i:
            self.turn = i
            yield i
        self.c.loop = self.loop = self.turn = None
        self.c.trips[loop] = trips
        for name, n in self.c.now.items():
            step = n - before.get(name, 0)
            if step:
                self.c.stride[loop, name] = step
                self.c.now[name] = n + step * (trips - 1)


def build(nc, blob, vec, const, dlam, nfin, x_in, out, known):
    counts = Counts(known)
    counts.trips = {}
    units = attention_units()
    with ExitStack() as ctx:
        def sem(name):
            return ctx.enter_context(nc.semaphore(name))

        def sb(name, cols, dt=F32):
            return ctx.enter_context(nc.sbuf_tensor(name, [P, cols], dt))

        xT = sb("xT", KD * S)
        h_hi, h_lo = sb("h_hi", KD * S, F32R), sb("h_lo", KD * S, F32R)
        raw = [sb(f"raw{j}", BLK) for j in range(2)]
        w_hi = [sb(f"w_hi{j}", BLK, F32R) for j in range(2)]
        w_lo = [sb(f"w_lo{j}", BLK, F32R) for j in range(2)]
        cst = sb("cst", NCONST)
        vecs = sb("vecs", L * NV)
        nf = sb("nf", KD)
        lsum, rinv, negm = sb("lsum", 16), sb("rinv", 16), sb("negm", 8)
        dgate, fz, neglam = sb("dgate", 4 * 24), sb("fz", 64), sb("neglam", 8)
        epst = sb("epst", 1)
        YT, QKV, WORK = 0, 32768, 32768 + 34816
        base = (nc.sbuf_base + 31) // 32 * 32
        region = sb("region", (WORK + 22528) // 4)
        assert nc.sbuf_base == base + WORK + 22528

        def reg(byte, cols):
            return region[:, byte // 4:byte // 4 + cols]

        def overlay(name, byte, cols):
            return nc.alloc_sbuf_tensor_at(name, [P, cols], F32R, offset=base + byte)

        SP4 = [reg(WORK + 2048 * j, S) for j in range(4)]
        PT2 = [reg(WORK + 8192 + 2048 * j, S) for j in range(2)]
        y = reg(WORK + 12288, NT * S)
        tmp = reg(WORK + 20480, S)
        yT = reg(YT, 16 * S)
        sw_hi = overlay("sw_hi", WORK + 12288, KD * SWC)
        sw_lo = overlay("sw_lo", WORK + 12288 + 4 * KD * SWC, KD * SWC)
        q_, k_, v_ = reg(QKV, 4 * S), reg(QKV + 8192, 4 * S), reg(QKV + 16384, NT * S)
        negc = reg(QKV + 24576, 4 * S)
        bq, bqp, bk = reg(QKV, 4 * S), reg(QKV + 8192, 4 * S), reg(QKV + 16384, 4 * S)
        bv, kpe = reg(QKV + 24576, NT * S), reg(QKV + 32768, S)
        bias_a = reg(QKV + 28672, S)
        nlfb = SP4[3]
        cfl = reg(YT + 3 * 8192, 4 * S)
        cn_hi = [overlay("cq_hi", WORK + 12288, 2 * S), overlay("ckv_hi", YT + 8192, 2 * S)]
        cn_lo = [overlay("cq_lo", WORK + 16384, 2 * S), overlay("ckv_lo", YT + 8192 + 4096, 2 * S)]
        dq, dks, dkw = reg(QKV, 8 * S), reg(QKV + 16384, 2 * S), reg(QKV + 20480, 2 * S)
        dv = reg(QKV + 24576, NT * 256)
        o = QKV + 28672
        bias_s, bias_w, bias_c = reg(o, S), reg(o + 2048, 384), reg(o + 3584, NT * NCMP)
        o += 4080
        kc, vc, w2c, hid = reg(o, 62), reg(o + 248, 128), reg(o + 760, 128), reg(o + 1272, 124)
        NZ = 16 * 2 * NCMP
        z = [reg(WORK, NZ), reg(WORK + 4096, NZ)]
        z_hi = [overlay(f"z_hi{j}", WORK + 12288 + j * 4 * NZ, NZ) for j in range(2)]
        z_lo = [overlay(f"z_lo{j}", YT + 3 * 8192 + j * 4 * NZ, NZ) for j in range(2)]
        y_hi = [overlay(f"y_hi{j}", QKV + 16384 * j, 4 * S) for j in range(2)]
        y_lo = [overlay(f"y_lo{j}", QKV + 16384 * j + 8192, 4 * S) for j in range(2)]
        merged = reg(WORK, KD * S)
        sg = [reg(WORK + 16384 + 2048 * j, S) for j in range(2)]
        m_hi, m_lo = overlay("m_hi", YT, KD * S), overlay("m_lo", YT + 16384, KD * S)
        a_hi, a_lo = overlay("a_hi", 0, 12 * S), overlay("a_lo", 24576, 12 * S)
        ua = [reg(WORK + 2048 * j, S) for j in range(2)]
        ug = [reg(WORK + 4096 + 2048 * j, S) for j in range(2)]
        us = [reg(WORK + 8192 + 2048 * j, S) for j in range(2)]
        uf = [reg(WORK + 12288 + 2048 * j, S) for j in range(2)]
        stage = reg(0, NT * D)

        ps = ctx.enter_context(nc.psum_tensor("ps", [P, 8, S], F32))

        ident = cst[:, C_ID:C_ID + P]
        tri = cst[:, C_TRI:C_TRI + S]
        ones = cst[:, C_TRI + P:C_TRI + 2 * P]
        rot = cst[:, C_ROT:C_ROT + P]
        cos, sin = cst[:, C_COS:C_COS + S], cst[:, C_SIN:C_SIN + S]

        landed = [sem(f"block_landed{j}") for j in range(2)]
        hi_done = sem("hi_done")
        lo_done = sem("lo_done")
        gemm_steps = sem("gemm_steps")
        misc_ready = sem("misc_ready")
        out_free = sem("out_free")
        f_ready = sem("f_ready")
        f_hi = sem("f_hi")
        f_split = sem("f_split")
        sq_ready = sem("sq_ready")
        act_ready = sem("act_ready")
        dve_chain = sem("dve_chain")
        act_chain = sem("act_chain")
        s_ready = sem("s_ready")
        sb_ready = sem("sb_ready")
        p_ready = sem("p_ready")
        t_ready = sem("t_ready")
        pt_ready = sem("pt_ready")
        pv_done = sem("pv_done")
        o_free = sem("o_free")
        loaded = sem("loaded")
        x_in_s = sem("x_in_s")
        stored = sem("stored")
        out_ready = sem("out_ready")

        block = ctx.enter_context(nc.Block())

        def wt(b, t):
            s, c = (b + t // TILES) % 2, t % TILES * P
            return w_hi[s][:, c:c + P], w_lo[s][:, c:c + P]

        def bank(en, key):
            n = 1 if en.c.known is None else en.c.known.base["out_free", key][0] - 4
            return (n - 1) % 4

        @block.sync
        def _(sp):
            sp.dma_start(stage.rearrange("p (t d) -> p t d", t=NT), x_in.rearrange("(t p) d -> p t d", p=P)).then_inc(x_in_s, 16)
            sp.dma_start(cst[:], const).then_inc(x_in_s, 16)
            sp.dma_start(raw[0][:], blob[0]).then_inc(landed[0], 16)
            sp.dma_start(raw[1][:], blob[1]).then_inc(landed[1], 16)
            with sp.Fori(1, L * NBLK // 2) as i:
                for j in range(2):
                    sp.wait_ge(lo_done, i * 2 + (j - 1))
                    sp.dma_start(raw[j][:], blob[i * 2 + j]).then_inc(landed[j], 16)
            for j in range(2):
                sp.wait_ge(lo_done, L * NBLK + j - 1)
                sp.dma_start(raw[j][:], blob[j]).then_inc(landed[j], 16)
            for t in range(NT):
                sp.wait_ge(out_ready, 2 * (t + 1))
                sp.dma_start(out[t * P:(t + 1) * P, :], stage[:, t * D:(t + 1) * D]).then_inc(stored, 16)
            sp.wait_ge(stored, 16 * NT)

        @block.gpsimd
        def _(pool):
            with pool.Fori(0, L * NBLK // 2 + 1) as i:
                for j in range(2):
                    pool.wait_ge(hi_done, i * 2 + (j + 1))
                    pool.tensor_tensor(w_lo[j][:], raw[j][:], w_hi[j][:].bitcast(F32), ALU.subtract).then_inc(lo_done, 1)

        @block.scalar
        def _(act):
            en = Engine(counts)
            tick, at = en.tick, en.at
            A = nc.scalar.activation

            def split_block(b):
                if b >= 2:
                    n = STEPS * (b - 1)
                    act.wait_ge(gemm_steps, at_block(n))
                slot = b % 2
                g = b // 2
                g = en.layer * (NBLK // 2) + g if en.layer is not None else g
                if en.loop is not None:
                    g = en.turn * (en.loop_blocks // 2) + g
                act.wait_ge(landed[slot], g * 16 + 16)
                A(w_hi[slot][:], raw[slot][:], ACT.Copy).then_inc(hi_done, 1)

            def at_block(n):
                if en.loop is not None:
                    n = en.turn * (en.loop_blocks * STEPS) + n
                return en.layer * (NBLK * STEPS) + n

            def blocks(b, n):
                for j in range(b, b + n):
                    split_block(j + 2)

            def split_hi(dst, src, key, wait=None):
                if wait is None:
                    act.wait_ge(f_ready, at("f_ready", key))
                A(dst, src, ACT.Copy).then_inc(f_hi, tick("f_hi", key))

            def rms_root(key, n, bank_key):
                act.wait_ge(misc_ready, at("misc_ready", bank_key))
                A(SP4[2], ps[:, bank(en, bank_key), :], ACT.Sqrt, bias=epst[:, 0:1], scale=1.0 / n).then_inc(
                    act_ready, tick("act_ready", key))

            def norm(key):
                for k in range(KD):
                    act.wait_ge(out_free, at("out_free", key, k - KD))
                    if k >= 2:
                        act.wait_ge(misc_ready, at("misc_ready", (key, k - 2)))
                    A(SP4[k % 2], xT[:, k * S:(k + 1) * S], ACT.Square).then_inc(sq_ready, tick("sq_ready", (key, k)))
                rms_root((key, "root"), D, key)

            def attend(br):
                us_ = units[br]
                for n, (_, h, part, i, m) in enumerate(us_):
                    u = (br, n)
                    sbuf, w = SP4[n % 4], unit_width(br, part, i)
                    act.wait_ge(sb_ready, at("sb_ready", u))
                    if part == 2 and br == BR_D:
                        A(sbuf[:, 0:w], sbuf[:, 0:w], ACT.Exp).then_inc(p_ready, tick("p_ready", u))
                    else:
                        A(sbuf[:, 0:w], sbuf[:, 0:w], ACT.Exp, scale=-1.0, bias=negm[:, n % 8:n % 8 + 1],
                          accum_out=lsum[:, m % 4 * 4 + i:m % 4 * 4 + i + 1]).then_inc(p_ready, tick("p_ready", u))
                    if n >= 1:
                        spread(br, n - 1)
                spread(br, len(us_) - 1)

            def spread(br, n):
                _, h, part, i, m = units[br][n]
                act.wait_ge(t_ready, at("t_ready", (br, n)))
                if n >= 2:
                    act.wait_ge(pv_done, at("pv_done", (br, n), -2))
                if br == BR_D and part == 2:
                    src, dst = ps[0:NCMP, 4 + n % 2, 0:S], PT2[n % 2][0:NCMP, :]
                else:
                    w = unit_width(br, part, i)
                    src, dst = ps[:, 4 + n % 2, 0:w], PT2[n % 2][:, 0:w]
                A(dst, src, ACT.Copy).then_inc(pt_ready, tick("pt_ready", (br, n)))

            act.dma_start(vecs[:].rearrange("p (l v) -> p l v", l=L), vec.rearrange("l p v -> p l v")).then_inc(loaded, 16)
            act.dma_start(y[:, 0:L * 256], dlam).then_inc(loaded, 16)
            act.dma_start(nf[:], nfin).then_inc(loaded, 16)
            act.wait_ge(landed[0], 16)
            A(w_hi[0][:], raw[0][:], ACT.Copy).then_inc(hi_done, 1)
            act.wait_ge(landed[1], 16)
            A(w_hi[1][:], raw[1][:], ACT.Copy).then_inc(hi_done, 1)
            act.wait_ge(f_ready, at("f_ready", "lam"))
            A(neglam[:, 4:8], neglam[:, 4:8], ACT.Exp).then_inc(act_ready, tick("act_ready", "lam"))

            with en.layers(act):
                norm("n1")
                for k in range(KD):
                    split_hi(h_hi[:, k * S:(k + 1) * S], PT2[k % 2], ("n1", k))
                split_hi(sw_hi[:], vecs_slice(vecs, en.layer, V_SW, KD * SWC), "sw", wait=False)
                act.wait_ge(f_ready, at("f_ready", "tok"))
                A(dgate[:], dgate[:], ACT.Sigmoid).then_inc(act_ready, tick("act_ready", "dgate"))
                A(fz[:, 16:32], fz[:, 16:32], ACT.Exp, scale=-1.0).then_inc(act_chain, tick("act_chain"))
                act.wait_ge(act_chain, en.mine("act_chain"))
                A(fz[:, 16:32], fz[:, 16:32], ACT.Ln, bias=ones[:, 0:1]).then_inc(act_ready, tick("act_ready", "flog"))
                blocks(B_A, 6)
                attend(BR_A)
                act.wait_ge(f_ready, at("f_ready", "subln"))
                A(fz[:, 32:48], fz[:, 32:48], ACT.Sqrt, bias=epst[:, 0:1], scale=1.0 / P).then_inc(
                    act_ready, tick("act_ready", "subln"))
                blocks(B_C, 6)
                attend(BR_C)
                blocks(B_B, 2)
                for j, key in enumerate(("cq", "ckv")):
                    for c in range(2):
                        act.wait_ge(out_free, at("out_free", (key, c)))
                        if j:
                            act.wait_ge(misc_ready, at("misc_ready", ("cq", "n", c)))
                        A(SP4[c], cfl[:, (2 * j + c) * S:(2 * j + c + 1) * S], ACT.Square).then_inc(
                            sq_ready, tick("sq_ready", (key, c)))
                    act.wait_ge(misc_ready, at("misc_ready", (key, "n")))
                    if j:
                        act.wait_ge(f_split, at("f_split", ("cq", 1)))
                    A(SP4[2], ps[:, bank(en, (key, "n")), :], ACT.Sqrt, bias=epst[:, 0:1], scale=1.0 / 256).then_inc(
                        act_ready, tick("act_ready", (key, "root")))
                    for c in range(2):
                        split_hi(cn_hi[j][:, c * S:(c + 1) * S], PT2[c], (key, c))
                blocks(B_B + 2, 2)
                attend(BR_B)
                blocks(B_D, 5)
                for j in range(2):
                    split_hi(z_hi[j][:], z[j], ("z", j))
                blocks(B_D + 5, 2)
                act.wait_ge(f_ready, at("f_ready", "hid"))
                A(hid, hid, ACT.Gelu_apprx_tanh).then_inc(act_ready, tick("act_ready", "hid"))
                attend(BR_D)
                en.loop_blocks = 12
                with en.turns(act, "gate", 2) as g:
                    for j in range(2):
                        for c in range(4):
                            act.wait_ge(out_free, at("out_free", ("yT", BR_D, 3)))
                            act.wait_ge(gemm_steps, at("gemm_steps", ("gate", j, 7, 1), -12 * STEPS))
                            A(y_hi[j][:, c * S:(c + 1) * S], yT[:, bass.ds((g * 2 + j) * 4 * S + c * S, S)], ACT.Copy).then_inc(
                                f_hi, tick("f_hi", ("y", j, c)))
                        done = j * 6
                        for dt in range(8):
                            act.wait_ge(gemm_steps, at("gemm_steps", ("gate", j, dt, 0)))
                            act.wait_ge(f_ready, at("f_ready", ("mul", j, dt), -2))
                            A(sg[dt % 2], ps[:, bank(en, ("gate", j, dt, 0)), :], ACT.Sigmoid).then_inc(
                                act_ready, tick("act_ready", ("sg", j, dt)))
                            while (done + 1 - j * 6) * TILES <= 12 * (dt + 1):
                                split_block(B_GATE + done + 2)
                                done += 1
                for k in range(KD):
                    act.wait_ge(out_free, at("out_free", ("gate", 1, k, 1)))
                    A(m_hi[:, k * S:(k + 1) * S], merged[:, k * S:(k + 1) * S], ACT.Copy).then_inc(
                        f_hi, tick("f_hi", ("m", k)))
                blocks(B_OUT, 4)
                norm("n2")
                for k in range(KD):
                    split_hi(h_hi[:, k * S:(k + 1) * S], PT2[k % 2], ("n2", k))
                b = B_MLP
                for half, (c0, nch) in enumerate(HALVES):
                    en.loop_blocks = 2
                    with en.turns(act, ("up", half), nch // 2) as g:
                        for j in range(2):
                            for part, dst in ((0, ua[j]), (1, ug[j])):
                                act.wait_ge(gemm_steps, at("gemm_steps", ("up", half, j, part)))
                                act.wait_ge(f_ready, at("f_ready", ("act", half, j), -4))
                                cv = V_CONV + (part * FFC + c0 + j) * 4
                                A(dst, ps[:, bank(en, ("up", half, j, part)), :], ACT.Identity,
                                  bias=col(vecs, en.layer, cv + 3, g, 8), scale=col(vecs, en.layer, cv + 2, g, 8)).then_inc(
                                    act_ready, tick("act_ready", ("up", half, j, part)))
                            split_block(b + j + 2)
                            act.wait_ge(f_ready, at("f_ready", ("conv", half, j)))
                            A(us[j], ua[j], ACT.Silu).then_inc(act_ready, tick("act_ready", ("silu", half, j)))
                            act.wait_ge(f_ready, at("f_ready", ("act", half, j)))
                            A(a_hi[:, bass.ds((g * 2 + j) * S, S)], uf[j], ACT.Copy).then_inc(
                                f_hi, tick("f_hi", ("act", half, j)))
                    b += nch
                    blocks(b, nch // 2)
                    b += nch // 2
            norm("n3")

        @block.vector
        def _(dve):
            en = Engine(counts)
            tick, at = en.tick, en.at
            V = nc.vector

            def link(ins):
                ins.then_inc(dve_chain, tick("dve_chain"))
                dve.wait_ge(dve_chain, en.mine("dve_chain"))

            def lo_part(dst, src, hi, key):
                dve.wait_ge(f_hi, at("f_hi", key))
                V.tensor_tensor(dst, src, hi.bitcast(F32), ALU.subtract).then_inc(f_split, tick("f_split", key))

            def evac(key, dst, scale=1.0, srcs=None, ready="gemm_steps"):
                sem_ = {"gemm_steps": gemm_steps, "misc_ready": misc_ready}[ready]
                dve.wait_ge(sem_, at(ready, key))
                src = ps[:, bank(en, key), :]
                parts = [(dst, src)] if srcs is None else [(d, f(src)) for d, f in srcs]
                for n, (d, s) in enumerate(parts):
                    ins = V.tensor_scalar(d, s, scale, None, ALU.mult)
                    if n == len(parts) - 1:
                        ins.then_inc(out_free, tick("out_free", key))

            def normalise(key, nk, src, gain, dsts):
                dve.wait_ge(act_ready, at("act_ready", (key, "root")))
                V.reciprocal(SP4[3], SP4[2]).then_inc(out_free, tick("out_free", key if nk == KD else (key, "n")))
                dve.wait_ge(out_free, en.mine("out_free"))
                for k in range(nk + 1):
                    if k < nk:
                        if k >= 2 or nk < KD:
                            dve.wait_ge(f_split, en.mine("f_split"))
                        V.scalar_tensor_tensor(PT2[k % 2], src(k), gain(k), SP4[3], ALU.mult, ALU.mult).then_inc(
                            f_ready, tick("f_ready", (key, k)))
                    if k >= 1:
                        hi, lo = dsts(k - 1)
                        lo_part(lo, PT2[(k - 1) % 2], hi, (key, k - 1))

            def attend(br):
                us_ = units[br]
                ends = {}
                for n, (_, h, part, i, m) in enumerate(us_):
                    if n + 1 == len(us_) or us_[n + 1][4] != m:
                        ends[n] = (h, part, m)
                for n in range(len(us_) + 3):
                    if n < len(us_):
                        piece(br, n)
                    if n - 3 in ends:
                        map_out(br, n - 3, *ends[n - 3])
                if br == BR_A:
                    subln()
                for c in range(4):
                    key = ("yT", br, c)
                    evac(key, yT[:, (br * 4 + c) * S:(br * 4 + c + 1) * S], ready="misc_ready")

            def wait_last_piece(n):
                if n:
                    dve.wait_ge(sb_ready, en.mine("sb_ready"))

            def piece(br, n):
                _, h, part, i, m = units[br][n]
                first = i == 0
                if br == BR_A and part == 0 and first:
                    wait_last_piece(n)
                    link(V.tensor_scalar(bias_a, cst[:, C_ND:C_ND + S], 2.0 ** (-8.0 * (h + 1) / HEADS), None, ALU.mult))
                if br == BR_D and part == 0 and first:
                    slope = 2.0 ** (-8.0 * (h + 1) / NSA_H)
                    wait_last_piece(n)
                    V.tensor_scalar(bias_s, cst[:, C_ND:C_ND + S], slope, None, ALU.mult).then_inc(dve_chain, tick("dve_chain"))
                    V.tensor_scalar(bias_w, cst[:, C_NDW:C_NDW + 384], slope, None, ALU.mult).then_inc(dve_chain, tick("dve_chain"))
                    link(V.tensor_scalar(bias_c, cst[:, C_NDC:C_NDC + NT * NCMP], slope, None, ALU.mult))
                w = unit_width(br, part, i)
                dst, src = SP4[n % 4][:, 0:w], ps[:, n % 4, 0:w]
                dve.wait_ge(s_ready, at("s_ready", (br, n)))
                if n >= 4:
                    dve.wait_ge(t_ready, at("t_ready", (br, n), -4))
                if br == BR_D and part == 2:
                    cm = negm_c
                    link(V.tensor_tensor(dst, src, bias_c, ALU.add))
                    d3 = dst.rearrange("p (t c) -> p t c", t=NT)
                    link(V.tensor_reduce(cm, d3, AX.X, ALU.max))
                    V.tensor_tensor(d3, d3, cm.rearrange("p (t o) -> p t o", o=1).to_broadcast([P, NT, NCMP]), ALU.subtract).then_inc(
                        sb_ready, tick("sb_ready", (br, n)))
                    return
                if br == BR_A:
                    bias = bias_a[:, S - w:S]
                elif br == BR_B:
                    bias = cst[:, C_CM + S - w:C_CM + S]
                elif br == BR_C:
                    bias = negc[:, h * S:h * S + w]
                elif part == 0:
                    bias = bias_s[:, S - w:S]
                else:
                    bias = bias_w[:, 384 - w:384]
                dve.sem_inc(dve_chain, tick("dve_chain"))
                V.tensor_tensor_reduce(dst, src, bias, -1.0, 3e38, ALU.add, ALU.min, negm[:, n % 8:n % 8 + 1]).then_inc(
                    sb_ready, tick("sb_ready", (br, n)))

            negm_c = fz[:, 48:52]

            def map_out(br, n, h, part, m):
                r = rinv[:, m % 4 * 4:m % 4 * 4 + 4]
                ls = lsum[:, m % 4 * 4:m % 4 * 4 + 4]
                dve.wait_ge(p_ready, at("p_ready", (br, n)))
                if br == BR_D and part == 2:
                    pc = SP4[n % 4][:, 0:NT * NCMP].rearrange("p (t c) -> p t c", t=NT)
                    link(V.tensor_reduce(ls, pc, AX.X, ALU.add))
                link(V.reciprocal(r, ls))
                if br == BR_A and part == 1:
                    link(V.tensor_scalar(r, r, neglam[:, bass.ds(en.layer, 1)], None, ALU.mult))
                if br == BR_D:
                    g = dgate[:].rearrange("p (t c) -> p t c", t=NT)[:, :, 3 * h + (1, 2, 0)[part]]
                    link(V.tensor_tensor(r, r, g, ALU.mult))
                    if part == 2:
                        link(V.tensor_tensor(r, r, cst[:, C_ROW:C_ROW + NT], ALU.mult))
                wd = NSA_D if br == BR_D else P
                ob = ps[:, 6 + m % 2, 0:NT * wd].rearrange("p (t d) -> p t d", t=NT)
                rb = r.rearrange("p (t o) -> p t o", o=1).to_broadcast([P, NT, wd])
                yh = y.rearrange("p (t d) -> p t d", t=NT)[:, :, h * wd:(h + 1) * wd]
                dve.wait_ge(pv_done, at("pv_done", (br, n)))
                if part == 0:
                    V.tensor_tensor(yh, ob, rb, ALU.mult).then_inc(o_free, tick("o_free", m))
                    dve.wait_ge(o_free, en.mine("o_free"))
                else:
                    t3 = tmp[:, 0:NT * wd].rearrange("p (t d) -> p t d", t=NT)
                    V.tensor_tensor(t3, ob, rb, ALU.mult).then_inc(o_free, tick("o_free", m))
                    dve.wait_ge(o_free, en.mine("o_free"))
                    link(V.tensor_tensor(yh, yh, t3, ALU.add))
                if n == len(units[br]) - 1 and br != BR_A:
                    dve.sem_inc(f_ready, tick("f_ready", ("y", br)))

            def subln():
                y4 = y.rearrange("p (t h d) -> p t h d", t=NT, h=HEADS)
                for h in range(HEADS):
                    t3 = tmp.rearrange("p (t d) -> p t d", t=NT)
                    link(V.tensor_tensor(t3, y4[:, :, h, :], y4[:, :, h, :], ALU.mult))
                    ins = V.tensor_reduce(fz[:, 32 + 4 * h:36 + 4 * h], t3, AX.X, ALU.add)
                    if h < HEADS - 1:
                        link(ins)
                    else:
                        ins.then_inc(f_ready, tick("f_ready", "subln"))
                dve.wait_ge(act_ready, at("act_ready", "subln"))
                link(V.reciprocal(fz[:, 32:48], fz[:, 32:48]))
                link(V.tensor_scalar(fz[:, 32:48], fz[:, 32:48], neglam[:, bass.ds(en.layer + L, 1)], None, ALU.mult))
                g = vecs_slice(vecs, en.layer, V_SUB, P)
                for h in range(HEADS):
                    r = fz[:, 32 + 4 * h:36 + 4 * h].rearrange("p (t o) -> p t o", o=1).to_broadcast([P, NT, P])
                    link(V.tensor_tensor(y4[:, :, h, :], y4[:, :, h, :], r, ALU.mult))
                    gb = g.rearrange("p (o d) -> p o d", o=1).to_broadcast([P, NT, P])
                    ins = V.tensor_tensor(y4[:, :, h, :], y4[:, :, h, :], gb, ALU.mult)
                    if h < HEADS - 1:
                        link(ins)
                    else:
                        ins.then_inc(f_ready, tick("f_ready", ("y", BR_A)))

            def rotary(raw_t, rot_key, dsts, rows=P):
                link(V.tensor_tensor(SP4[1][0:rows, :], raw_t[0:rows, :], cos[0:rows, :], ALU.mult))
                dve.wait_ge(misc_ready, at("misc_ready", rot_key))
                V.tensor_tensor(SP4[2][0:rows, :], ps[0:rows, bank(en, rot_key), :], sin[0:rows, :], ALU.mult).then_inc(out_free, tick("out_free", rot_key))
                dve.wait_ge(out_free, en.mine("out_free"))
                for d, part in dsts:
                    link(V.tensor_tensor(d, SP4[1][part, :], SP4[2][part, :], ALU.add))

            def add_out(key, k, src_sem="gemm_steps"):
                dve.wait_ge(gemm_steps, at("gemm_steps", key))
                xk = xT[:, k * S:(k + 1) * S]
                V.tensor_tensor(xk, ps[:, bank(en, key), :], xk, ALU.add).then_inc(out_free, tick("out_free", key))

            def norm(key, gain):
                normalise(key, KD, lambda k: xT[:, k * S:(k + 1) * S], gain,
                          lambda k: (h_hi[:, k * S:(k + 1) * S], h_lo[:, k * S:(k + 1) * S]))

            dve.sem_inc(out_free, tick("out_free", "credit", 4))
            dve.sem_inc(o_free, tick("o_free", "credit", 2))
            V.memset(epst[:], EPS).then_inc(dve_chain, tick("dve_chain"))
            dve.wait_ge(dve_chain, en.mine("dve_chain"))
            dve.wait_ge(loaded, 48)
            dve.wait_ge(x_in_s, 32)
            dl = y[:, 0:L * 256].rearrange("p (l f d) -> p l f d", l=L, f=4)
            for a in range(2):
                pr = tmp[:, a * 128:(a + 1) * 128].rearrange("p (l d) -> p l d", l=L)
                link(V.tensor_tensor(pr, dl[:, :, 2 * a, :], dl[:, :, 2 * a + 1, :], ALU.mult))
                ins = V.tensor_reduce(neglam[:, 4 + 2 * a:6 + 2 * a], pr, AX.X, ALU.add)
                if a == 0:
                    link(ins)
                else:
                    ins.then_inc(f_ready, tick("f_ready", "lam"))
            dve.wait_ge(act_ready, at("act_ready", "lam"))
            link(V.tensor_tensor(neglam[:, 0:2], neglam[:, 6:8], neglam[:, 4:6], ALU.subtract))
            lam0 = cst[:, C_LAM:C_LAM + L]
            link(V.tensor_tensor(neglam[:, 0:2], neglam[:, 0:2], lam0, ALU.subtract))
            link(V.tensor_scalar(neglam[:, 2:4], lam0, -1.0, 1.0, ALU.mult, ALU.add))
            for k in range(KD):
                evac(("x", k), xT[:, k * S:(k + 1) * S], ready="misc_ready")

            with en.layers(dve):
                nmix = lambda k: col(vecs, en.layer, V_NM + k)
                norm("n1", nmix)
                lo_part(sw_lo[:], vecs_slice(vecs, en.layer, V_SW, KD * SWC), sw_hi[:], "sw")
                evac("kr", None, srcs=[(SP4[0][0:ROPE, :], lambda s: s[0:ROPE, :])], ready="misc_ready")
                dve.wait_ge(out_free, en.mine("out_free"))
                rotary(SP4[0], "krrot", [(kpe[0:64, :], slice(0, 64))], ROPE)
                dve.wait_ge(misc_ready, at("misc_ready", "tok"))
                tok = ps[:, bank(en, "tok"), 0:NT * 28].rearrange("p (t c) -> p t c", t=NT)
                z4 = fz[:, 0:16].rearrange("p (t h) -> p t h", t=NT)
                bf = vecs_slice(vecs, en.layer, V_BF, HEADS).rearrange("p (o h) -> p o h", o=1).to_broadcast([P, NT, HEADS])
                link(V.tensor_tensor(z4, tok[:, :, 0:4], bf, ALU.add))
                V.tensor_copy(dgate[:].rearrange("p (t c) -> p t c", t=NT), tok[:, :, 4:28]).then_inc(out_free, tick("out_free", "tok"))
                link(V.tensor_scalar(fz[:, 16:32], fz[:, 0:16], -1.0, None, ALU.mult))
                V.tensor_tensor(fz[:, 16:32], fz[:, 16:32], fz[:, 0:16], ALU.max).then_inc(f_ready, tick("f_ready", "tok"))
                dve.wait_ge(act_ready, at("act_ready", "flog"))
                dve.sem_inc(out_free, tick("out_free", "pad"))
                link(V.tensor_scalar(fz[:, 0:16], fz[:, 0:16], 0.0, None, ALU.min))
                link(V.tensor_tensor(fz[:, 0:16], fz[:, 16:32], fz[:, 0:16], ALU.subtract))

                def qkv(br, scale):
                    for t in range(8):
                        evac((br, "fm", t), (q_ if t < 4 else k_)[:, t % 4 * S:(t % 4 + 1) * S], scale if t < 4 else 1.0)
                    for t in range(NT):
                        evac((br, "v", t), v_[:, t * S:(t + 1) * S])

                qkv(BR_A, 64 ** -0.5)
                attend(BR_A)
                qkv(BR_C, P ** -0.5)
                for h in range(HEADS):
                    if h:
                        dve.wait_ge(misc_ready, at("misc_ready", ("negc", h - 1)))
                    src = fz[:, 0:16].rearrange("p (t h) -> p t h", t=NT)[:, :, h:h + 1].to_broadcast([P, NT, P])
                    V.tensor_copy(nlfb.rearrange("p (t d) -> p t d", t=NT), src).then_inc(f_ready, tick("f_ready", ("nlf", h)))
                    evac(("negc", h), negc[:, h * S:(h + 1) * S], ready="misc_ready")
                dve.wait_ge(out_free, en.mine("out_free"))
                attend(BR_C)
                for j, key in enumerate(("cq", "ckv")):
                    for c in range(2):
                        evac((key, c), cfl[:, (2 * j + c) * S:(2 * j + c + 1) * S])
                dve.wait_ge(out_free, en.mine("out_free"))
                for j, key in enumerate(("cq", "ckv")):
                    vg = (V_NQ, V_NKV)[j]
                    normalise(key, 2, lambda c: cfl[:, (2 * j + c) * S:(2 * j + c + 1) * S],
                              lambda c: col(vecs, en.layer, vg + c),
                              lambda c: (cn_hi[j][:, c * S:(c + 1) * S], cn_lo[j][:, c * S:(c + 1) * S]))
                scale = (128 + 64) ** -0.5
                for h in range(HEADS):
                    evac(("bq", h), bq[:, h * S:(h + 1) * S], scale)
                for pr in range(2):
                    evac(("bqp", pr), SP4[0] if pr == 0 else SP4[3], scale)
                dve.wait_ge(f_split, en.mine("f_split"))
                dve.wait_ge(out_free, en.mine("out_free"))
                for pr in range(2):
                    rotary(SP4[0] if pr == 0 else SP4[3], ("bqrot", pr),
                           [(bqp[0:64, (2 * pr + e) * S:(2 * pr + e + 1) * S], slice(64 * e, 64 * e + 64)) for e in range(2)])
                for h in range(HEADS):
                    evac(("bk", h), bk[:, h * S:(h + 1) * S])
                for t in range(NT):
                    evac(("bv", t), bv[:, t * S:(t + 1) * S])
                attend(BR_B)
                for t in range(4):
                    evac(("dq", t), None, NSA_D ** -0.5, [(dq[0:64, (2 * t + e) * S:(2 * t + e + 1) * S],
                                                          (lambda s, e=e: s[64 * e:64 * e + 64, :])) for e in range(2)])
                for key, dst in (("dks", dks), ("dkw", dkw)):
                    evac(key, None, 1.0, [(dst[0:64, g * S:(g + 1) * S], (lambda s, g=g: s[64 * g:64 * g + 64, :])) for g in range(2)])
                for j in range(2):
                    key = ("dc", j)
                    dve.wait_ge(gemm_steps, at("gemm_steps", key))
                    pe = vecs_slice(vecs, en.layer, V_PE + 16 * j, 16)
                    zz = z[j].rearrange("p (l g c) -> p l g c", l=16, g=2)
                    for g in range(2):
                        for e in range(2):
                            rows = slice(64 * e, 64 * e + 64)
                            src = ps[64 * g:64 * g + 64, bank(en, key), :]
                            for half in range(2):
                                s3 = src[:, 16 * half:16 * half + 16 * NCMP].rearrange("p (c l e) -> p l e c", l=8, e=2)[:, :, e, :]
                                d3 = zz[rows, 8 * half:8 * half + 8, g, :]
                                pb = pe[rows, 8 * half:8 * half + 8].rearrange("p (l o) -> p l o", o=1).to_broadcast([64, 8, NCMP])
                                ins = V.tensor_tensor(d3, s3, pb, ALU.add)
                                if g + e + half == 3:
                                    ins.then_inc(out_free, tick("out_free", key))
                                else:
                                    ins.then_inc(dve_chain, tick("dve_chain"))
                    dve.wait_ge(dve_chain, en.mine("dve_chain"))
                    dve.wait_ge(out_free, en.mine("out_free"))
                    dve.sem_inc(f_ready, tick("f_ready", ("z", j)))
                for t in range(NT):
                    evac(("dv", t), dv[:, t * 256:(t + 1) * 256], srcs=[(dv[:, t * 256:(t + 1) * 256], lambda s: s[:, 0:256])])
                for j in range(2):
                    lo_part(z_lo[j][:], z[j], z_hi[j][:], ("z", j))
                link(V.tensor_copy(w2c, vecs_slice(vecs, en.layer, V_W2, P)))
                for j in range(2):
                    key = ("hid", j)
                    dve.wait_ge(gemm_steps, at("gemm_steps", key))
                    V.tensor_copy(hid[:, 62 * j:62 * j + 62], ps[:, bank(en, key), 0:62]).then_inc(out_free, tick("out_free", key))
                dve.wait_ge(out_free, en.mine("out_free"))
                dve.sem_inc(f_ready, tick("f_ready", "hid"))
                evac("kc", None, srcs=[(kc[0:64, :], lambda s: s[0:64, 0:62])], ready="misc_ready")
                evac("vc", None, srcs=[(vc[0:NCMP, :], lambda s: s[0:NCMP, 0:128])], ready="misc_ready")
                attend(BR_D)
                dve.wait_ge(out_free, en.mine("out_free"))
                V.memset(merged, 0.0).then_inc(dve_chain, tick("dve_chain", "merged"))
                with en.turns(dve, "gate", 2) as g:
                    for j in range(2):
                        for c in range(4):
                            dve.wait_ge(f_hi, at("f_hi", ("y", j, c)))
                            V.tensor_tensor(y_lo[j][:, c * S:(c + 1) * S], yT[:, bass.ds((g * 2 + j) * 4 * S + c * S, S)],
                                            y_hi[j][:, c * S:(c + 1) * S].bitcast(F32), ALU.subtract).then_inc(
                                f_split, tick("f_split", ("y", j, c)))
                        dve.wait_ge(dve_chain, at("dve_chain", "merged"))
                        for dt in range(8):
                            dve.wait_ge(act_ready, at("act_ready", ("sg", j, dt)))
                            dve.sem_inc(out_free, tick("out_free", ("gate", j, dt, 0)))
                            dve.wait_ge(gemm_steps, at("gemm_steps", ("gate", j, dt, 1)))
                            V.tensor_tensor(tmp, ps[:, bank(en, ("gate", j, dt, 1)), :], sg[dt % 2], ALU.mult).then_inc(
                                f_ready, tick("f_ready", ("mul", j, dt)))
                            dve.wait_ge(f_ready, en.mine("f_ready"))
                            mk = merged[:, dt * S:(dt + 1) * S]
                            V.tensor_tensor(mk, mk, tmp, ALU.add).then_inc(out_free, tick("out_free", ("gate", j, dt, 1)))
                            dve.wait_ge(out_free, en.mine("out_free"))
                for k in range(KD):
                    lo_part(m_lo[:, k * S:(k + 1) * S], merged[:, k * S:(k + 1) * S], m_hi[:, k * S:(k + 1) * S], ("m", k))
                for k in range(KD):
                    add_out(("wo", k), k)
                dve.wait_ge(out_free, en.mine("out_free"))
                norm("n2", lambda k: col(vecs, en.layer, V_NF + k))
                for half, (c0, nch) in enumerate(HALVES):
                    with en.turns(dve, ("up", half), nch // 2) as g:
                        for j in range(2):
                            for part, dst in ((0, ua[j]), (1, ug[j])):
                                key = ("up", half, j, part)
                                dve.wait_ge(act_ready, at("act_ready", key))
                                cv = V_CONV + (part * FFC + c0 + j) * 4
                                b = ps[:, bank(en, key), :]
                                link(V.scalar_tensor_tensor(dst[:, 1:S], b[:, 0:S - 1], col(vecs, en.layer, cv + 1, g, 8),
                                                            dst[:, 1:S], ALU.mult, ALU.add))
                                V.scalar_tensor_tensor(dst[:, 2:S], b[:, 0:S - 2], col(vecs, en.layer, cv, g, 8),
                                                       dst[:, 2:S], ALU.mult, ALU.add).then_inc(out_free, tick("out_free", key))
                                if part == 0:
                                    dve.wait_ge(out_free, en.mine("out_free"))
                                    dve.sem_inc(f_ready, tick("f_ready", ("conv", half, j)))
                            dve.wait_ge(out_free, en.mine("out_free"))
                            dve.wait_ge(act_ready, at("act_ready", ("silu", half, j)))
                            dve.wait_ge(f_split, at("f_split", ("act", half, j), -2))
                            V.tensor_tensor(uf[j], us[j], ug[j], ALU.mult).then_inc(f_ready, tick("f_ready", ("act", half, j)))
                            dve.wait_ge(f_hi, at("f_hi", ("act", half, j)))
                            V.tensor_tensor(a_lo[:, bass.ds((g * 2 + j) * S, S)], uf[j],
                                            a_hi[:, bass.ds((g * 2 + j) * S, S)].bitcast(F32), ALU.subtract).then_inc(
                                f_split, tick("f_split", ("act", half, j)))
                    for k in range(KD):
                        add_out(("down", half, k), k)
            dve.wait_ge(act_ready, at("act_ready", ("n3", "root")))
            V.reciprocal(SP4[3], SP4[2]).then_inc(out_free, tick("out_free", "n3"))
            dve.wait_ge(out_free, en.mine("out_free"))
            for k in range(KD):
                xk = xT[:, k * S:(k + 1) * S]
                V.scalar_tensor_tensor(xk, xk, nf[:, k:k + 1], SP4[3], ALU.mult, ALU.mult).then_inc(f_ready, tick("f_ready", ("n3", k)))
            for t in range(NT):
                for half in range(2):
                    dve.wait_ge(misc_ready, at("misc_ready", ("o", t, half)))
                    V.tensor_copy(stage[:, t * D + half * S:t * D + (half + 1) * S], ps[:, bank(en, ("o", t, half)), :]).then_inc(
                        out_ready, tick("out_ready", (t, half)))
                    dve.wait_ge(out_ready, en.mine("out_ready"))
                    dve.sem_inc(out_free, tick("out_free", ("o", t, half)))

        @block.tensor
        def _(pe):
            en = Engine(counts)
            tick, at = en.tick, en.at
            MM = nc.tensor.matmul
            half_tiles = [0]

            def three(dst, a, b, start, stop):
                MM(dst, a[0], b[0], start=start, stop=False)
                MM(dst, a[0], b[1], start=False, stop=False)
                return MM(dst, a[1], b[0], start=False, stop=stop)

            def free_bank(key):
                pe.wait_ge(out_free, at("out_free", key, -4))
                return ps[:, bank(en, key), :]

            def step(ins, key=None, by=1):
                ins.then_inc(gemm_steps, tick("gemm_steps", key, by))

            def enter_block(b):
                n = b + 1
                if en.loop is not None:
                    n = en.turn * en.loop_blocks + n
                pe.wait_ge(lo_done, en.layer * NBLK + n)

            def gemm(b, t0, key, rhs, nk, width=S, waits=None, tail=0):
                dst = free_bank(key)[:, 0:width]
                for k in range(nk):
                    t = t0 + k
                    if t % TILES == 0:
                        enter_block(b + t // TILES)
                    if waits is not None:
                        waits(k)
                    ins = three(dst, wt(b, t), rhs(k), k == 0, k == nk - 1)
                    last = k == nk - 1
                    if t % 2 == 1:
                        step(ins, key if last else None, 1 + (tail if last else 0))

            def h(k):
                return h_hi[:, k * S:(k + 1) * S], h_lo[:, k * S:(k + 1) * S]

            def hcols(k, t):
                c = k * S + t * P
                return h_hi[:, c:c + P], h_lo[:, c:c + P]

            def misc(ins, key):
                ins.then_inc(misc_ready, tick("misc_ready", key))

            def norm(key, n=KD):
                dst = free_bank(key)
                for k in range(n):
                    pe.wait_ge(sq_ready, at("sq_ready", (key, k)))
                    ins = MM(dst, ones, SP4[k % 2], start=k == 0, stop=k == n - 1)
                    misc(ins, (key, k) if k < n - 1 else key)

            def values(b, key, width, nk_block, lhs, nblocks):
                keys = [key + (t,) for t in range(NT)]
                dsts = [free_bank(k)[:, 0:width] for k in keys]
                total = nblocks * nk_block
                per_step = NT * nk_block // STEPS
                for bb in range(nblocks):
                    enter_block(b + bb)
                    s = (b + bb) % 2
                    for t in range(NT):
                        for kk in range(nk_block):
                            k = bb * nk_block + kk
                            w = (w_hi[s][:, kk * width:(kk + 1) * width], w_lo[s][:, kk * width:(kk + 1) * width])
                            ins = three(dsts[t], lhs(k, t), w, k == 0, k == total - 1)
                            g = t * nk_block + kk
                            if (g + 1) % per_step == 0:
                                step(ins, keys[t] if k == total - 1 else None)

            def scores(br, n):
                _, hd, part, i, m = units[br][n]
                w = unit_width(br, part, i)
                dst = ps[:, n % 4, 0:w]
                qs = slice(hd * S + i * P, hd * S + (i + 1) * P)
                if br == BR_A:
                    r = slice(64 * part, 64 * part + 64)
                    ins = MM(dst, q_[r, qs], k_[r, hd * S:hd * S + w], start=True, stop=True)
                elif br == BR_C:
                    MM(dst, q_[:, qs], k_[:, hd * S:hd * S + w], start=True, stop=False)
                    ins = MM(dst[:, w - P:w], ident, cst[:, C_CM + 3 * P:C_CM + 4 * P], start=False, stop=True)
                elif br == BR_B:
                    MM(dst, bq[:, qs], bk[:, hd * S:hd * S + w], start=True, stop=False)
                    ins = MM(dst, bqp[0:64, qs], kpe[0:64, 0:w], start=False, stop=True)
                else:
                    g = hd // 4
                    if part == 2:
                        for ii in range(NT):
                            ins = MM(dst[:, ii * NCMP:(ii + 1) * NCMP], dq[0:64, hd * S + ii * P:hd * S + (ii + 1) * P],
                                     kc[0:64, g * NCMP:(g + 1) * NCMP], start=True, stop=True)
                    else:
                        kk = dks if part == 0 else dkw
                        e = (i + 1) * P
                        ins = MM(dst, dq[0:64, qs], kk[0:64, g * S + e - w:g * S + e], start=True, stop=True)
                ins.then_inc(s_ready, tick("s_ready", (br, n)))

            def turn(br, n):
                _, hd, part, i, m = units[br][n]
                pe.wait_ge(p_ready, at("p_ready", (br, n)))
                pt = ps[:, 4 + n % 2, :]
                if br == BR_D and part == 2:
                    for ii in range(NT):
                        ins = nc.tensor.transpose(pt[0:NCMP, ii * P:(ii + 1) * P], SP4[n % 4][:, ii * NCMP:(ii + 1) * NCMP], ident)
                else:
                    for j in range(unit_width(br, part, i) // P):
                        ins = nc.tensor.transpose(pt[:, j * P:(j + 1) * P], SP4[n % 4][:, j * P:(j + 1) * P], ident)
                ins.then_inc(t_ready, tick("t_ready", (br, n)))

            def weigh(br, n):
                _, hd, part, i, m = units[br][n]
                pe.wait_ge(pt_ready, at("pt_ready", (br, n)))
                if i == 0:
                    pe.wait_ge(o_free, at("o_free", m, -2))
                ob = ps[:, 6 + m % 2, :]
                pt = PT2[n % 2]
                if br == BR_D:
                    g = hd // 4
                    if part == 2:
                        for ii in range(NT):
                            ins = MM(ob[:, ii * NSA_D:(ii + 1) * NSA_D], pt[0:NCMP, ii * P:(ii + 1) * P],
                                     vc[0:NCMP, g * NSA_D:(g + 1) * NSA_D], start=True, stop=True)
                    else:
                        nb = unit_width(br, part, i) // P
                        for jj in range(nb):
                            j = i + 1 - nb + jj
                            c = j * 256 + part * 128 + g * NSA_D
                            ins = MM(ob[:, i * NSA_D:(i + 1) * NSA_D], pt[:, jj * P:(jj + 1) * P], dv[:, c:c + NSA_D],
                                     start=jj == 0, stop=jj == nb - 1)
                else:
                    vv = bv if br == BR_B else v_
                    for j in range(i + 1):
                        ins = MM(ob[:, i * P:(i + 1) * P], pt[:, j * P:(j + 1) * P], vv[:, j * S + hd * P:j * S + (hd + 1) * P],
                                 start=j == 0, stop=j == i)
                ins.then_inc(pv_done, tick("pv_done", (br, n)))

            def attend(br, last_out):
                n_u = len(units[br])
                pe.wait_ge(out_free, at("out_free", last_out))
                scores(br, 0)
                scores(br, 1)
                for n in range(n_u + 1):
                    if n + 2 < n_u:
                        scores(br, n + 2)
                    if n < n_u:
                        turn(br, n)
                    if n >= 1:
                        weigh(br, n - 1)
                pe.wait_ge(f_ready, at("f_ready", ("y", br)))
                for c in range(4):
                    key = ("yT", br, c)
                    dst = free_bank(key)
                    for t in range(NT):
                        ins = nc.tensor.transpose(dst[:, t * P:(t + 1) * P], y[:, t * S + c * P:t * S + (c + 1) * P], ident)
                    misc(ins, key)

            pe.wait_ge(x_in_s, 32)
            for k in range(KD):
                dst = free_bank(("x", k))
                for t in range(NT):
                    ins = nc.tensor.transpose(dst[:, t * P:(t + 1) * P], stage[:, t * D + k * P:t * D + (k + 1) * P], ident)
                misc(ins, ("x", k))

            with en.layers(pe):
                norm("n1")
                hw1 = lambda k: pe.wait_ge(f_split, at("f_split", ("n1", k)))
                sw = lambda c, w: (sw_hi[:, c:c + w], sw_lo[:, c:c + w])
                dst = free_bank("kr")
                pe.wait_ge(f_split, at("f_split", "sw"))
                for k in range(KD):
                    ins = three(dst[0:ROPE, :], sw(k * SWC, ROPE), h(k), k == 0, k == KD - 1)
                misc(ins, "kr")
                dst = free_bank("krrot")
                pe.wait_ge(out_free, at("out_free", "kr"))
                misc(MM(dst, rot[0:ROPE, :], SP4[0][0:ROPE, :], start=True, stop=True), "krrot")
                dst = free_bank("tok")
                for t in range(NT):
                    for k in range(KD):
                        ins = three(dst[:, t * 28:(t + 1) * 28], hcols(k, t), sw(k * SWC + ROPE, 28), k == 0, k == KD - 1)
                misc(ins, "tok")
                for br, b in ((BR_A, B_A), (BR_C, B_C)):
                    for t in range(8):
                        gemm(b, 8 * t, (br, "fm", t), h, KD)
                    values(b + 4, (br, "v"), S, 4, hcols, 2)
                    if br == BR_C:
                        for hd in range(HEADS):
                            dst = free_bank(("negc", hd))
                            pe.wait_ge(f_ready, at("f_ready", ("nlf", hd)))
                            for t in range(NT):
                                ins = MM(dst[:, t * P:S], nlfb[:, t * P:(t + 1) * P], tri[:, 0:S - t * P], start=t == 0, stop=t == NT - 1)
                            misc(ins, ("negc", hd))
                    attend(br, (br, "v", NT - 1) if br == BR_A else ("negc", HEADS - 1))
                for j, key in enumerate(("cq", "ckv")):
                    for c in range(2):
                        gemm(B_B + j, 8 * c, (key, c), h, KD)
                for key in ("cq", "ckv"):
                    dst = free_bank((key, "n"))
                    for c in range(2):
                        pe.wait_ge(sq_ready, at("sq_ready", (key, c)))
                        ins = MM(dst, ones, SP4[c], start=c == 0, stop=c == 1)
                        misc(ins, (key, "n", 0) if c == 0 else (key, "n", 1))
                    alias(counts, "misc_ready", (key, "n"))
                lat = lambda j: (lambda c: (cn_hi[j][:, c * S:(c + 1) * S], cn_lo[j][:, c * S:(c + 1) * S]))
                pe.wait_ge(f_split, at("f_split", ("cq", 1)))
                for t in range(6):
                    key = ("bq", t) if t < 4 else ("bqp", t - 4)
                    gemm(B_B + 2, 2 * t, key, lat(0), 2, tail=2 if t == 5 else 0)
                for pr in range(2):
                    dst = free_bank(("bqrot", pr))
                    pe.wait_ge(out_free, at("out_free", ("bqp", pr)))
                    misc(MM(dst, rot, SP4[0] if pr == 0 else SP4[3], start=True, stop=True), ("bqrot", pr))
                pe.wait_ge(f_split, at("f_split", ("ckv", 1)))
                for t in range(4):
                    gemm(B_B + 3, 2 * t, ("bk", t), lat(1), 2)
                s = (B_B + 3) % 2
                for t in range(NT):
                    dst = free_bank(("bv", t))
                    for k in range(2):
                        c = 8 * P + k * S
                        lhs = (cn_hi[1][:, k * S + t * P:k * S + (t + 1) * P], cn_lo[1][:, k * S + t * P:k * S + (t + 1) * P])
                        ins = three(dst, lhs, (w_hi[s][:, c:c + S], w_lo[s][:, c:c + S]), k == 0, k == 1)
                    step(ins, ("bv", t))
                attend(BR_B, ("bv", NT - 1))
                for t in range(4):
                    gemm(B_D, 8 * t, ("dq", t), h, KD)
                for t, key in enumerate(("dks", "dkw", ("dc", 0), ("dc", 1))):
                    gemm(B_D + 2, 8 * t, key, h, KD)
                values(B_D + 4, ("dv",), 256, 8, hcols, 1)
                for j in range(2):
                    pe.wait_ge(f_split, at("f_split", ("z", j)))
                    zs = lambda k: (z_hi[j][:, k * 62:(k + 1) * 62], z_lo[j][:, k * 62:(k + 1) * 62])
                    gemm(B_D + 5 + j, 0, ("hid", j), zs, 16, width=62)
                dst = free_bank("kc")
                pe.wait_ge(act_ready, at("act_ready", "hid"))
                misc(MM(dst[0:64, 0:62], w2c[:, 0:64], hid[:, 0:62], start=True, stop=True), "kc")
                dst = free_bank("vc")
                for g in range(2):
                    ins = MM(dst[0:NCMP, g * 64:(g + 1) * 64], hid[:, 62 + g * NCMP:62 + (g + 1) * NCMP], w2c[:, 64:128], start=True, stop=True)
                misc(ins, "vc")
                attend(BR_D, "vc")
                en.loop_blocks = 12
                with en.turns(pe, "gate", 2):
                    for j in range(2):
                        ys = lambda c: (y_hi[j][:, c * S:(c + 1) * S], y_lo[j][:, c * S:(c + 1) * S])
                        for dt in range(8):
                            t0 = 96 * j + 12 * dt
                            gemm(B_GATE, t0, ("gate", j, dt, 0), h, KD)
                            wy = (lambda c: pe.wait_ge(f_split, at("f_split", ("y", j, c)))) if dt == 0 else None
                            gemm(B_GATE, t0 + 8, ("gate", j, dt, 1), ys, 4, waits=wy)
                mm = lambda k: (m_hi[:, k * S:(k + 1) * S], m_lo[:, k * S:(k + 1) * S])
                for dt in range(8):
                    wm = (lambda k: pe.wait_ge(f_split, at("f_split", ("m", k)))) if dt == 0 else None
                    gemm(B_OUT, 8 * dt, ("wo", dt), mm, KD, waits=wm)
                norm("n2")
                b = B_MLP
                for half, (c0, nch) in enumerate(HALVES):
                    en.loop_blocks = 2
                    with en.turns(pe, ("up", half), nch // 2):
                        for j in range(2):
                            for part in range(2):
                                w2 = (lambda k: pe.wait_ge(f_split, at("f_split", ("n2", k)))) if half == 0 and j == part == 0 else None
                                gemm(b, 16 * j + 8 * part, ("up", half, j, part), h, KD, waits=w2)
                    b += nch
                    aa = lambda k: (a_hi[:, k * S:(k + 1) * S], a_lo[:, k * S:(k + 1) * S])
                    pe.wait_ge(f_split, at("f_split", ("act", half, 1)))
                    for dt in range(8):
                        gemm(b, nch * dt, ("down", half, dt), aa, nch)
                    b += nch // 2
            norm("n3")
            for t in range(NT):
                for half in range(2):
                    dst = free_bank(("o", t, half))
                    for c in range(4):
                        k = half * 4 + c
                        pe.wait_ge(f_ready, at("f_ready", ("n3", k)))
                        ins = nc.tensor.transpose(dst[:, c * P:(c + 1) * P], xT[:, k * S + t * P:k * S + (t + 1) * P], ident)
                    misc(ins, ("o", t, half))

    return counts


def vecs_slice(vecs, layer, c, n):
    return vecs[:, bass.ds(layer * NV + c, n)]


def col(vecs, layer, c, turn=None, per_turn=0):
    at = layer * NV + c
    if turn is not None:
        at = turn * per_turn + at
    return vecs[:, bass.ds(at, 1)]


def alias(counts, name, key):
    counts.base[name, key] = (counts.now[name], counts.loop)


def unit_width(br, part, i):
    if br == BR_D and part == 2:
        return NT * NCMP
    if br == BR_D and part == 1:
        return P * min(i + 1, WIN // P + 1)
    return P * (i + 1)


def _tiles(w):
    k, n = w.shape
    return w.reshape(k // P, P, n // P, P).transpose(2, 0, 1, 3).reshape(-1, P, P)


def _blocks(tiles):
    return tiles.reshape(-1, TILES, P, P).transpose(0, 2, 1, 3).reshape(-1, P, BLK)


def _wide(w, k):
    n = w.shape[1]
    return w.reshape(-1, k, P, n).transpose(0, 2, 1, 3).reshape(-1, P, k * n)


def _weights(i, l):
    w = i["w_in"][l]
    cuts = np.cumsum([512, 512, 512, 256, 256, 64, 512, 512, 512, 4, 512, 768, 24])
    aq, ak, av, cq, ckv, kr, fq, fk, fv, cf, dq, dkv, dg, gate = np.split(w, cuts, axis=1)
    fm = lambda *ws: _blocks(_tiles(np.concatenate(ws, axis=1)))
    uq = i["mla_w_uq"][l].reshape(256, HEADS, 192)
    ukv = i["mla_w_ukv"][l].reshape(256, HEADS, 256)
    t = _tiles(np.concatenate([uq[:, :, :P].reshape(256, -1), uq[:, :, P:].reshape(256, -1)], axis=1))
    uq = _blocks(np.concatenate([t, np.zeros((4, P, P), np.float32)]))
    kn = _tiles(ukv[:, :, :P].reshape(256, 512)).transpose(1, 0, 2).reshape(P, 8 * P)
    vv = _wide(ukv[:, :, P:].reshape(256, 512), 2)[0]
    ukv = np.concatenate([kn, vv], axis=1)[None]
    k = dkv.reshape(D, 3, 2, P)
    parts = [fm(aq, ak), _wide(av, 4), fm(fq, fk), _wide(fv, 4), fm(cq, ckv), uq, ukv, fm(dq),
             fm(k[:, 1, 0], k[:, 2, 0], k[:, 0, 0], k[:, 0, 1]), _wide(np.concatenate([k[:, 1, 1], k[:, 2, 1]], axis=1), 8)]
    parts += [_blocks(i["nsa_cmp_w1"][l, j].reshape(16, P, P)) for j in range(2)]
    tiles = []
    for n in range(4):
        g, b = _tiles(gate[:, n * D:(n + 1) * D]), _tiles(i["w_branch"][l, n])
        for dt in range(8):
            tiles += [g[dt * 8:dt * 8 + 8], b[dt * 4:dt * 4 + 4]]
    parts += [_blocks(np.concatenate(tiles)), fm(i["w_out"][l])]
    up = _tiles(i["w_up"][l]).reshape(2, FFC, 8, P, P).transpose(1, 0, 2, 3, 4)
    for c0, n in HALVES:
        parts.append(_blocks(up[c0:c0 + n].reshape(-1, P, P)))
        parts.append(_blocks(_tiles(i["w_down"][l, c0 * P:(c0 + n) * P])))
    return np.concatenate(parts)


def _small(i, l):
    v = np.zeros((P, NV), np.float32)
    feat = lambda a: np.ascontiguousarray(a.reshape(-1, P).T)
    v[:, V_NM:V_NM + 8] = feat(i["norm_mix"][l])
    v[:, V_NF:V_NF + 8] = feat(i["norm_ffn"][l])
    v[:, V_NQ:V_NQ + 2] = feat(i["mla_norm_q"][l])
    v[:, V_NKV:V_NKV + 2] = feat(i["mla_norm_kv"][l])
    conv = np.concatenate([i["conv_w"][l], i["conv_b"][l][None]])
    v[:, V_CONV:V_SW] = conv.reshape(4, 2 * FFC, P).transpose(2, 1, 0).reshape(P, -1)
    w = i["w_in"][l]
    kr, cf, dg = w[:, 2048:2112], w[:, 3648:3652], w[:, 4932:4956]
    v[:, V_SW:V_W2] = np.concatenate([kr, cf, dg], axis=1).reshape(KD, P, SWC).transpose(1, 0, 2).reshape(P, -1)
    v[:, V_W2:V_PE] = np.concatenate([i["nsa_cmp_w2"][l, 0], i["nsa_cmp_w2"][l, 1]], axis=1)
    v[:, V_PE:V_SUB] = i["nsa_cmp_pe"][l].reshape(2, 16, P).transpose(2, 0, 1).reshape(P, 32)
    v[:, V_SUB:V_BF] = i["diff_subln"][l][None]
    v[:, V_BF:] = i["fox_b_f"][l][None]
    return v


def _constants():
    c = np.zeros((P, NCONST), np.float32)
    p = np.arange(P)[:, None]
    c[:, C_ID:C_ID + P] = np.eye(P)
    c[:, C_TRI:C_TRI + S] = np.arange(S)[None] >= p
    dist = p - (np.arange(S)[None] - 3 * P)
    c[:, C_ND:C_ND + S] = np.where(dist >= 0, -dist, NEG)
    c[:, C_CM:C_CM + S] = np.where(dist >= 0, 0, NEG)
    dist = p - (np.arange(3 * P)[None] - WIN)
    c[:, C_NDW:C_NDW + 3 * P] = np.where((dist >= 0) & (dist < WIN), -dist, NEG)
    pos = np.arange(NT)[None, :, None] * P + p[:, :, None]
    dist = pos - (np.arange(NCMP)[None, None] * 16 + 31)
    c[:, C_NDC:C_NDC + NT * NCMP] = np.where(dist >= 0, -dist, NEG).reshape(P, -1)
    c[:, C_ROW:C_ROW + NT] = (dist >= 0).any(axis=2)
    f32 = np.float32
    inv = f32(10000.0) ** (-np.arange(0, 64, 2, dtype=f32) / f32(64))
    ang = (np.arange(S, dtype=f32)[None] * inv[:, None]).astype(f32)
    c[:, C_COS:C_COS + S] = np.tile(np.cos(ang.astype(np.float64)), (4, 1))
    c[:, C_SIN:C_SIN + S] = np.tile(np.sin(ang.astype(np.float64)), (4, 1))
    for b in (0, 64):
        for m in range(32):
            c[b + m + 32, C_ROT + b + m] = -1.0
            c[b + m, C_ROT + b + m + 32] = 1.0
    c[:, C_LAM:C_LAM + L] = [0.8 - 0.6 * math.exp(-0.3 * l) for l in range(L)]
    return c


def kernel(**inputs):
    import concourse.bacc as _bacc
    from concourse.bass_utils import run_bass_kernel_spmd as _run

    i = {k: np.asarray(v) for k, v in inputs.items()}
    arrays = {
        "blob": np.concatenate([_weights(i, l) for l in range(L)]),
        "vec": np.stack([_small(i, l) for l in range(L)]),
        "const": _constants(),
        "dlam": np.ascontiguousarray(np.broadcast_to(i["diff_lambda"].reshape(1, -1), (P, L * 256))),
        "nfin": np.ascontiguousarray(i["norm_final"].reshape(KD, P).T),
        "x_in": np.ascontiguousarray(i["x"][0]),
    }

    def program(known):
        nc = _bacc.Bacc("TRN2", target_bir_lowering=False, num_devices=1)
        args = [nc.dram_tensor(n, a.shape, F32, kind="ExternalInput").ap() for n, a in arrays.items()]
        out = nc.dram_tensor("out", (S, D), F32, kind="ExternalOutput").ap()
        return nc, build(nc, *args, out, known)

    _, known = program(None)
    nc, _ = program(known)
    r = _run(nc, [arrays], core_ids=[0])
    return r.results[0]["out"].reshape(1, S, D)
```

```python
import math
from contextlib import ExitStack, contextmanager

import numpy as np

import concourse.bass as bass
from concourse import mybir

F32 = mybir.dt.float32
F32R = mybir.dt.float32r
ALU = mybir.AluOpType
ACT = mybir.ActivationFunctionType
AX = mybir.AxisListType

P = 128
S, D, L = 512, 1024, 2
NT = S // P
KD = D // P
TILES = 16
BLK = TILES * P
EPS = 1e-6
NEG = -1e30
BR_A, BR_B, BR_C, BR_D = range(4)
HEADS = 4
NSA_H, NSA_G, NSA_D = 8, 2, 64
NCMP = S // 16 - 1
WIN = 256
FFC = 2816 // P
HALVES = ((0, 12), (12, FFC - 12))
B_A, B_LAT, B_C, B_B, B_D = 0, 6, 8, 14, 16
B_GATE = B_D + 7
B_OUT = B_GATE + 24
B_MLP = B_OUT + 4
NBLK = B_MLP + FFC + 8 * FFC // TILES
STEPS = 8
V_NM, V_NF, V_NQ, V_NKV, V_CONV = 0, 8, 16, 18, 20
V_SW = V_CONV + 4 * 2 * FFC
ROPE = 64
SWC = ROPE + 28
V_W2 = V_SW + KD * SWC
V_PE = V_W2 + P
V_SUB = V_PE + 2 * 16
V_BF = V_SUB + P
NV = V_BF + HEADS
C_ID = 0
C_TRI = C_ID + P
C_ND = C_TRI + S
C_CM = C_ND + S
C_NDW = C_CM + S
C_NDC = C_NDW + 3 * P
C_COS = C_NDC + NT * NCMP
C_SIN = C_COS + S
C_ROT = C_SIN + S
C_ROW = C_ROT + P
C_LAM = C_ROW + NT
NCONST = C_LAM + L


def attention_units():
    units = {b: [] for b in range(4)}
    maps = 0
    for br, heads, parts in ((BR_A, HEADS, 2), (BR_C, HEADS, 1), (BR_B, HEADS, 1), (BR_D, NSA_H, 3)):
        for h in range(heads):
            for part in range(parts):
                blocks = [0] if (br == BR_D and part == 2) else range(NT)
                units[br] += [(br, h, part, i, maps) for i in blocks]
                maps += 1
    return units


class Counts:

    def __init__(self, known=None):
        self.known = known
        self.now, self.base, self.stride, self.total, self.start = {}, {}, {}, {}, {}
        self.loop = None

    def tick(self, name, key=None, by=1):
        self.now[name] = self.now.get(name, 0) + by
        self.base[name, key] = (self.now[name], self.loop)
        return by


class Engine:

    def __init__(self, counts):
        self.c, self.layer, self.turn, self.loop = counts, None, None, None

    def tick(self, name, key=None, by=1):
        return self.c.tick(name, key, by)

    def _value(self, name, n, loop, last=None):
        known = self.c.known
        if known is None:
            return 1
        if loop is not None:
            step = known.stride.get((loop, name), 0)
            if self.loop == loop:
                n = self.turn * step + n if step else n
            else:
                n += step * (known.trips[loop] - 1)
        if self.layer is not None:
            n = self.layer * known.total.get(name, 0) + n
        return n

    def at(self, name, key, off=0):
        if self.c.known is None:
            return 1
        n, loop = self.c.known.base[name, key]
        return self._value(name, n + off, loop)

    def after(self, name, key):
        if self.c.known is None:
            return 1
        return self.c.known.base[name, key][0] + (L - 1) * self.c.known.total[name]

    def mine(self, name):
        return self._value(name, self.c.now[name], self.loop)

    @contextmanager
    def layers(self, e):
        before = dict(self.c.now)
        with e.Fori(0, L) as i:
            self.layer = i
            yield
        for name, n in self.c.now.items():
            per = n - before.get(name, 0)
            if per:
                self.c.total[name] = per
                self.c.now[name] = n + per * (L - 1)
        self.layer = None

    @contextmanager
    def turns(self, e, loop, trips):
        before = dict(self.c.now)
        self.c.loop = self.loop = loop
        with e.Fori(0, trips) as i:
            self.turn = i
            yield i
        self.c.loop = self.loop = self.turn = None
        self.c.trips[loop] = trips
        for name, n in self.c.now.items():
            step = n - before.get(name, 0)
            if step:
                self.c.stride[loop, name] = step
                self.c.now[name] = n + step * (trips - 1)


def build(nc, blob, vec, const, dlam, nfin, x_in, out, known):
    counts = Counts(known)
    counts.trips = {}
    units = attention_units()
    with ExitStack() as ctx:
        def sem(name):
            return ctx.enter_context(nc.semaphore(name))

        def sb(name, cols, dt=F32):
            return ctx.enter_context(nc.sbuf_tensor(name, [P, cols], dt))

        xT = sb("xT", KD * S)
        h_hi, h_lo = sb("h_hi", KD * S, F32R), sb("h_lo", KD * S, F32R)
        raw = [sb(f"raw{j}", BLK) for j in range(2)]
        w_hi = [sb(f"w_hi{j}", BLK, F32R) for j in range(2)]
        w_lo = [sb(f"w_lo{j}", BLK, F32R) for j in range(2)]
        cst = sb("cst", NCONST)
        vecs = sb("vecs", L * NV)
        nf = sb("nf", KD)
        lsum, rinv, negm = sb("lsum", 16), sb("rinv", 16), sb("negm", 8)
        dgate, fz, neglam = sb("dgate", 4 * 24), sb("fz", 64), sb("neglam", 8)
        epst = sb("epst", 1)
        YT, QKV, WORK = 0, 32768, 32768 + 34816
        base = (nc.sbuf_base + 31) // 32 * 32
        region = sb("region", (WORK + 22528) // 4)
        assert nc.sbuf_base == base + WORK + 22528

        def reg(byte, cols):
            return region[:, byte // 4:byte // 4 + cols]

        def overlay(name, byte, cols):
            return nc.alloc_sbuf_tensor_at(name, [P, cols], F32R, offset=base + byte)

        SP4 = [reg(WORK + 2048 * j, S) for j in range(4)]
        PT2 = [reg(WORK + 8192 + 2048 * j, S) for j in range(2)]
        y = reg(WORK + 12288, NT * S)
        tmp = reg(WORK + 20480, S)
        yT = reg(YT, 16 * S)
        sw_hi = overlay("sw_hi", WORK + 12288, KD * SWC)
        sw_lo = overlay("sw_lo", WORK + 12288 + 4 * KD * SWC, KD * SWC)
        q_, k_, v_ = reg(QKV, 4 * S), reg(QKV + 8192, 4 * S), reg(QKV + 16384, NT * S)
        negc = reg(QKV + 24576, 4 * S)
        bq, bqp, bk = reg(QKV, 4 * S), reg(QKV + 8192, 4 * S), reg(QKV + 16384, 4 * S)
        bv, kpe = reg(QKV + 24576, NT * S), reg(QKV + 32768, S)
        q2_ = reg(QKV + 24576, 4 * S)
        bias_a = reg(YT + 8192, S)
        nlfb = SP4[3]
        cfl = reg(YT + 3 * 8192, 4 * S)
        cn_hi = [overlay("cq_hi", YT + 3 * 8192 + 4096, 2 * S), overlay("ckv_hi", YT + 8192, 2 * S)]
        cn_lo = [overlay("cq_lo", YT + 3 * 8192, 2 * S), overlay("ckv_lo", YT + 8192 + 4096, 2 * S)]
        dq, dks, dkw = reg(QKV, 8 * S), reg(QKV + 16384, S), reg(QKV + 18432, S)
        dv = reg(QKV + 24576, NT * 256)
        o = QKV + 28672
        bias_s, bias_w, bias_c = reg(o, S), reg(o + 2048, 384), reg(o + 3584, NT * NCMP)
        o += 4080
        kc, vc, w2c, hid = reg(o, 62), reg(o + 248, 128), reg(o + 760, 128), reg(o + 1272, 124)
        NZ = 16 * 2 * NCMP
        z = [reg(WORK, NZ), reg(WORK + 4096, NZ)]
        z_hi = [overlay(f"z_hi{j}", WORK + 12288 + j * 4 * NZ, NZ) for j in range(2)]
        z_lo = [overlay(f"z_lo{j}", YT + 3 * 8192 + j * 4 * NZ, NZ) for j in range(2)]
        y_hi = [overlay(f"y_hi{j}", QKV + 16384 * j, 4 * S) for j in range(2)]
        y_lo = [overlay(f"y_lo{j}", QKV + 16384 * j + 8192, 4 * S) for j in range(2)]
        merged = reg(WORK, KD * S)
        sg = [reg(WORK + 16384 + 2048 * j, S) for j in range(2)]
        m_hi, m_lo = overlay("m_hi", YT, KD * S), overlay("m_lo", YT + 16384, KD * S)
        a_hi, a_lo = overlay("a_hi", 0, 12 * S), overlay("a_lo", 24576, 12 * S)
        ua = [reg(WORK + 2048 * j, S) for j in range(2)]
        ug = [reg(WORK + 4096 + 2048 * j, S) for j in range(2)]
        us = [reg(WORK + 8192 + 2048 * j, S) for j in range(2)]
        uf = [reg(WORK + 12288 + 2048 * j, S) for j in range(2)]
        stage = reg(0, NT * D)

        ps = ctx.enter_context(nc.psum_tensor("ps", [P, 8, S], F32))

        ident = cst[:, C_ID:C_ID + P]
        tri = cst[:, C_TRI:C_TRI + S]
        ones = cst[:, C_TRI + P:C_TRI + 2 * P]
        rot = cst[:, C_ROT:C_ROT + P]
        cos, sin = cst[:, C_COS:C_COS + S], cst[:, C_SIN:C_SIN + S]

        landed = [sem(f"block_landed{j}") for j in range(2)]
        hi_done = sem("hi_done")
        lo_done = sem("lo_done")
        gemm_steps = sem("gemm_steps")
        misc_ready = sem("misc_ready")
        out_free = sem("out_free")
        f_ready = sem("f_ready")
        f_hi = sem("f_hi")
        f_split = sem("f_split")
        sq_ready = sem("sq_ready")
        act_ready = sem("act_ready")
        dve_chain = sem("dve_chain")
        act_chain = sem("act_chain")
        s_ready = sem("s_ready")
        sb_ready = sem("sb_ready")
        p_ready = sem("p_ready")
        t_ready = sem("t_ready")
        pt_ready = sem("pt_ready")
        pv_done = sem("pv_done")
        o_free = sem("o_free")
        sq_used = sem("sq_used")
        ident_in = sem("ident_in")
        const_in = sem("const_in")
        lam_in = sem("lam_in")
        small_in = sem("small_in")
        x_part_in = [sem(f"x_part_in{j}") for j in range(4)]
        stored = sem("stored")
        out_ready = sem("out_ready")

        block = ctx.enter_context(nc.Block())

        def wt(b, t):
            s, c = (b + t // TILES) % 2, t % TILES * P
            return w_hi[s][:, c:c + P], w_lo[s][:, c:c + P]

        def bank(en, key):
            n = 1 if en.c.known is None else en.c.known.base["out_free", key][0] - 4
            return (n - 1) % 4

        @block.sync
        def _(sp):
            sp.dma_start(cst[:, 0:C_CM], const[:, 0:C_CM]).then_inc(ident_in, 16)
            tokens, x3 = stage.rearrange("p (t d) -> p t d", t=NT), x_in.rearrange("(t p) d -> p t d", p=P)
            for j in range(4):
                f = slice(j * 256, (j + 1) * 256)
                sp.dma_start(tokens[:, :, f], x3[:, :, f]).then_inc(x_part_in[j], 16)
            sp.dma_start(raw[0][:], blob[0]).then_inc(landed[0], 16)
            sp.dma_start(raw[1][:], blob[1]).then_inc(landed[1], 16)
            sp.dma_start(cst[:, C_CM:], const[:, C_CM:]).then_inc(const_in, 16)
            with sp.Fori(1, L * NBLK // 2) as i:
                for j in range(2):
                    sp.wait_ge(lo_done, i * 2 + (j - 1))
                    sp.dma_start(raw[j][:], blob[i * 2 + j]).then_inc(landed[j], 16)
            for j in range(2):
                sp.wait_ge(lo_done, L * NBLK + j - 1)
                sp.dma_start(raw[j][:], blob[j]).then_inc(landed[j], 16)
            for t in range(NT):
                sp.wait_ge(out_ready, 2 * (t + 1))
                sp.dma_start(out[t * P:(t + 1) * P, :], stage[:, t * D:(t + 1) * D]).then_inc(stored, 16)
            sp.wait_ge(stored, 16 * NT)

        @block.gpsimd
        def _(pool):
            with pool.Fori(0, L * NBLK // 2 + 1) as i:
                for j in range(2):
                    pool.wait_ge(hi_done, i * 2 + (j + 1))
                    pool.tensor_tensor(w_lo[j][:], raw[j][:], w_hi[j][:].bitcast(F32), ALU.subtract).then_inc(lo_done, 1)

        @block.scalar
        def _(act):
            en = Engine(counts)
            tick, at = en.tick, en.at
            A = nc.scalar.activation

            def split_block(b):
                if b >= 2:
                    n = STEPS * (b - 1)
                    act.wait_ge(gemm_steps, at_block(n))
                slot = b % 2
                g = b // 2
                g = en.layer * (NBLK // 2) + g if en.layer is not None else g
                if en.loop is not None:
                    g = en.turn * (en.loop_blocks // 2) + g
                act.wait_ge(landed[slot], g * 16 + 16)
                A(w_hi[slot][:], raw[slot][:], ACT.Copy).then_inc(hi_done, 1)

            def at_block(n):
                if en.loop is not None:
                    n = en.turn * (en.loop_blocks * STEPS) + n
                return en.layer * (NBLK * STEPS) + n

            def blocks(b, n):
                for j in range(b, b + n):
                    split_block(j + 2)

            def split_hi(dst, src, key, wait=None):
                if wait is None:
                    act.wait_ge(f_ready, at("f_ready", key))
                A(dst, src, ACT.Copy).then_inc(f_hi, tick("f_hi", key))

            def square(key, k, ready):
                act.wait_ge(out_free, at("out_free", ready))
                if k >= 2:
                    act.wait_ge(sq_used, at("sq_used", (key, k - 2)))
                A(SP4[k % 2], xT[:, k * S:(k + 1) * S], ACT.Square).then_inc(sq_ready, tick("sq_ready", (key, k)))

            def root(key):
                act.wait_ge(sq_used, at("sq_used", (key, KD - 1)))
                A(SP4[2], ps[:, 4, :], ACT.Sqrt, bias=epst[:, 0:1], scale=1.0 / D).then_inc(
                    act_ready, tick("act_ready", (key, "root")))

            def blocks_and_squares(b, nk, key, ready):
                done = 0
                for k in range(KD):
                    while (done + 1) * TILES <= nk * (k + 1) and k < KD - 1:
                        split_block(b + done + 2)
                        done += 1
                    square(key, k, ready(k))
                root(key)
                while done < nk * KD // TILES:
                    split_block(b + done + 2)
                    done += 1

            def attend(br):
                us_ = units[br]
                for n, (_, h, part, i, m) in enumerate(us_):
                    u = (br, n)
                    sbuf, w = SP4[n % 4], unit_width(br, part, i)
                    act.wait_ge(sb_ready, at("sb_ready", u))
                    if part == 2 and br == BR_D:
                        A(sbuf[:, 0:w], sbuf[:, 0:w], ACT.Exp).then_inc(p_ready, tick("p_ready", u))
                    else:
                        A(sbuf[:, 0:w], sbuf[:, 0:w], ACT.Exp, scale=-1.0, bias=negm[:, n % 8:n % 8 + 1],
                          accum_out=lsum[:, m % 4 * 4 + i:m % 4 * 4 + i + 1]).then_inc(p_ready, tick("p_ready", u))
                    if n >= 1:
                        spread(br, n - 1)
                spread(br, len(us_) - 1)

            def spread(br, n):
                _, h, part, i, m = units[br][n]
                act.wait_ge(t_ready, at("t_ready", (br, n)))
                if n >= 2:
                    act.wait_ge(pv_done, at("pv_done", (br, n), -2))
                if br == BR_D and part == 2:
                    src, dst = ps[0:NCMP, 4 + n % 2, 0:S], PT2[n % 2][0:NCMP, :]
                else:
                    w = unit_width(br, part, i)
                    src, dst = ps[:, 4 + n % 2, 0:w], PT2[n % 2][:, 0:w]
                A(dst, src, ACT.Copy).then_inc(pt_ready, tick("pt_ready", (br, n)))

            act.dma_start(y[:, 0:L * 256], dlam).then_inc(lam_in, 16)
            act.wait_ge(x_part_in[3], 16)
            act.dma_start(vecs[:].rearrange("p (l v) -> p l v", l=L), vec.rearrange("l p v -> p l v")).then_inc(small_in, 16)
            act.dma_start(nf[:], nfin).then_inc(small_in, 16)
            act.wait_ge(f_ready, at("f_ready", "lam"))
            A(neglam[:, 4:8], neglam[:, 4:8], ACT.Exp).then_inc(act_ready, tick("act_ready", "lam"))
            for k in range(KD):
                if k in (3, 6):
                    j = k // 3 - 1
                    act.wait_ge(landed[j], 16)
                    A(w_hi[j][:], raw[j][:], ACT.Copy).then_inc(hi_done, 1)
                square("x", k, ("x", k))
            root("x")

            with en.layers(act):
                for k in range(KD):
                    split_hi(h_hi[:, k * S:(k + 1) * S], PT2[k % 2], ("n1", k))
                split_hi(sw_hi[:], vecs_slice(vecs, en.layer, V_SW, KD * SWC), "sw", wait=False)
                blocks(B_A, 6)
                attend(BR_A)
                act.wait_ge(f_ready, at("f_ready", "subln"))
                A(fz[:, 32:48], fz[:, 32:48], ACT.Sqrt, bias=epst[:, 0:1], scale=1.0 / P).then_inc(
                    act_ready, tick("act_ready", "subln"))
                blocks(B_LAT, 2)
                act.wait_ge(f_ready, at("f_ready", "tok"))
                A(dgate[:], dgate[:], ACT.Sigmoid).then_inc(act_ready, tick("act_ready", "dgate"))
                A(fz[:, 16:32], fz[:, 16:32], ACT.Exp, scale=-1.0).then_inc(act_chain, tick("act_chain"))
                act.wait_ge(act_chain, en.mine("act_chain"))
                A(fz[:, 16:32], fz[:, 16:32], ACT.Ln, bias=ones[:, 0:1]).then_inc(act_ready, tick("act_ready", "flog"))
                for j, key in ((1, "ckv"), (0, "cq")):
                    for c in range(2):
                        act.wait_ge(out_free, at("out_free", (key, c)))
                        if key == "cq":
                            act.wait_ge(misc_ready, at("misc_ready", ("ckv", "n", c)))
                        A(SP4[c], cfl[:, (2 * j + c) * S:(2 * j + c + 1) * S], ACT.Square).then_inc(
                            sq_ready, tick("sq_ready", (key, c)))
                    act.wait_ge(misc_ready, at("misc_ready", (key, "n", 1)))
                    if key == "cq":
                        act.wait_ge(f_split, at("f_split", ("ckv", 1)))
                    A(SP4[2], ps[:, bank(en, (key, "n")), :], ACT.Sqrt, bias=epst[:, 0:1], scale=1.0 / 256).then_inc(
                        act_ready, tick("act_ready", (key, "root")))
                    for c in range(2):
                        split_hi(cn_hi[j][:, c * S:(c + 1) * S], PT2[c], (key, c))
                blocks(B_C, 6)
                attend(BR_C)
                blocks(B_B, 2)
                attend(BR_B)
                blocks(B_D, 1)
                act.wait_ge(out_free, at("out_free", ("yT", BR_B, 3)))
                for j in range(2):
                    split_hi(z_hi[j][:], z[j], ("z", j))
                blocks(B_D + 1, 5)
                act.wait_ge(f_ready, at("f_ready", "hid"))
                A(hid, hid, ACT.Gelu_apprx_tanh).then_inc(act_ready, tick("act_ready", "hid"))
                blocks(B_D + 6, 1)
                attend(BR_D)
                en.loop_blocks = 12
                with en.turns(act, "gate", 2) as g:
                    for j in range(2):
                        for c in range(4):
                            act.wait_ge(out_free, at("out_free", ("yT", BR_D, 3)))
                            act.wait_ge(gemm_steps, at("gemm_steps", ("gate", j, 7, 1), -12 * STEPS))
                            A(y_hi[j][:, c * S:(c + 1) * S], yT[:, bass.ds((g * 2 + j) * 4 * S + c * S, S)], ACT.Copy).then_inc(
                                f_hi, tick("f_hi", ("y", j, c)))
                        done = j * 6
                        for dt in range(8):
                            act.wait_ge(gemm_steps, at("gemm_steps", ("gate", j, dt, 0)))
                            act.wait_ge(f_ready, at("f_ready", ("mul", j, dt), -2))
                            A(sg[dt % 2], ps[:, bank(en, ("gate", j, dt, 0)), :], ACT.Sigmoid).then_inc(
                                act_ready, tick("act_ready", ("sg", j, dt)))
                            while (done + 1 - j * 6) * TILES <= 12 * (dt + 1):
                                split_block(B_GATE + done + 2)
                                done += 1
                for k in range(KD):
                    act.wait_ge(out_free, at("out_free", ("gate", 1, k, 1)))
                    A(m_hi[:, k * S:(k + 1) * S], merged[:, k * S:(k + 1) * S], ACT.Copy).then_inc(
                        f_hi, tick("f_hi", ("m", k)))
                blocks_and_squares(B_OUT, KD, "n2", lambda k: ("wo", k))
                for k in range(KD):
                    split_hi(h_hi[:, k * S:(k + 1) * S], PT2[k % 2], ("n2", k))
                b = B_MLP
                for half, (c0, nch) in enumerate(HALVES):
                    en.loop_blocks = 2
                    with en.turns(act, ("up", half), nch // 2) as g:
                        for j in range(2):
                            for part, dst in ((0, ua[j]), (1, ug[j])):
                                act.wait_ge(gemm_steps, at("gemm_steps", ("up", half, j, part)))
                                act.wait_ge(f_ready, at("f_ready", ("act", half, j), -4))
                                cv = V_CONV + (part * FFC + c0 + j) * 4
                                A(dst, ps[:, bank(en, ("up", half, j, part)), :], ACT.Identity,
                                  bias=col(vecs, en.layer, cv + 3, g, 8), scale=col(vecs, en.layer, cv + 2, g, 8)).then_inc(
                                    act_ready, tick("act_ready", ("up", half, j, part)))
                            split_block(b + j + 2)
                            act.wait_ge(f_ready, at("f_ready", ("conv", half, j)))
                            A(us[j], ua[j], ACT.Silu).then_inc(act_ready, tick("act_ready", ("silu", half, j)))
                            act.wait_ge(f_ready, at("f_ready", ("act", half, j)))
                            A(a_hi[:, bass.ds((g * 2 + j) * S, S)], uf[j], ACT.Copy).then_inc(
                                f_hi, tick("f_hi", ("act", half, j)))
                    b += nch
                    if half == 0:
                        blocks(b, nch // 2)
                    else:
                        blocks_and_squares(b, nch, "n1", lambda k: ("down", 1, k))
                    b += nch // 2

        @block.vector
        def _(dve):
            en = Engine(counts)
            tick, at = en.tick, en.at
            V = nc.vector

            def link(ins):
                ins.then_inc(dve_chain, tick("dve_chain"))
                dve.wait_ge(dve_chain, en.mine("dve_chain"))

            def lo_part(dst, src, hi, key):
                dve.wait_ge(f_hi, at("f_hi", key))
                V.tensor_tensor(dst, src, hi.bitcast(F32), ALU.subtract).then_inc(f_split, tick("f_split", key))

            def evac(key, dst, scale=1.0, srcs=None, ready="gemm_steps"):
                sem_ = {"gemm_steps": gemm_steps, "misc_ready": misc_ready}[ready]
                dve.wait_ge(sem_, at(ready, key))
                src = ps[:, bank(en, key), :]
                parts = [(dst, src)] if srcs is None else [(d, f(src)) for d, f in srcs]
                for n, (d, s) in enumerate(parts):
                    ins = V.tensor_scalar(d, s, scale, None, ALU.mult)
                    if n == len(parts) - 1:
                        ins.then_inc(out_free, tick("out_free", key))

            def normalise(key, root, nk, src, gain, dsts):
                dve.wait_ge(act_ready, at("act_ready", (root, "root")))
                if nk == KD:
                    link(V.reciprocal(SP4[3], SP4[2]))
                else:
                    V.reciprocal(SP4[3], SP4[2]).then_inc(out_free, tick("out_free", (key, "n")))
                    dve.wait_ge(out_free, en.mine("out_free"))
                for k in range(nk + 1):
                    if k < nk:
                        if k >= 2 or nk < KD:
                            dve.wait_ge(f_split, en.mine("f_split"))
                        V.scalar_tensor_tensor(PT2[k % 2], src(k), gain(k), SP4[3], ALU.mult, ALU.mult).then_inc(
                            f_ready, tick("f_ready", (key, k)))
                    if k >= 1:
                        hi, lo = dsts(k - 1)
                        lo_part(lo, PT2[(k - 1) % 2], hi, (key, k - 1))

            def attend(br):
                us_ = units[br]
                ends = {}
                for n, (_, h, part, i, m) in enumerate(us_):
                    if n + 1 == len(us_) or us_[n + 1][4] != m:
                        ends[n] = (h, part, m)
                for n in range(len(us_) + 3):
                    if n < len(us_):
                        piece(br, n)
                    if n - 3 in ends:
                        map_out(br, n - 3, *ends[n - 3])
                if br == BR_A:
                    subln()

            def keep_y(br):
                for c in range(4):
                    key = ("yT", br, c)
                    evac(key, yT[:, (br * 4 + c) * S:(br * 4 + c + 1) * S], ready="misc_ready")

            def wait_last_piece(n):
                if n:
                    dve.wait_ge(sb_ready, en.mine("sb_ready"))

            def piece(br, n):
                _, h, part, i, m = units[br][n]
                first = i == 0
                if br == BR_A and part == 0 and first:
                    wait_last_piece(n)
                    link(V.tensor_scalar(bias_a, cst[:, C_ND:C_ND + S], 2.0 ** (-8.0 * (h + 1) / HEADS), None, ALU.mult))
                if br == BR_D and part == 0 and first:
                    slope = 2.0 ** (-8.0 * (h + 1) / NSA_H)
                    wait_last_piece(n)
                    V.tensor_scalar(bias_s, cst[:, C_ND:C_ND + S], slope, None, ALU.mult).then_inc(dve_chain, tick("dve_chain"))
                    V.tensor_scalar(bias_w, cst[:, C_NDW:C_NDW + 384], slope, None, ALU.mult).then_inc(dve_chain, tick("dve_chain"))
                    link(V.tensor_scalar(bias_c, cst[:, C_NDC:C_NDC + NT * NCMP], slope, None, ALU.mult))
                w = unit_width(br, part, i)
                dst, src = SP4[n % 4][:, 0:w], ps[:, n % 4, 0:w]
                dve.wait_ge(s_ready, at("s_ready", (br, n)))
                if n >= 4:
                    dve.wait_ge(t_ready, at("t_ready", (br, n), -4))
                if br == BR_D and part == 2:
                    cm = negm_c
                    link(V.tensor_tensor(dst, src, bias_c, ALU.add))
                    d3 = dst.rearrange("p (t c) -> p t c", t=NT)
                    link(V.tensor_reduce(cm, d3, AX.X, ALU.max))
                    V.tensor_tensor(d3, d3, cm.rearrange("p (t o) -> p t o", o=1).to_broadcast([P, NT, NCMP]), ALU.subtract).then_inc(
                        sb_ready, tick("sb_ready", (br, n)))
                    return
                if br == BR_A:
                    bias = bias_a[:, S - w:S]
                elif br == BR_B:
                    bias = cst[:, C_CM + S - w:C_CM + S]
                elif br == BR_C:
                    bias = negc[:, h * S:h * S + w]
                elif part == 0:
                    bias = bias_s[:, S - w:S]
                else:
                    bias = bias_w[:, 384 - w:384]
                dve.sem_inc(dve_chain, tick("dve_chain"))
                V.tensor_tensor_reduce(dst, src, bias, -1.0, 3e38, ALU.add, ALU.min, negm[:, n % 8:n % 8 + 1]).then_inc(
                    sb_ready, tick("sb_ready", (br, n)))

            negm_c = fz[:, 48:52]

            def map_out(br, n, h, part, m):
                r = rinv[:, m % 4 * 4:m % 4 * 4 + 4]
                ls = lsum[:, m % 4 * 4:m % 4 * 4 + 4]
                dve.wait_ge(p_ready, at("p_ready", (br, n)))
                if br == BR_D and part == 2:
                    pc = SP4[n % 4][:, 0:NT * NCMP].rearrange("p (t c) -> p t c", t=NT)
                    link(V.tensor_reduce(ls, pc, AX.X, ALU.add))
                link(V.reciprocal(r, ls))
                if br == BR_A and part == 1:
                    link(V.tensor_scalar(r, r, neglam[:, bass.ds(en.layer, 1)], None, ALU.mult))
                if br == BR_D:
                    g = dgate[:].rearrange("p (t c) -> p t c", t=NT)[:, :, 3 * h + (1, 2, 0)[part]]
                    link(V.tensor_tensor(r, r, g, ALU.mult))
                    if part == 2:
                        link(V.tensor_tensor(r, r, cst[:, C_ROW:C_ROW + NT], ALU.mult))
                wd = NSA_D if br == BR_D else P
                ob = ps[:, 6 + m % 2, 0:NT * wd].rearrange("p (t d) -> p t d", t=NT)
                rb = r.rearrange("p (t o) -> p t o", o=1).to_broadcast([P, NT, wd])
                yh = y.rearrange("p (t d) -> p t d", t=NT)[:, :, h * wd:(h + 1) * wd]
                dve.wait_ge(pv_done, at("pv_done", (br, n)))
                if part == 0:
                    V.tensor_tensor(yh, ob, rb, ALU.mult).then_inc(o_free, tick("o_free", m))
                    dve.wait_ge(o_free, en.mine("o_free"))
                else:
                    t3 = tmp[:, 0:NT * wd].rearrange("p (t d) -> p t d", t=NT)
                    V.tensor_tensor(t3, ob, rb, ALU.mult).then_inc(o_free, tick("o_free", m))
                    dve.wait_ge(o_free, en.mine("o_free"))
                    link(V.tensor_tensor(yh, yh, t3, ALU.add))
                if n == len(units[br]) - 1 and br != BR_A:
                    dve.sem_inc(f_ready, tick("f_ready", ("y", br)))

            def subln():
                y4 = y.rearrange("p (t h d) -> p t h d", t=NT, h=HEADS)
                for h in range(HEADS):
                    t3 = tmp.rearrange("p (t d) -> p t d", t=NT)
                    link(V.tensor_tensor(t3, y4[:, :, h, :], y4[:, :, h, :], ALU.mult))
                    ins = V.tensor_reduce(fz[:, 32 + 4 * h:36 + 4 * h], t3, AX.X, ALU.add)
                    if h < HEADS - 1:
                        link(ins)
                    else:
                        ins.then_inc(f_ready, tick("f_ready", "subln"))
                dve.wait_ge(act_ready, at("act_ready", "subln"))
                link(V.reciprocal(fz[:, 32:48], fz[:, 32:48]))
                link(V.tensor_scalar(fz[:, 32:48], fz[:, 32:48], neglam[:, bass.ds(en.layer + L, 1)], None, ALU.mult))
                g = vecs_slice(vecs, en.layer, V_SUB, P)
                for h in range(HEADS):
                    r = fz[:, 32 + 4 * h:36 + 4 * h].rearrange("p (t o) -> p t o", o=1).to_broadcast([P, NT, P])
                    link(V.tensor_tensor(y4[:, :, h, :], y4[:, :, h, :], r, ALU.mult))
                    gb = g.rearrange("p (o d) -> p o d", o=1).to_broadcast([P, NT, P])
                    ins = V.tensor_tensor(y4[:, :, h, :], y4[:, :, h, :], gb, ALU.mult)
                    if h < HEADS - 1:
                        link(ins)
                    else:
                        ins.then_inc(f_ready, tick("f_ready", ("y", BR_A)))

            def rotary(raw_t, rot_key, dsts, rows=P):
                link(V.tensor_tensor(SP4[1][0:rows, :], raw_t[0:rows, :], cos[0:rows, :], ALU.mult))
                dve.wait_ge(misc_ready, at("misc_ready", rot_key))
                V.tensor_tensor(SP4[2][0:rows, :], ps[0:rows, bank(en, rot_key), :], sin[0:rows, :], ALU.mult).then_inc(out_free, tick("out_free", rot_key))
                dve.wait_ge(out_free, en.mine("out_free"))
                for d, part in dsts:
                    link(V.tensor_tensor(d, SP4[1][part, :], SP4[2][part, :], ALU.add))

            def add_out(key, k, src_sem="gemm_steps"):
                dve.wait_ge(gemm_steps, at("gemm_steps", key))
                xk = xT[:, k * S:(k + 1) * S]
                V.tensor_tensor(xk, ps[:, bank(en, key), :], xk, ALU.add).then_inc(out_free, tick("out_free", key))

            def norm(key, root, gain):
                normalise(key, root, KD, lambda k: xT[:, k * S:(k + 1) * S], gain,
                          lambda k: (h_hi[:, k * S:(k + 1) * S], h_lo[:, k * S:(k + 1) * S]))

            dve.sem_inc(out_free, tick("out_free", "credit", 4))
            dve.sem_inc(o_free, tick("o_free", "credit", 2))
            V.memset(epst[:], EPS).then_inc(dve_chain, tick("dve_chain"))
            dve.wait_ge(dve_chain, en.mine("dve_chain"))
            dve.wait_ge(lam_in, 16)
            dl = y[:, 0:L * 256].rearrange("p (l f d) -> p l f d", l=L, f=4)
            for a in range(2):
                pr = tmp[:, a * 128:(a + 1) * 128].rearrange("p (l d) -> p l d", l=L)
                link(V.tensor_tensor(pr, dl[:, :, 2 * a, :], dl[:, :, 2 * a + 1, :], ALU.mult))
                ins = V.tensor_reduce(neglam[:, 4 + 2 * a:6 + 2 * a], pr, AX.X, ALU.add)
                if a == 0:
                    link(ins)
                else:
                    ins.then_inc(f_ready, tick("f_ready", "lam"))
            for k in range(KD):
                evac(("x", k), xT[:, k * S:(k + 1) * S], ready="misc_ready")
            dve.wait_ge(small_in, 32)
            dve.wait_ge(const_in, 16)
            dve.wait_ge(act_ready, at("act_ready", "lam"))
            link(V.tensor_tensor(neglam[:, 0:2], neglam[:, 6:8], neglam[:, 4:6], ALU.subtract))
            lam0 = cst[:, C_LAM:C_LAM + L]
            link(V.tensor_tensor(neglam[:, 0:2], neglam[:, 0:2], lam0, ALU.subtract))
            link(V.tensor_scalar(neglam[:, 2:4], lam0, -1.0, 1.0, ALU.mult, ALU.add))

            with en.layers(dve):
                nmix = lambda k: col(vecs, en.layer, V_NM + k)
                norm("n1", "x", nmix)
                lo_part(sw_lo[:], vecs_slice(vecs, en.layer, V_SW, KD * SWC), sw_hi[:], "sw")

                def token_scalars():
                    dve.wait_ge(misc_ready, at("misc_ready", "tok"))
                    tok = ps[:, bank(en, "tok"), 0:NT * 28].rearrange("p (t c) -> p t c", t=NT)
                    z4 = fz[:, 0:16].rearrange("p (t h) -> p t h", t=NT)
                    bf = vecs_slice(vecs, en.layer, V_BF, HEADS).rearrange("p (o h) -> p o h", o=1).to_broadcast([P, NT, HEADS])
                    link(V.tensor_tensor(z4, tok[:, :, 0:4], bf, ALU.add))
                    V.tensor_copy(dgate[:].rearrange("p (t c) -> p t c", t=NT), tok[:, :, 4:28]).then_inc(out_free, tick("out_free", "tok"))
                    link(V.tensor_scalar(fz[:, 16:32], fz[:, 0:16], -1.0, None, ALU.mult))
                    V.tensor_tensor(fz[:, 16:32], fz[:, 16:32], fz[:, 0:16], ALU.max).then_inc(f_ready, tick("f_ready", "tok"))

                def fm(br, scale, t):
                    cols = slice(t % 4 * S, (t % 4 + 1) * S)
                    if br == BR_A and t < 4:
                        evac((br, "fm", t), None, scale, [(q_[0:64, cols], lambda s: s[0:64, :]),
                                                          (q2_[64:128, cols], lambda s: s[64:128, :])])
                    else:
                        evac((br, "fm", t), (q_ if t < 4 else k_)[:, cols], scale if t < 4 else 1.0)

                V.memset(q_[64:128, :], 0.0).then_inc(dve_chain, tick("dve_chain"))
                V.memset(q2_[0:64, :], 0.0).then_inc(dve_chain, tick("dve_chain"))
                for t in range(8):
                    fm(BR_A, 64 ** -0.5, t)
                evac("kr", None, srcs=[(SP4[0][0:SWC, :], lambda s: s[0:SWC, :])], ready="misc_ready")
                for t in range(NT):
                    evac((BR_A, "v", t), v_[:, t * S:(t + 1) * S])
                rotary(SP4[0], "krrot", [(kpe[0:64, :], slice(0, 64))], ROPE)
                token_scalars()
                attend(BR_A)
                for j, key in enumerate(("cq", "ckv")):
                    for c in range(2):
                        evac((key, c), cfl[:, (2 * j + c) * S:(2 * j + c + 1) * S])
                keep_y(BR_A)
                dve.wait_ge(act_ready, at("act_ready", "flog"))
                link(V.tensor_scalar(fz[:, 0:16], fz[:, 0:16], 0.0, None, ALU.min))
                link(V.tensor_tensor(fz[:, 0:16], fz[:, 16:32], fz[:, 0:16], ALU.subtract))
                for t in range(8):
                    fm(BR_C, P ** -0.5, t)
                    if t < 2:
                        j, key, vg = ((1, "ckv", V_NKV), (0, "cq", V_NQ))[t]
                        normalise(key, key, 2, lambda c: cfl[:, (2 * j + c) * S:(2 * j + c + 1) * S],
                                  lambda c: col(vecs, en.layer, vg + c),
                                  lambda c: (cn_hi[j][:, c * S:(c + 1) * S], cn_lo[j][:, c * S:(c + 1) * S]))
                for t in range(NT):
                    evac((BR_C, "v", t), v_[:, t * S:(t + 1) * S])
                for h in range(HEADS):
                    if h:
                        dve.wait_ge(misc_ready, at("misc_ready", ("negc", h - 1)))
                    src = fz[:, 0:16].rearrange("p (t h) -> p t h", t=NT)[:, :, h:h + 1].to_broadcast([P, NT, P])
                    V.tensor_copy(nlfb.rearrange("p (t d) -> p t d", t=NT), src).then_inc(f_ready, tick("f_ready", ("nlf", h)))
                    evac(("negc", h), negc[:, h * S:(h + 1) * S], ready="misc_ready")
                dve.wait_ge(out_free, en.mine("out_free"))
                attend(BR_C)
                scale = (128 + 64) ** -0.5
                for h in range(HEADS):
                    evac(("bq", h), bq[:, h * S:(h + 1) * S], scale)
                keep_y(BR_C)
                for pr in range(2):
                    evac(("bqp", pr), SP4[0] if pr == 0 else SP4[3], scale)
                dve.wait_ge(f_split, en.mine("f_split"))
                dve.wait_ge(out_free, en.mine("out_free"))
                for pr in range(2):
                    rotary(SP4[0] if pr == 0 else SP4[3], ("bqrot", pr),
                           [(bqp[0:64, (2 * pr + e) * S:(2 * pr + e + 1) * S], slice(64 * e, 64 * e + 64)) for e in range(2)])
                for h in range(HEADS):
                    evac(("bk", h), bk[:, h * S:(h + 1) * S])
                for t in range(NT):
                    evac(("bv", t), bv[:, t * S:(t + 1) * S])
                attend(BR_B)
                for j in range(2):
                    key = ("dc", j)
                    dve.wait_ge(gemm_steps, at("gemm_steps", key))
                    pe = vecs_slice(vecs, en.layer, V_PE + 16 * j, 16)
                    zz = z[j].rearrange("p (l g c) -> p l g c", l=16, g=2)
                    for g in range(2):
                        for e in range(2):
                            rows = slice(64 * e, 64 * e + 64)
                            src = ps[64 * g:64 * g + 64, bank(en, key), :]
                            for half in range(2):
                                s3 = src[:, 16 * half:16 * half + 16 * NCMP].rearrange("p (c l e) -> p l e c", l=8, e=2)[:, :, e, :]
                                d3 = zz[rows, 8 * half:8 * half + 8, g, :]
                                pb = pe[rows, 8 * half:8 * half + 8].rearrange("p (l o) -> p l o", o=1).to_broadcast([64, 8, NCMP])
                                ins = V.tensor_tensor(d3, s3, pb, ALU.add)
                                if g + e + half == 3:
                                    ins.then_inc(out_free, tick("out_free", key))
                                else:
                                    ins.then_inc(dve_chain, tick("dve_chain"))
                    dve.wait_ge(dve_chain, en.mine("dve_chain"))
                    dve.wait_ge(out_free, en.mine("out_free"))
                    dve.sem_inc(f_ready, tick("f_ready", ("z", j)))
                keep_y(BR_B)
                evac("dks", dks)
                lo_part(z_lo[0][:], z[0], z_hi[0][:], ("z", 0))
                evac("dkw", dkw)
                lo_part(z_lo[1][:], z[1], z_hi[1][:], ("z", 1))
                V.memset(dq[64:128, 0:4 * S], 0.0).then_inc(dve_chain, tick("dve_chain"))
                V.memset(dq[0:64, 4 * S:8 * S], 0.0).then_inc(dve_chain, tick("dve_chain"))
                for t in range(4):
                    evac(("dq", t), None, NSA_D ** -0.5, [(dq[64 * g:64 * g + 64, (t + 4 * g) * S:(t + 4 * g + 1) * S],
                                                          (lambda s, g=g: s[64 * g:64 * g + 64, :])) for g in range(2)])
                link(V.tensor_copy(w2c, vecs_slice(vecs, en.layer, V_W2, P)))
                for j in range(2):
                    key = ("hid", j)
                    dve.wait_ge(gemm_steps, at("gemm_steps", key))
                    V.tensor_copy(hid[:, 62 * j:62 * j + 62], ps[:, bank(en, key), 0:62]).then_inc(out_free, tick("out_free", key))
                dve.wait_ge(out_free, en.mine("out_free"))
                dve.sem_inc(f_ready, tick("f_ready", "hid"))
                for t in range(NT):
                    evac(("dv", t), dv[:, t * 256:(t + 1) * 256], srcs=[(dv[:, t * 256:(t + 1) * 256], lambda s: s[:, 0:256])])
                evac("kc", None, srcs=[(kc[:, 0:NCMP], lambda s: s[:, 0:NCMP])], ready="misc_ready")
                evac("vc", None, srcs=[(vc[0:NCMP, :], lambda s: s[0:NCMP, 0:128])], ready="misc_ready")
                attend(BR_D)
                keep_y(BR_D)
                dve.wait_ge(out_free, en.mine("out_free"))
                V.memset(merged, 0.0).then_inc(dve_chain, tick("dve_chain", "merged"))
                with en.turns(dve, "gate", 2) as g:
                    for j in range(2):
                        for c in range(4):
                            dve.wait_ge(f_hi, at("f_hi", ("y", j, c)))
                            V.tensor_tensor(y_lo[j][:, c * S:(c + 1) * S], yT[:, bass.ds((g * 2 + j) * 4 * S + c * S, S)],
                                            y_hi[j][:, c * S:(c + 1) * S].bitcast(F32), ALU.subtract).then_inc(
                                f_split, tick("f_split", ("y", j, c)))
                        dve.wait_ge(dve_chain, at("dve_chain", "merged"))
                        for dt in range(8):
                            dve.wait_ge(act_ready, at("act_ready", ("sg", j, dt)))
                            dve.sem_inc(out_free, tick("out_free", ("gate", j, dt, 0)))
                            dve.wait_ge(gemm_steps, at("gemm_steps", ("gate", j, dt, 1)))
                            V.tensor_tensor(tmp, ps[:, bank(en, ("gate", j, dt, 1)), :], sg[dt % 2], ALU.mult).then_inc(
                                f_ready, tick("f_ready", ("mul", j, dt)))
                            dve.wait_ge(f_ready, en.mine("f_ready"))
                            mk = merged[:, dt * S:(dt + 1) * S]
                            V.tensor_tensor(mk, mk, tmp, ALU.add).then_inc(out_free, tick("out_free", ("gate", j, dt, 1)))
                            dve.wait_ge(out_free, en.mine("out_free"))
                for k in range(KD):
                    lo_part(m_lo[:, k * S:(k + 1) * S], merged[:, k * S:(k + 1) * S], m_hi[:, k * S:(k + 1) * S], ("m", k))
                for k in range(KD):
                    add_out(("wo", k), k)
                dve.wait_ge(out_free, en.mine("out_free"))
                norm("n2", "n2", lambda k: col(vecs, en.layer, V_NF + k))
                for half, (c0, nch) in enumerate(HALVES):
                    with en.turns(dve, ("up", half), nch // 2) as g:
                        for j in range(2):
                            for part, dst in ((0, ua[j]), (1, ug[j])):
                                key = ("up", half, j, part)
                                dve.wait_ge(act_ready, at("act_ready", key))
                                cv = V_CONV + (part * FFC + c0 + j) * 4
                                b = ps[:, bank(en, key), :]
                                link(V.scalar_tensor_tensor(dst[:, 1:S], b[:, 0:S - 1], col(vecs, en.layer, cv + 1, g, 8),
                                                            dst[:, 1:S], ALU.mult, ALU.add))
                                V.scalar_tensor_tensor(dst[:, 2:S], b[:, 0:S - 2], col(vecs, en.layer, cv, g, 8),
                                                       dst[:, 2:S], ALU.mult, ALU.add).then_inc(out_free, tick("out_free", key))
                                if part == 0:
                                    dve.wait_ge(out_free, en.mine("out_free"))
                                    dve.sem_inc(f_ready, tick("f_ready", ("conv", half, j)))
                            dve.wait_ge(out_free, en.mine("out_free"))
                            dve.wait_ge(act_ready, at("act_ready", ("silu", half, j)))
                            dve.wait_ge(f_split, at("f_split", ("act", half, j), -2))
                            V.tensor_tensor(uf[j], us[j], ug[j], ALU.mult).then_inc(f_ready, tick("f_ready", ("act", half, j)))
                            dve.wait_ge(f_hi, at("f_hi", ("act", half, j)))
                            V.tensor_tensor(a_lo[:, bass.ds((g * 2 + j) * S, S)], uf[j],
                                            a_hi[:, bass.ds((g * 2 + j) * S, S)].bitcast(F32), ALU.subtract).then_inc(
                                f_split, tick("f_split", ("act", half, j)))
                    for k in range(KD):
                        add_out(("down", half, k), k)
                dve.wait_ge(act_ready, at("act_ready", ("n1", "root")))
                dve.sem_inc(out_free, tick("out_free", "pad", -counts.now["out_free"] % 4))
            dve.wait_ge(act_ready, en.after("act_ready", ("n1", "root")))
            link(V.reciprocal(SP4[3], SP4[2]))
            for k in range(KD):
                xk = xT[:, k * S:(k + 1) * S]
                V.scalar_tensor_tensor(xk, xk, nf[:, k:k + 1], SP4[3], ALU.mult, ALU.mult).then_inc(f_ready, tick("f_ready", ("n3", k)))
            for t in range(NT):
                for half in range(2):
                    dve.wait_ge(misc_ready, at("misc_ready", ("o", t, half)))
                    V.tensor_copy(stage[:, t * D + half * S:t * D + (half + 1) * S], ps[:, bank(en, ("o", t, half)), :]).then_inc(
                        out_ready, tick("out_ready", (t, half)))
                    dve.wait_ge(out_ready, en.mine("out_ready"))
                    dve.sem_inc(out_free, tick("out_free", ("o", t, half)))

        @block.tensor
        def _(pe):
            en = Engine(counts)
            tick, at = en.tick, en.at
            MM = nc.tensor.matmul
            half_tiles = [0]

            def three(dst, a, b, start, stop):
                MM(dst, a[0], b[0], start=start, stop=False)
                MM(dst, a[0], b[1], start=False, stop=False)
                return MM(dst, a[1], b[0], start=False, stop=stop)

            def free_bank(key):
                pe.wait_ge(out_free, at("out_free", key, -4))
                return ps[:, bank(en, key), :]

            def step(ins, key=None, by=1):
                ins.then_inc(gemm_steps, tick("gemm_steps", key, by))

            def enter_block(b):
                n = b + 1
                if en.loop is not None:
                    n = en.turn * en.loop_blocks + n
                pe.wait_ge(lo_done, en.layer * NBLK + n)

            def gemm(b, t0, key, rhs, nk, width=S, waits=None, tail=0):
                dst = free_bank(key)[:, 0:width]
                for k in range(nk):
                    t = t0 + k
                    if t % TILES == 0:
                        enter_block(b + t // TILES)
                    if waits is not None:
                        waits(k)
                    ins = three(dst, wt(b, t), rhs(k), k == 0, k == nk - 1)
                    last = k == nk - 1
                    if t % 2 == 1:
                        step(ins, key if last else None, 1 + (tail if last else 0))

            def h(k):
                return h_hi[:, k * S:(k + 1) * S], h_lo[:, k * S:(k + 1) * S]

            def hcols(k, t):
                c = k * S + t * P
                return h_hi[:, c:c + P], h_lo[:, c:c + P]

            def misc(ins, key):
                ins.then_inc(misc_ready, tick("misc_ready", key))

            def sum_squares(key, k):
                pe.wait_ge(sq_ready, at("sq_ready", (key, k)))
                MM(ps[:, 4, :], ones, SP4[k % 2], start=k == 0, stop=k == KD - 1).then_inc(sq_used, tick("sq_used", (key, k)))

            def onto_residual(b, key, rhs, nk, norm_key=None, waits=None):
                for dt in range(KD):
                    gemm(b, nk * dt, key + (dt,), rhs, nk, waits=waits if dt == 0 else None)
                    if norm_key and dt >= 1:
                        sum_squares(norm_key, dt - 1)
                if norm_key:
                    sum_squares(norm_key, KD - 1)

            def values(b, key, width, nk_block, lhs, nblocks):
                keys = [key + (t,) for t in range(NT)]
                dsts = [free_bank(k)[:, 0:width] for k in keys]
                total = nblocks * nk_block
                per_step = NT * nk_block // STEPS
                for bb in range(nblocks):
                    enter_block(b + bb)
                    s = (b + bb) % 2
                    for t in range(NT):
                        for kk in range(nk_block):
                            k = bb * nk_block + kk
                            w = (w_hi[s][:, kk * width:(kk + 1) * width], w_lo[s][:, kk * width:(kk + 1) * width])
                            ins = three(dsts[t], lhs(k, t), w, k == 0, k == total - 1)
                            g = t * nk_block + kk
                            if (g + 1) % per_step == 0:
                                step(ins, keys[t] if k == total - 1 else None)

            def scores(br, n):
                _, hd, part, i, m = units[br][n]
                w = unit_width(br, part, i)
                dst = ps[:, n % 4, 0:w]
                qs = slice(hd * S + i * P, hd * S + (i + 1) * P)
                if br == BR_A:
                    ins = MM(dst, (q_, q2_)[part][:, qs], k_[:, hd * S:hd * S + w], start=True, stop=True)
                elif br == BR_C:
                    MM(dst, q_[:, qs], k_[:, hd * S:hd * S + w], start=True, stop=False)
                    ins = MM(dst[:, w - P:w], ident, cst[:, C_CM + 3 * P:C_CM + 4 * P], start=False, stop=True)
                elif br == BR_B:
                    MM(dst, bq[:, qs], bk[:, hd * S:hd * S + w], start=True, stop=False)
                    ins = MM(dst, bqp[0:64, qs], kpe[0:64, 0:w], start=False, stop=True)
                else:
                    g = hd // 4
                    if part == 2:
                        for ii in range(NT):
                            ins = MM(dst[:, ii * NCMP:(ii + 1) * NCMP], dq[:, hd * S + ii * P:hd * S + (ii + 1) * P],
                                     kc[:, 0:NCMP], start=True, stop=True)
                    else:
                        kk = dks if part == 0 else dkw
                        e = (i + 1) * P
                        ins = MM(dst, dq[:, qs], kk[:, e - w:e], start=True, stop=True)
                ins.then_inc(s_ready, tick("s_ready", (br, n)))

            def turn(br, n):
                _, hd, part, i, m = units[br][n]
                pe.wait_ge(p_ready, at("p_ready", (br, n)))
                pt = ps[:, 4 + n % 2, :]
                if br == BR_D and part == 2:
                    for ii in range(NT):
                        ins = nc.tensor.transpose(pt[0:NCMP, ii * P:(ii + 1) * P], SP4[n % 4][:, ii * NCMP:(ii + 1) * NCMP], ident)
                else:
                    for j in range(unit_width(br, part, i) // P):
                        ins = nc.tensor.transpose(pt[:, j * P:(j + 1) * P], SP4[n % 4][:, j * P:(j + 1) * P], ident)
                ins.then_inc(t_ready, tick("t_ready", (br, n)))

            def weigh(br, n):
                _, hd, part, i, m = units[br][n]
                pe.wait_ge(pt_ready, at("pt_ready", (br, n)))
                if i == 0:
                    pe.wait_ge(o_free, at("o_free", m, -2))
                ob = ps[:, 6 + m % 2, :]
                pt = PT2[n % 2]
                if br == BR_D:
                    g = hd // 4
                    if part == 2:
                        for ii in range(NT):
                            ins = MM(ob[:, ii * NSA_D:(ii + 1) * NSA_D], pt[0:NCMP, ii * P:(ii + 1) * P],
                                     vc[0:NCMP, g * NSA_D:(g + 1) * NSA_D], start=True, stop=True)
                    else:
                        nb = unit_width(br, part, i) // P
                        for jj in range(nb):
                            j = i + 1 - nb + jj
                            c = j * 256 + part * 128 + g * NSA_D
                            ins = MM(ob[:, i * NSA_D:(i + 1) * NSA_D], pt[:, jj * P:(jj + 1) * P], dv[:, c:c + NSA_D],
                                     start=jj == 0, stop=jj == nb - 1)
                else:
                    vv = bv if br == BR_B else v_
                    for j in range(i + 1):
                        ins = MM(ob[:, i * P:(i + 1) * P], pt[:, j * P:(j + 1) * P], vv[:, j * S + hd * P:j * S + (hd + 1) * P],
                                 start=j == 0, stop=j == i)
                ins.then_inc(pv_done, tick("pv_done", (br, n)))

            def attend(br, last_out):
                n_u = len(units[br])
                pe.wait_ge(out_free, at("out_free", last_out))
                scores(br, 0)
                scores(br, 1)
                for n in range(n_u + 1):
                    if n + 2 < n_u:
                        scores(br, n + 2)
                    if n < n_u:
                        turn(br, n)
                    if n >= 1:
                        weigh(br, n - 1)

            def turn_y(br):
                pe.wait_ge(f_ready, at("f_ready", ("y", br)))
                for c in range(4):
                    key = ("yT", br, c)
                    dst = free_bank(key)
                    for t in range(NT):
                        ins = nc.tensor.transpose(dst[:, t * P:(t + 1) * P], y[:, t * S + c * P:t * S + (c + 1) * P], ident)
                    misc(ins, key)

            pe.wait_ge(ident_in, 16)
            for k in range(KD):
                pe.wait_ge(x_part_in[k // 2], 16)
                dst = free_bank(("x", k))
                for t in range(NT):
                    ins = nc.tensor.transpose(dst[:, t * P:(t + 1) * P], stage[:, t * D + k * P:t * D + (k + 1) * P], ident)
                misc(ins, ("x", k))
            for k in range(KD):
                sum_squares("x", k)

            with en.layers(pe):
                normed = lambda key: (lambda k: pe.wait_ge(f_split, at("f_split", (key, k))))
                sw = lambda c, w: (sw_hi[:, c:c + w], sw_lo[:, c:c + w])
                for t in range(8):
                    gemm(B_A, 8 * t, (BR_A, "fm", t), h, KD, waits=normed("n1") if t == 0 else None)
                dst = free_bank("kr")
                pe.wait_ge(f_split, at("f_split", "sw"))
                for k in range(KD):
                    ins = three(dst[0:SWC, :], sw(k * SWC, SWC), h(k), k == 0, k == KD - 1)
                misc(ins, "kr")
                values(B_A + 4, (BR_A, "v"), S, 4, hcols, 2)
                dst, dst_tok = free_bank("krrot"), free_bank("tok")
                pe.wait_ge(out_free, at("out_free", "kr"))
                misc(MM(dst, rot[0:ROPE, :], SP4[0][0:ROPE, :], start=True, stop=True), "krrot")
                for t in range(NT):
                    ins = nc.tensor.transpose(dst_tok[:, t * 28:(t + 1) * 28], SP4[0][ROPE:SWC, t * P:(t + 1) * P], ident[ROPE:SWC, ROPE:SWC])
                misc(ins, "tok")
                attend(BR_A, "tok")
                for j, key in enumerate(("cq", "ckv")):
                    for c in range(2):
                        gemm(B_LAT + j, 8 * c, (key, c), h, KD)
                turn_y(BR_A)
                for t in range(8):
                    gemm(B_C, 8 * t, (BR_C, "fm", t), h, KD)
                    if t < 2:
                        key = ("ckv", "cq")[t]
                        dst = free_bank((key, "n"))
                        for c in range(2):
                            pe.wait_ge(sq_ready, at("sq_ready", (key, c)))
                            misc(MM(dst, ones, SP4[c], start=c == 0, stop=c == 1), (key, "n", c))
                values(B_C + 4, (BR_C, "v"), S, 4, hcols, 2)
                for hd in range(HEADS):
                    dst = free_bank(("negc", hd))
                    pe.wait_ge(f_ready, at("f_ready", ("nlf", hd)))
                    for t in range(NT):
                        ins = MM(dst[:, t * P:S], nlfb[:, t * P:(t + 1) * P], tri[:, 0:S - t * P], start=t == 0, stop=t == NT - 1)
                    misc(ins, ("negc", hd))
                attend(BR_C, ("negc", HEADS - 1))
                lat = lambda j: (lambda c: (cn_hi[j][:, c * S:(c + 1) * S], cn_lo[j][:, c * S:(c + 1) * S]))
                pe.wait_ge(f_split, at("f_split", ("cq", 1)))
                for t in range(6):
                    key = ("bq", t) if t < 4 else ("bqp", t - 4)
                    gemm(B_B, 2 * t, key, lat(0), 2, tail=2 if t == 5 else 0)
                    if t == 3:
                        turn_y(BR_C)
                for pr in range(2):
                    dst = free_bank(("bqrot", pr))
                    pe.wait_ge(out_free, at("out_free", ("bqp", pr)))
                    misc(MM(dst, rot, SP4[0] if pr == 0 else SP4[3], start=True, stop=True), ("bqrot", pr))
                pe.wait_ge(f_split, at("f_split", ("ckv", 1)))
                for t in range(4):
                    gemm(B_B + 1, 2 * t, ("bk", t), lat(1), 2)
                s = (B_B + 1) % 2
                for t in range(NT):
                    dst = free_bank(("bv", t))
                    for k in range(2):
                        c = 8 * P + k * S
                        lhs = (cn_hi[1][:, k * S + t * P:k * S + (t + 1) * P], cn_lo[1][:, k * S + t * P:k * S + (t + 1) * P])
                        ins = three(dst, lhs, (w_hi[s][:, c:c + S], w_lo[s][:, c:c + S]), k == 0, k == 1)
                    step(ins, ("bv", t))
                attend(BR_B, ("bv", NT - 1))
                for t, key in enumerate((("dc", 0), ("dc", 1), "dks", "dkw")):
                    gemm(B_D, 8 * t, key, h, KD)
                    if t == 1:
                        turn_y(BR_B)
                for t in range(4):
                    gemm(B_D + 2, 8 * t, ("dq", t), h, KD)
                for j in range(2):
                    pe.wait_ge(f_split, at("f_split", ("z", j)))
                    zs = lambda k: (z_hi[j][:, k * 62:(k + 1) * 62], z_lo[j][:, k * 62:(k + 1) * 62])
                    gemm(B_D + 4 + j, 0, ("hid", j), zs, 16, width=62)
                values(B_D + 6, ("dv",), 256, 8, hcols, 1)
                dst = free_bank("kc")
                pe.wait_ge(act_ready, at("act_ready", "hid"))
                for g in range(2):
                    ins = MM(dst[64 * g:64 * g + 64, 0:NCMP], w2c[:, 0:64], hid[:, g * NCMP:(g + 1) * NCMP], start=True, stop=True)
                misc(ins, "kc")
                dst = free_bank("vc")
                for g in range(2):
                    ins = MM(dst[0:NCMP, g * 64:(g + 1) * 64], hid[:, 62 + g * NCMP:62 + (g + 1) * NCMP], w2c[:, 64:128], start=True, stop=True)
                misc(ins, "vc")
                attend(BR_D, "vc")
                turn_y(BR_D)
                en.loop_blocks = 12
                with en.turns(pe, "gate", 2):
                    for j in range(2):
                        ys = lambda c: (y_hi[j][:, c * S:(c + 1) * S], y_lo[j][:, c * S:(c + 1) * S])
                        for dt in range(8):
                            t0 = 96 * j + 12 * dt
                            gemm(B_GATE, t0, ("gate", j, dt, 0), h, KD)
                            wy = (lambda c: pe.wait_ge(f_split, at("f_split", ("y", j, c)))) if dt == 0 else None
                            gemm(B_GATE, t0 + 8, ("gate", j, dt, 1), ys, 4, waits=wy)
                mm = lambda k: (m_hi[:, k * S:(k + 1) * S], m_lo[:, k * S:(k + 1) * S])
                onto_residual(B_OUT, ("wo",), mm, KD, "n2", lambda k: pe.wait_ge(f_split, at("f_split", ("m", k))))
                b = B_MLP
                for half, (c0, nch) in enumerate(HALVES):
                    en.loop_blocks = 2
                    with en.turns(pe, ("up", half), nch // 2):
                        for j in range(2):
                            for part in range(2):
                                w2 = normed("n2") if half == 0 and j == part == 0 else None
                                gemm(b, 16 * j + 8 * part, ("up", half, j, part), h, KD, waits=w2)
                    b += nch
                    aa = lambda k: (a_hi[:, k * S:(k + 1) * S], a_lo[:, k * S:(k + 1) * S])
                    pe.wait_ge(f_split, at("f_split", ("act", half, 1)))
                    onto_residual(b, ("down", half), aa, nch, "n1" if half else None)
                    b += nch // 2
            for t in range(NT):
                for half in range(2):
                    dst = free_bank(("o", t, half))
                    for c in range(4):
                        k = half * 4 + c
                        pe.wait_ge(f_ready, at("f_ready", ("n3", k)))
                        ins = nc.tensor.transpose(dst[:, c * P:(c + 1) * P], xT[:, k * S + t * P:k * S + (t + 1) * P], ident)
                    misc(ins, ("o", t, half))

    return counts


def vecs_slice(vecs, layer, c, n):
    return vecs[:, bass.ds(layer * NV + c, n)]


def col(vecs, layer, c, turn=None, per_turn=0):
    at = layer * NV + c
    if turn is not None:
        at = turn * per_turn + at
    return vecs[:, bass.ds(at, 1)]


def unit_width(br, part, i):
    if br == BR_D and part == 2:
        return NT * NCMP
    if br == BR_D and part == 1:
        return P * min(i + 1, WIN // P + 1)
    return P * (i + 1)


def _tiles(w):
    k, n = w.shape
    return w.reshape(k // P, P, n // P, P).transpose(2, 0, 1, 3).reshape(-1, P, P)


def _blocks(tiles):
    return tiles.reshape(-1, TILES, P, P).transpose(0, 2, 1, 3).reshape(-1, P, BLK)


def _wide(w, k):
    n = w.shape[1]
    return w.reshape(-1, k, P, n).transpose(0, 2, 1, 3).reshape(-1, P, k * n)


def _weights(i, l):
    w = i["w_in"][l]
    cuts = np.cumsum([512, 512, 512, 256, 256, 64, 512, 512, 512, 4, 512, 768, 24])
    aq, ak, av, cq, ckv, kr, fq, fk, fv, cf, dq, dkv, dg, gate = np.split(w, cuts, axis=1)
    fm = lambda *ws: _blocks(_tiles(np.concatenate(ws, axis=1)))
    dq = dq.reshape(D, NSA_G, NSA_H // NSA_G, NSA_D).transpose(0, 2, 1, 3).reshape(D, -1)
    uq = i["mla_w_uq"][l].reshape(256, HEADS, 192)
    ukv = i["mla_w_ukv"][l].reshape(256, HEADS, 256)
    t = _tiles(np.concatenate([uq[:, :, :P].reshape(256, -1), uq[:, :, P:].reshape(256, -1)], axis=1))
    uq = _blocks(np.concatenate([t, np.zeros((4, P, P), np.float32)]))
    kn = _tiles(ukv[:, :, :P].reshape(256, 512)).transpose(1, 0, 2).reshape(P, 8 * P)
    vv = _wide(ukv[:, :, P:].reshape(256, 512), 2)[0]
    ukv = np.concatenate([kn, vv], axis=1)[None]
    k = dkv.reshape(D, 3, 2, P)
    parts = [fm(aq, ak), _wide(av, 4), fm(cq, ckv), fm(fq, fk), _wide(fv, 4), uq, ukv,
             fm(k[:, 0, 0], k[:, 0, 1], k[:, 1, 0], k[:, 2, 0]), fm(dq)]
    parts += [_blocks(i["nsa_cmp_w1"][l, j].reshape(16, P, P)) for j in range(2)]
    parts += [_wide(np.concatenate([k[:, 1, 1], k[:, 2, 1]], axis=1), 8)]
    tiles = []
    for n in range(4):
        g, b = _tiles(gate[:, n * D:(n + 1) * D]), _tiles(i["w_branch"][l, n])
        for dt in range(8):
            tiles += [g[dt * 8:dt * 8 + 8], b[dt * 4:dt * 4 + 4]]
    parts += [_blocks(np.concatenate(tiles)), fm(i["w_out"][l])]
    up = _tiles(i["w_up"][l]).reshape(2, FFC, 8, P, P).transpose(1, 0, 2, 3, 4)
    for c0, n in HALVES:
        parts.append(_blocks(up[c0:c0 + n].reshape(-1, P, P)))
        parts.append(_blocks(_tiles(i["w_down"][l, c0 * P:(c0 + n) * P])))
    return np.concatenate(parts)


def _small(i, l):
    v = np.zeros((P, NV), np.float32)
    feat = lambda a: np.ascontiguousarray(a.reshape(-1, P).T)
    v[:, V_NM:V_NM + 8] = feat(i["norm_mix"][l])
    v[:, V_NF:V_NF + 8] = feat(i["norm_ffn"][l])
    v[:, V_NQ:V_NQ + 2] = feat(i["mla_norm_q"][l])
    v[:, V_NKV:V_NKV + 2] = feat(i["mla_norm_kv"][l])
    conv = np.concatenate([i["conv_w"][l], i["conv_b"][l][None]])
    v[:, V_CONV:V_SW] = conv.reshape(4, 2 * FFC, P).transpose(2, 1, 0).reshape(P, -1)
    w = i["w_in"][l]
    kr, cf, dg = w[:, 2048:2112], w[:, 3648:3652], w[:, 4932:4956]
    v[:, V_SW:V_W2] = np.concatenate([kr, cf, dg], axis=1).reshape(KD, P, SWC).transpose(1, 0, 2).reshape(P, -1)
    v[:, V_W2:V_PE] = np.concatenate([i["nsa_cmp_w2"][l, 0], i["nsa_cmp_w2"][l, 1]], axis=1)
    v[:, V_PE:V_SUB] = i["nsa_cmp_pe"][l].reshape(2, 16, P).transpose(2, 0, 1).reshape(P, 32)
    v[:, V_SUB:V_BF] = i["diff_subln"][l][None]
    v[:, V_BF:] = i["fox_b_f"][l][None]
    return v


def _constants():
    c = np.zeros((P, NCONST), np.float32)
    p = np.arange(P)[:, None]
    c[:, C_ID:C_ID + P] = np.eye(P)
    c[:, C_TRI:C_TRI + S] = np.arange(S)[None] >= p
    dist = p - (np.arange(S)[None] - 3 * P)
    c[:, C_ND:C_ND + S] = np.where(dist >= 0, -dist, NEG)
    c[:, C_CM:C_CM + S] = np.where(dist >= 0, 0, NEG)
    dist = p - (np.arange(3 * P)[None] - WIN)
    c[:, C_NDW:C_NDW + 3 * P] = np.where((dist >= 0) & (dist < WIN), -dist, NEG)
    pos = np.arange(NT)[None, :, None] * P + p[:, :, None]
    dist = pos - (np.arange(NCMP)[None, None] * 16 + 31)
    c[:, C_NDC:C_NDC + NT * NCMP] = np.where(dist >= 0, -dist, NEG).reshape(P, -1)
    c[:, C_ROW:C_ROW + NT] = (dist >= 0).any(axis=2)
    f32 = np.float32
    inv = f32(10000.0) ** (-np.arange(0, 64, 2, dtype=f32) / f32(64))
    ang = (np.arange(S, dtype=f32)[None] * inv[:, None]).astype(f32)
    c[:, C_COS:C_COS + S] = np.tile(np.cos(ang.astype(np.float64)), (4, 1))
    c[:, C_SIN:C_SIN + S] = np.tile(np.sin(ang.astype(np.float64)), (4, 1))
    for b in (0, 64):
        for m in range(32):
            c[b + m + 32, C_ROT + b + m] = -1.0
            c[b + m, C_ROT + b + m + 32] = 1.0
    c[:, C_LAM:C_LAM + L] = [0.8 - 0.6 * math.exp(-0.3 * l) for l in range(L)]
    return c


def kernel(**inputs):
    import concourse.bacc as _bacc
    from concourse.bass_utils import run_bass_kernel_spmd as _run

    i = {k: np.asarray(v) for k, v in inputs.items()}
    arrays = {
        "blob": np.concatenate([_weights(i, l) for l in range(L)]),
        "vec": np.stack([_small(i, l) for l in range(L)]),
        "const": _constants(),
        "dlam": np.ascontiguousarray(np.broadcast_to(i["diff_lambda"].reshape(1, -1), (P, L * 256))),
        "nfin": np.ascontiguousarray(i["norm_final"].reshape(KD, P).T),
        "x_in": np.ascontiguousarray(i["x"][0]),
    }

    def program(known):
        nc = _bacc.Bacc("TRN2", target_bir_lowering=False, num_devices=1)
        args = [nc.dram_tensor(n, a.shape, F32, kind="ExternalInput").ap() for n, a in arrays.items()]
        out = nc.dram_tensor("out", (S, D), F32, kind="ExternalOutput").ap()
        return nc, build(nc, *args, out, known)

    _, known = program(None)
    nc, _ = program(known)
    r = _run(nc, [arrays], core_ids=[0])
    return r.results[0]["out"].reshape(1, S, D)
```

```python
import math
from contextlib import ExitStack, contextmanager

import numpy as np

import concourse.bass as bass
from concourse import mybir

F32 = mybir.dt.float32
F32R = mybir.dt.float32r
ALU = mybir.AluOpType
ACT = mybir.ActivationFunctionType
AX = mybir.AxisListType

P = 128
S, D, L = 512, 1024, 2
NT = S // P
KD = D // P
TILES = 16
BLK = TILES * P
EPS = 1e-6
NEG = -1e30
BR_A, BR_B, BR_C, BR_D = range(4)
HEADS = 4
NSA_H, NSA_G, NSA_D = 8, 2, 64
NCMP = S // 16 - 1
WIN = 256
FFC = 2816 // P
HALVES = ((0, 12), (12, FFC - 12))
B_A, B_LAT, B_C, B_B, B_D = 0, 6, 8, 14, 16
B_GATE = B_D + 7
B_OUT = B_GATE + 24
B_MLP = B_OUT + 4
NBLK = B_MLP + FFC + 8 * FFC // TILES
AHEAD = 4
BEHIND = 5
STEPS = 8
V_NM, V_NF, V_NQ, V_NKV, V_CONV = 0, 8, 16, 18, 20
V_SW = V_CONV + 4 * 2 * FFC
ROPE = 64
SWC = ROPE + 28
V_W2 = V_SW + KD * SWC
V_PE = V_W2 + P
V_SUB = V_PE + 2 * 16
V_BF = V_SUB + P
NV = V_BF + HEADS
C_ID = 0
C_TRI = C_ID + P
C_LAM = C_TRI + 2 * P
C_ND = C_LAM + L
C_CM = C_ND + S
C_NDW = C_CM + S
C_NDC = C_NDW + 3 * P
C_COS = C_NDC + NT * NCMP
C_SIN = C_COS + S
C_ROT = C_SIN + S
C_ROW = C_ROT + P
NCONST = C_ROW + NT


def attention_units():
    units = {b: [] for b in range(4)}
    blocks = lambda m: range(NT)[::1 - 2 * (m % 2)]
    units[BR_A] = [(BR_A, h, part, i, h) for h in range(HEADS) for i in blocks(h) for part in range(2)]
    maps = HEADS
    for br, heads, parts in ((BR_C, HEADS, 1), (BR_B, HEADS, 1), (BR_D, NSA_H, 3)):
        for h in range(heads):
            for part in range(parts):
                these = [0] if br == BR_D and part == 2 else blocks(part if br == BR_D else h)
                units[br] += [(br, h, part, i, maps) for i in these]
                maps += 1
    return units


class Counts:

    def __init__(self, known=None):
        self.known = known
        self.now, self.base, self.stride, self.total, self.trips = {}, {}, {}, {}, {}
        self.loop = None

    def tick(self, name, key=None, by=1):
        self.now[name] = self.now.get(name, 0) + by
        self.base[name, key] = (self.now[name], self.loop)
        return by


class Engine:

    def __init__(self, counts):
        self.c, self.layer, self.turn, self.loop = counts, None, None, None

    def tick(self, name, key=None, by=1):
        return self.c.tick(name, key, by)

    def _value(self, name, n, loop, last=None):
        known = self.c.known
        if known is None:
            return 1
        if loop is not None:
            step = known.stride.get((loop, name), 0)
            if self.loop == loop:
                n = self.turn * step + n if step else n
            else:
                n += step * (known.trips[loop] - 1)
        if self.layer is not None:
            n = self.layer * known.total.get(name, 0) + n
        return n

    def at(self, name, key, off=0):
        if self.c.known is None:
            return 1
        n, loop = self.c.known.base[name, key]
        return self._value(name, n + off, loop)

    def after(self, name, key):
        if self.c.known is None:
            return 1
        return self.c.known.base[name, key][0] + (L - 1) * self.c.known.total[name]

    def mine(self, name):
        return self._value(name, self.c.now[name], self.loop)

    @contextmanager
    def layers(self, e):
        before = dict(self.c.now)
        with e.Fori(0, L) as i:
            self.layer = i
            yield
        for name, n in self.c.now.items():
            per = n - before.get(name, 0)
            if per:
                self.c.total[name] = per
                self.c.now[name] = n + per * (L - 1)
        self.layer = None

    @contextmanager
    def turns(self, e, loop, trips):
        before = dict(self.c.now)
        self.c.loop = self.loop = loop
        with e.Fori(0, trips) as i:
            self.turn = i
            yield i
        self.c.loop = self.loop = self.turn = None
        self.c.trips[loop] = trips
        for name, n in self.c.now.items():
            step = n - before.get(name, 0)
            if step:
                self.c.stride[loop, name] = step
                self.c.now[name] = n + step * (trips - 1)


def build(nc, blob, vec, const, dlam, nfin, x_in, out, known):
    counts = Counts(known)
    units = attention_units()
    with ExitStack() as ctx:
        def sem(name):
            return ctx.enter_context(nc.semaphore(name))

        def sb(name, cols, dt=F32):
            return ctx.enter_context(nc.sbuf_tensor(name, [P, cols], dt))

        xT = sb("xT", KD * S)
        h_hi, h_lo = sb("h_hi", KD * S, F32R), sb("h_lo", KD * S, F32R)
        raw = [sb(f"raw{j}", BLK) for j in range(2)]
        w_hi = [sb(f"w_hi{j}", BLK, F32R) for j in range(2)]
        w_lo = [sb(f"w_lo{j}", BLK, F32R) for j in range(2)]
        cst = sb("cst", NCONST)
        vecs = sb("vecs", L * NV)
        nf = sb("nf", KD)
        lsum, rinv, negm = sb("lsum", 16), sb("rinv", 16), sb("negm", 8)
        dgate, fz, neglam = sb("dgate", 4 * 24), sb("fz", 64), sb("neglam", 8)
        epst, scratch, root_t = sb("epst", 1), sb("scratch", 1), sb("root_t", NT)
        YT, QKV, WORK = 0, 32768, 32768 + 34816
        base = (nc.sbuf_base + 31) // 32 * 32
        region = sb("region", (WORK + 22528) // 4)
        assert nc.sbuf_base == base + WORK + 22528

        def reg(byte, cols):
            return region[:, byte // 4:byte // 4 + cols]

        def overlay(name, byte, cols):
            return nc.alloc_sbuf_tensor_at(name, [P, cols], F32R, offset=base + byte)

        SP4 = [reg(WORK + 2048 * j, S) for j in range(4)]
        PT2 = [reg(WORK + 8192 + 2048 * j, S) for j in range(2)]
        norm_buf = [SP4[0], SP4[1], PT2[0], PT2[1]]
        sq_sum = SP4[0]
        square_of = lambda k: sq_sum if k == 0 else norm_buf[1 + (k - 1) % 3]
        y = reg(WORK + 12288, NT * S)
        tmp = reg(WORK + 20480, S)
        yT = reg(YT, 16 * S)
        sw_hi = overlay("sw_hi", WORK + 12288, KD * SWC)
        sw_lo = overlay("sw_lo", WORK + 12288 + 4 * KD * SWC, KD * SWC)
        q_, k_, v_ = reg(QKV, 4 * S), reg(QKV + 8192, 4 * S), reg(QKV + 16384, NT * S)
        negc = reg(QKV + 24576, 4 * S)
        bq, bqp, bk = reg(QKV, 4 * S), reg(QKV + 8192, 4 * S), reg(QKV + 16384, 4 * S)
        bv, kpe = reg(QKV + 24576, NT * S), reg(QKV + 32768, S)
        q2_ = reg(QKV + 24576, 4 * S)
        nlfb = [SP4[2], SP4[3]]
        mixed = [reg(YT + 8192 + 2048 * j, S) for j in range(2)]
        SP6 = SP4 + [reg(YT + 12288 + 2048 * j, S) for j in range(2)]
        cfl = reg(YT + 3 * 8192, 4 * S)
        cn_hi = [overlay("cq_hi", YT + 3 * 8192 + 4096, 2 * S), overlay("ckv_hi", YT + 8192, 2 * S)]
        cn_lo = [overlay("cq_lo", YT + 3 * 8192, 2 * S), overlay("ckv_lo", YT + 8192 + 4096, 2 * S)]
        dq, dks, dkw = reg(QKV, 8 * S), reg(QKV + 16384, S), reg(QKV + 18432, S)
        dv = reg(QKV + 24576, NT * 256)
        o = QKV + 28672
        kc, vc, w2c, hid = reg(o, 62), reg(o + 248, 128), reg(o + 760, 128), reg(o + 1272, 124)
        hid_t = reg(o + 1792, 2 * P)
        NZ = 16 * 2 * NCMP
        z = [reg(WORK, NZ), reg(WORK + 4096, NZ)]
        z_hi = [overlay(f"z_hi{j}", WORK + 12288 + j * 4 * NZ, NZ) for j in range(2)]
        z_lo = [overlay(f"z_lo{j}", YT + 3 * 8192 + j * 4 * NZ, NZ) for j in range(2)]
        y_hi = [overlay(f"y_hi{j}", QKV + 16384 * j, 4 * S) for j in range(2)]
        y_lo = [overlay(f"y_lo{j}", QKV + 16384 * j + 8192, 4 * S) for j in range(2)]
        merged = reg(WORK, KD * S)
        sg = [reg(WORK + 16384 + 2048 * j, S) for j in range(2)]
        m_hi, m_lo = overlay("m_hi", YT, KD * S), overlay("m_lo", YT + 16384, KD * S)
        a_hi, a_lo = overlay("a_hi", 0, 12 * S), overlay("a_lo", 24576, 12 * S)
        ua = [reg(WORK + 2048 * j, S) for j in range(2)]
        ug = [reg(WORK + 4096 + 2048 * j, S) for j in range(2)]
        us = [reg(WORK + 8192 + 2048 * j, S) for j in range(2)]
        uf = [reg(WORK + 12288 + 2048 * j, S) for j in range(2)]
        stage = reg(0, NT * D)

        ps = ctx.enter_context(nc.psum_tensor("ps", [P, 8, S], F32))

        ident = cst[:, C_ID:C_ID + P]
        tri = cst[:, C_TRI:C_TRI + P]
        ones = cst[:, C_TRI + P:C_TRI + 2 * P]
        rot = cst[:, C_ROT:C_ROT + P]
        cos, sin = cst[:, C_COS:C_COS + S], cst[:, C_SIN:C_SIN + S]

        landed = [sem(f"block_landed{j}") for j in range(2)]
        hi_done = sem("hi_done")
        lo_done = sem("lo_done")
        gemm_steps = sem("gemm_steps")
        misc_ready = sem("misc_ready")
        out_free = sem("out_free")
        f_ready = sem("f_ready")
        f_hi = sem("f_hi")
        f_split = sem("f_split")
        sq_ready = sem("sq_ready")
        act_ready = sem("act_ready")
        dve_chain = sem("dve_chain")
        act_chain = sem("act_chain")
        s_ready = sem("s_ready")
        sb_ready = sem("sb_ready")
        p_ready = sem("p_ready")
        mixed_ready = sem("mixed_ready")
        t_ready = sem("t_ready")
        pt_ready = sem("pt_ready")
        pv_done = sem("pv_done")
        o_free = sem("o_free")
        sq_used = sem("sq_used")
        sums_ready = sem("sums_ready")
        diag_ready = sem("diag_ready")
        ident_in = sem("ident_in")
        const_in = sem("const_in")
        lam_in = sem("lam_in")
        small_in = sem("small_in")
        x_part_in = [sem(f"x_part_in{j}") for j in range(4)]
        stored = sem("stored")
        out_ready = sem("out_ready")

        block = ctx.enter_context(nc.Block())

        def wt(b, t):
            s, c = (b + t // TILES) % 2, t % TILES * P
            return w_hi[s][:, c:c + P], w_lo[s][:, c:c + P]

        def bank(en, key):
            n = 1 if en.c.known is None else en.c.known.base["out_free", key][0] - 4
            return (n - 1) % 4

        @block.sync
        def _(sp):
            sp.dma_start(cst[:, 0:C_ND], const[:, 0:C_ND]).then_inc(ident_in, 16)
            tokens, x3 = stage.rearrange("p (t d) -> p t d", t=NT), x_in.rearrange("(t p) d -> p t d", p=P)
            for j in range(4):
                f = slice(j * 256, (j + 1) * 256)
                sp.dma_start(tokens[:, :, f], x3[:, :, f]).then_inc(x_part_in[j], 16)
            sp.dma_start(raw[0][:], blob[0]).then_inc(landed[0], 16)
            sp.dma_start(vecs[:, 0:NV], vec[0]).then_inc(small_in, 16)
            sp.dma_start(raw[1][:], blob[1]).then_inc(landed[1], 16)
            sp.dma_start(cst[:, C_ND:], const[:, C_ND:]).then_inc(const_in, 16)
            sp.dma_start(vecs[:, NV:].rearrange("p (l v) -> p l v", l=L - 1), vec[1:].rearrange("l p v -> p l v")).then_inc(const_in, 16)
            sp.dma_start(nf[:], nfin).then_inc(const_in, 16)
            with sp.Fori(1, L * NBLK // 2) as i:
                for j in range(2):
                    sp.wait_ge(lo_done, i * 2 + (j - 1))
                    sp.dma_start(raw[j][:], blob[i * 2 + j]).then_inc(landed[j], 16)
            for j in range(2):
                sp.wait_ge(lo_done, L * NBLK + j - 1)
                sp.dma_start(raw[j][:], blob[j]).then_inc(landed[j], 16)
            for t in range(NT):
                sp.wait_ge(out_ready, 2 * (t + 1))
                sp.dma_start(out[t * P:(t + 1) * P, :], stage[:, t * D:(t + 1) * D]).then_inc(stored, 16)
            sp.wait_ge(stored, 16 * NT)

        @block.gpsimd
        def _(pool):
            with pool.Fori(0, L * NBLK // 2 + 1) as i:
                for j in range(2):
                    pool.wait_ge(hi_done, i * 2 + (j + 1))
                    pool.tensor_tensor(w_lo[j][:], raw[j][:], w_hi[j][:].bitcast(F32), ALU.subtract).then_inc(lo_done, 1)

        @block.scalar
        def _(act):
            en = Engine(counts)
            tick, at = en.tick, en.at
            A = nc.scalar.activation

            def split_block(b):
                if b >= 2:
                    n = STEPS * (b - 1)
                    act.wait_ge(gemm_steps, at_block(n))
                slot = b % 2
                g = b // 2
                g = en.layer * (NBLK // 2) + g if en.layer is not None else g
                if en.loop is not None:
                    g = en.turn * (en.loop_blocks // 2) + g
                act.wait_ge(landed[slot], g * 16 + 16)
                A(w_hi[slot][:], raw[slot][:], ACT.Copy).then_inc(hi_done, 1)

            def at_block(n):
                if en.loop is not None:
                    n = en.turn * (en.loop_blocks * STEPS) + n
                return en.layer * (NBLK * STEPS) + n

            def blocks(b, n):
                for j in range(b, b + n):
                    split_block(j + 2)

            def preload(func):
                A(scratch[:, 0:1], epst[:, 0:1], func)

            def split_hi(dst, src, key, computed=True):
                if computed:
                    act.wait_ge(f_ready, at("f_ready", key))
                A(dst, src, ACT.Copy).then_inc(f_hi, tick("f_hi", key))

            def square(key, k, ready):
                act.wait_ge(out_free, at("out_free", ready))
                if k >= 4:
                    act.wait_ge(sq_used, at("sq_used", (key, k - 3)))
                A(square_of(k), xT[:, k * S:(k + 1) * S], ACT.Square).then_inc(sq_ready, tick("sq_ready", (key, k)))

            def root(key):
                act.wait_ge(sums_ready, at("sums_ready", key))
                A(root_t[:], ps[:, 4, 0:NT], ACT.Sqrt, bias=epst[:, 0:1], scale=1.0 / D).then_inc(
                    act_ready, tick("act_ready", (key, "root")))

            def blocks_and_squares(b, nk, key, ready):
                done = 0
                preload(ACT.Sqrt)
                for k in range(KD):
                    while (done + 1) * TILES <= nk * (k + 1) and k < KD - 1:
                        split_block(b + done + 2)
                        done += 1
                    square(key, k, ready(k))
                root(key)
                while done < nk * KD // TILES:
                    split_block(b + done + 2)
                    done += 1

            def attend(br):
                us_ = units[br]
                for n, (_, h, part, i, m) in enumerate(us_):
                    u = (br, n)
                    sbuf, w = SP4[n % 4], unit_width(br, part, i)
                    act.wait_ge(sb_ready, at("sb_ready", u))
                    if part == 2 and br == BR_D:
                        A(sbuf[:, 0:w], sbuf[:, 0:w], ACT.Exp, scale=slope(br, h)).then_inc(p_ready, tick("p_ready", u))
                    else:
                        A(sbuf[:, 0:w], sbuf[:, 0:w], ACT.Exp, scale=-1.0, bias=negm[:, n % 8:n % 8 + 1],
                          accum_out=lsum[:, m % 4 * 4 + i:m % 4 * 4 + i + 1]).then_inc(p_ready, tick("p_ready", u))
                    if n >= 1:
                        spread(br, n - 1)
                spread(br, len(us_) - 1)

            def attend_pairs():
                n_g = len(units[BR_A]) // 2
                for g in range(n_g + 1):
                    if g < n_g:
                        for n in (2 * g, 2 * g + 1):
                            _, h, part, i, m = units[BR_A][n]
                            sbuf = SP6[n % 6][:, 0:P * (i + 1)]
                            act.wait_ge(sb_ready, at("sb_ready", (BR_A, n)))
                            c = map_sums(h, part) + i
                            A(sbuf, sbuf, ACT.Exp, scale=-1.0, bias=negm[:, n % 8:n % 8 + 1], accum_out=lsum[:, c:c + 1]).then_inc(
                                p_ready, tick("p_ready", (BR_A, n)))
                    if g >= 1:
                        spread(BR_A, g - 1, P * (units[BR_A][2 * g - 2][3] + 1))

            def spread(br, n, w=None):
                _, h, part, i, m = units[br][n]
                w = w or unit_width(br, part, i)
                act.wait_ge(t_ready, at("t_ready", (br, n)))
                if n >= 2:
                    act.wait_ge(pv_done, at("pv_done", (br, n), -2))
                if br == BR_D and part == 2:
                    src, dst = ps[0:NCMP, 4 + n % 2, 0:S], PT2[n % 2][0:NCMP, :]
                else:
                    src, dst = ps[:, 4 + n % 2, 0:w], PT2[n % 2][:, 0:w]
                A(dst, src, ACT.Copy).then_inc(pt_ready, tick("pt_ready", (br, n)))

            act.dma_start(y[:, 0:L * 256], dlam).then_inc(lam_in, 16)
            act.wait_ge(f_ready, at("f_ready", "lam"))
            A(neglam[:, 4:8], neglam[:, 4:8], ACT.Exp).then_inc(act_ready, tick("act_ready", "lam"))
            act.wait_ge(dve_chain, at("dve_chain", "eps"))
            preload(ACT.Sqrt)
            for k in range(KD):
                square("x", k, ("x", k))
            act.wait_ge(landed[0], 16)
            A(w_hi[0][:], raw[0][:], ACT.Copy).then_inc(hi_done, 1)
            root("x")
            act.wait_ge(landed[1], 16)
            A(w_hi[1][:], raw[1][:], ACT.Copy).then_inc(hi_done, 1)

            with en.layers(act):
                for k in range(KD):
                    split_hi(h_hi[:, k * S:(k + 1) * S], norm_buf[k % 4], ("n1", k))
                split_hi(sw_hi[:], vecs_slice(vecs, en.layer, V_SW, KD * SWC), "sw", computed=False)
                blocks(B_A, 5)
                preload(ACT.Exp)
                blocks(B_A + 5, 1)
                attend_pairs()
                act.wait_ge(f_ready, at("f_ready", "subln"))
                A(fz[:, 32:48], fz[:, 32:48], ACT.Sqrt, bias=epst[:, 0:1], scale=1.0 / P).then_inc(
                    act_ready, tick("act_ready", "subln"))
                blocks(B_LAT, 2)
                for key, j in (("ckv", 1), ("cq", 0)):
                    for c in range(2):
                        act.wait_ge(out_free, at("out_free", (key, c)))
                        if key == "cq":
                            act.wait_ge(misc_ready, at("misc_ready", ("ckv", "n", c)))
                        A(SP4[c], cfl[:, (2 * j + c) * S:(2 * j + c + 1) * S], ACT.Square).then_inc(
                            sq_ready, tick("sq_ready", (key, c)))
                for key, j in (("ckv", 1), ("cq", 0)):
                    if key == "cq":
                        blocks(B_C, 1)
                    act.wait_ge(misc_ready, at("misc_ready", (key, "n", 1)))
                    if key == "cq":
                        act.wait_ge(f_split, at("f_split", ("ckv", 1)))
                    A(SP4[2], ps[:, bank(en, (key, "n")), :], ACT.Sqrt, bias=epst[:, 0:1], scale=1.0 / 256).then_inc(
                        act_ready, tick("act_ready", (key, "root")))
                    for c in range(2):
                        split_hi(cn_hi[j][:, c * S:(c + 1) * S], PT2[c], (key, c))
                blocks(B_C + 1, 1)
                act.wait_ge(f_ready, at("f_ready", "tok"))
                A(dgate[:], dgate[:], ACT.Sigmoid).then_inc(act_ready, tick("act_ready", "dgate"))
                A(fz[:, 16:32], fz[:, 16:32], ACT.Exp, scale=-1.0).then_inc(act_chain, tick("act_chain"))
                act.wait_ge(act_chain, en.mine("act_chain"))
                A(fz[:, 16:32], fz[:, 16:32], ACT.Ln, bias=ones[:, 0:1]).then_inc(act_ready, tick("act_ready", "flog"))
                blocks(B_C + 2, 3)
                preload(ACT.Exp)
                blocks(B_C + 5, 1)
                attend(BR_C)
                blocks(B_B, 2)
                attend(BR_B)
                blocks(B_D, 1)
                act.wait_ge(out_free, at("out_free", ("yT", BR_B, 3)))
                for j in range(2):
                    split_hi(z_hi[j][:], z[j], ("z", j))
                blocks(B_D + 1, 1)
                for j in range(2):
                    blocks(B_D + 2 + 2 * j, 1)
                    act.wait_ge(gemm_steps, at("gemm_steps", ("hid", j)))
                    A(hid_t[0:62, j * P:(j + 1) * P], ps[0:62, bank(en, ("hid", j)), 0:P], ACT.Gelu_apprx_tanh).then_inc(
                        act_ready, tick("act_ready", ("hid", j)))
                    if j:
                        preload(ACT.Exp)
                    blocks(B_D + 3 + 2 * j, 1)
                attend(BR_D)
                en.loop_blocks = 12
                with en.turns(act, "gate", 2) as g:
                    for j in range(2):
                        split_block(B_GATE + 6 * j + 1)
                        for c in range(4):
                            act.wait_ge(out_free, at("out_free", ("yT", BR_D, 3)))
                            act.wait_ge(gemm_steps, at("gemm_steps", ("gate", j, 7, 1), -12 * STEPS))
                            A(y_hi[j][:, c * S:(c + 1) * S], yT[:, bass.ds((g * 2 + j) * 4 * S + c * S, S)], ACT.Copy).then_inc(
                                f_hi, tick("f_hi", ("y", j, c)))
                        done = 0
                        for dt in range(8):
                            act.wait_ge(gemm_steps, at("gemm_steps", ("gate", j, dt, 0)))
                            act.wait_ge(f_ready, at("f_ready", ("mul", j, dt), -2))
                            A(sg[dt % 2], ps[:, bank(en, ("gate", j, dt, 0)), :], ACT.Sigmoid).then_inc(
                                act_ready, tick("act_ready", ("sg", j, dt)))
                            while (done + 1) * TILES <= 12 * (dt + 1) and dt < 7:
                                split_block(B_GATE + 6 * j + done + 2)
                                done += 1
                for k in range(KD):
                    act.wait_ge(out_free, at("out_free", ("gate", 1, k, 1)))
                    A(m_hi[:, k * S:(k + 1) * S], merged[:, k * S:(k + 1) * S], ACT.Copy).then_inc(
                        f_hi, tick("f_hi", ("m", k)))
                split_block(B_OUT + 1)
                blocks_and_squares(B_OUT, KD, "n2", lambda k: ("wo", k))
                for k in range(KD):
                    split_hi(h_hi[:, k * S:(k + 1) * S], norm_buf[k % 4], ("n2", k))
                b = B_MLP
                for half, (c0, nch) in enumerate(HALVES):
                    en.loop_blocks = 2
                    with en.turns(act, ("up", half), nch // 2) as g:
                        for j in range(2):
                            for part, dst in ((0, ua[j]), (1, ug[j])):
                                act.wait_ge(gemm_steps, at("gemm_steps", ("up", half, j, part)))
                                act.wait_ge(f_ready, at("f_ready", ("act", half, j), -2))
                                cv = V_CONV + (part * FFC + c0 + j) * 4
                                A(dst, ps[:, bank(en, ("up", half, j, part)), :], ACT.Identity,
                                  bias=col(vecs, en.layer, cv + 3, g, 8), scale=col(vecs, en.layer, cv + 2, g, 8)).then_inc(
                                    act_ready, tick("act_ready", ("up", half, j, part)))
                            split_block(b + j + 2)
                            act.wait_ge(out_free, at("out_free", ("up", half, j, 0)))
                            A(us[j], ua[j], ACT.Silu).then_inc(act_ready, tick("act_ready", ("silu", half, j)))
                            act.wait_ge(f_ready, at("f_ready", ("act", half, j)))
                            A(a_hi[:, bass.ds((g * 2 + j) * S, S)], uf[j], ACT.Copy).then_inc(
                                f_hi, tick("f_hi", ("act", half, j)))
                    b += nch
                    if half == 0:
                        blocks(b, nch // 2)
                    else:
                        blocks_and_squares(b, nch, "n1", lambda k: ("down", 1, k))
                    b += nch // 2

        @block.vector
        def _(dve):
            en = Engine(counts)
            tick, at = en.tick, en.at
            V = nc.vector

            def link(ins):
                ins.then_inc(dve_chain, tick("dve_chain"))
                dve.wait_ge(dve_chain, en.mine("dve_chain"))

            def lo_part(dst, src, hi, key):
                dve.wait_ge(f_hi, at("f_hi", key))
                V.tensor_tensor(dst, src, hi.bitcast(F32), ALU.subtract).then_inc(f_split, tick("f_split", key))

            def evac(key, dst, scale=1.0, srcs=None, ready="gemm_steps"):
                sem_ = {"gemm_steps": gemm_steps, "misc_ready": misc_ready}[ready]
                dve.wait_ge(sem_, at(ready, key))
                src = ps[:, bank(en, key), :]
                parts = [(dst, src)] if srcs is None else [(d, f(src)) for d, f in srcs]
                for n, (d, s) in enumerate(parts):
                    ins = V.tensor_scalar(d, s, scale, None, ALU.mult)
                    if n == len(parts) - 1:
                        ins.then_inc(out_free, tick("out_free", key))

            eye = ident.rearrange("p (o d) -> p o d", o=1).to_broadcast([P, NT, P])

            def spread_scales(key):
                link(V.reciprocal(root_t[:], root_t[:]))
                r = root_t[:].rearrange("p (t o) -> p t o", o=1).to_broadcast([P, NT, P])
                V.tensor_tensor(SP4[2].rearrange("p (t d) -> p t d", t=NT), eye, r, ALU.mult).then_inc(
                    diag_ready, tick("diag_ready", key))
                dve.wait_ge(sums_ready, at("sums_ready", (key, "spread")))

            def normalise(key, root, nk, src, gain, dsts):
                dve.wait_ge(act_ready, at("act_ready", (root, "root")))
                bufs = PT2 if nk < KD else norm_buf
                nb = len(bufs)
                scale = ps[:, 5, :] if nk == KD else SP4[3]
                if nk == KD:
                    spread_scales(key)
                else:
                    V.reciprocal(SP4[3], SP4[2]).then_inc(out_free, tick("out_free", (key, "n")))
                    dve.wait_ge(out_free, en.mine("out_free"))
                for k in range(nk + 1):
                    if k < nk:
                        if nk < KD:
                            dve.wait_ge(f_split, en.mine("f_split"))
                        elif k >= nb:
                            dve.wait_ge(f_split, at("f_split", (key, k - nb)))
                        V.scalar_tensor_tensor(bufs[k % nb], src(k), gain(k), scale, ALU.mult, ALU.mult).then_inc(
                            f_ready, tick("f_ready", (key, k)))
                    if k >= 1:
                        hi, lo = dsts(k - 1)
                        lo_part(lo, bufs[(k - 1) % nb], hi, (key, k - 1))

            def attend(br):
                us_ = units[br]
                ends = {}
                for n, (_, h, part, i, m) in enumerate(us_):
                    if n + 1 == len(us_) or us_[n + 1][4] != m:
                        ends[n] = (h, part, m)
                for n in range(len(us_) + BEHIND):
                    if n < len(us_):
                        piece(br, n)
                    if n - 3 in ends and br == BR_D and ends[n - 3][1] == 2:
                        compressed_sums(br, n - 3, ends[n - 3][2])
                    if n - BEHIND in ends:
                        map_out(br, n - BEHIND, *ends[n - BEHIND])

            def attend_pairs():
                n_g = len(units[BR_A]) // 2
                for g in range(n_g + 3):
                    if g < n_g:
                        if g >= 3:
                            dve.wait_ge(mixed_ready, at("mixed_ready", g - 3))
                        piece(BR_A, 2 * g)
                        piece(BR_A, 2 * g + 1)
                    if 1 <= g <= n_g:
                        mix(g - 1)
                    if g >= 3 and (g - 3) % NT == NT - 1:
                        pairs_out(g - 3)
                subln()

            def mix(g):
                _, h, _, i, _ = units[BR_A][2 * g]
                w = P * (i + 1)
                c1, c2 = map_sums(h, 0) + i, map_sums(h, 1) + i
                inv, f = rinv[:, 8 + 2 * (g % 2):9 + 2 * (g % 2)], rinv[:, 9 + 2 * (g % 2):10 + 2 * (g % 2)]
                dve.wait_ge(p_ready, at("p_ready", (BR_A, 2 * g + 1)))
                link(V.reciprocal(inv, lsum[:, c2:c2 + 1]))
                link(V.tensor_scalar(f, inv, lsum[:, c1:c1 + 1], neglam[:, bass.ds(en.layer, 1)], ALU.mult, ALU.mult))
                if g >= 2:
                    dve.wait_ge(t_ready, at("t_ready", (BR_A, g), -2))
                V.scalar_tensor_tensor(mixed[g % 2][:, 0:w], SP6[(2 * g + 1) % 6][:, 0:w], f, SP6[2 * g % 6][:, 0:w],
                                       ALU.mult, ALU.add).then_inc(mixed_ready, tick("mixed_ready", g))

            def pairs_out(g):
                h = units[BR_A][2 * g][1]
                c = map_sums(h, 0)
                r = rinv[:, h % 2 * 4:h % 2 * 4 + 4]
                link(V.reciprocal(r, lsum[:, c:c + 4]))
                dve.wait_ge(pv_done, at("pv_done", (BR_A, g)))
                V.tensor_tensor(head_rows(y, h, P), out_rows(h, P), rows_of(r, P), ALU.mult).then_inc(o_free, tick("o_free", h))
                dve.wait_ge(o_free, en.mine("o_free"))

            def out_rows(m, wd):
                return ps[:, 6 + m % 2, 0:NT * wd].rearrange("p (t d) -> p t d", t=NT)

            def rows_of(r, wd):
                return r.rearrange("p (t o) -> p t o", o=1).to_broadcast([P, NT, wd])

            def head_rows(t, h, wd):
                return t.rearrange("p (t d) -> p t d", t=NT)[:, :, h * wd:(h + 1) * wd]

            def keep_y(br):
                for c in range(4):
                    key = ("yT", br, c)
                    evac(key, yT[:, (br * 4 + c) * S:(br * 4 + c + 1) * S], ready="misc_ready")

            def piece(br, n):
                _, h, part, i, m = units[br][n]
                w = unit_width(br, part, i)
                dst, src = (SP6[n % 6] if br == BR_A else SP4[n % 4])[:, 0:w], ps[:, n % 4, 0:w]
                dve.wait_ge(s_ready, at("s_ready", (br, n)))
                if n >= 4 and br != BR_A:
                    dve.wait_ge(t_ready, at("t_ready", (br, n), -4))
                if br == BR_D and part == 2:
                    cm = negm_c
                    link(V.tensor_tensor(dst, src, cst[:, C_NDC:C_NDC + NT * NCMP], ALU.add))
                    d3 = dst.rearrange("p (t c) -> p t c", t=NT)
                    link(V.tensor_reduce(cm, d3, AX.X, ALU.max))
                    V.tensor_tensor(d3, d3, cm.rearrange("p (t o) -> p t o", o=1).to_broadcast([P, NT, NCMP]), ALU.subtract).then_inc(
                        sb_ready, tick("sb_ready", (br, n)))
                    return
                if br == BR_A:
                    bias = cst[:, C_ND + S - w:C_ND + S]
                elif br == BR_B:
                    bias = cst[:, C_CM + S - w:C_CM + S]
                elif br == BR_C:
                    bias = negc[:, h * S:h * S + w]
                elif part == 0:
                    bias = cst[:, C_ND + S - w:C_ND + S]
                else:
                    bias = cst[:, C_NDW + 384 - w:C_NDW + 384]
                dve.sem_inc(dve_chain, tick("dve_chain"))
                V.tensor_tensor_reduce(dst, src, bias, -slope(br, h), 3e38, ALU.add, ALU.min, negm[:, n % 8:n % 8 + 1]).then_inc(
                    sb_ready, tick("sb_ready", (br, n)))

            negm_c = fz[:, 48:52]

            def compressed_sums(br, n, m):
                dve.wait_ge(p_ready, at("p_ready", (br, n)))
                pc = SP4[n % 4][:, 0:NT * NCMP].rearrange("p (t c) -> p t c", t=NT)
                link(V.tensor_reduce(lsum[:, m % 4 * 4:m % 4 * 4 + 4], pc, AX.X, ALU.add))

            def map_out(br, n, h, part, m):
                r = rinv[:, m % 4 * 4:m % 4 * 4 + 4]
                ls = lsum[:, m % 4 * 4:m % 4 * 4 + 4]
                dve.wait_ge(p_ready, at("p_ready", (br, n)))
                link(V.reciprocal(r, ls))
                if br == BR_D:
                    g = dgate[:].rearrange("p (t c) -> p t c", t=NT)[:, :, 3 * h + (1, 2, 0)[part]]
                    link(V.tensor_tensor(r, r, g, ALU.mult))
                    if part == 2:
                        link(V.tensor_tensor(r, r, cst[:, C_ROW:C_ROW + NT], ALU.mult))
                wd = NSA_D if br == BR_D else P
                ob, rb, yh = out_rows(m, wd), rows_of(r, wd), head_rows(y, h, wd)
                dve.wait_ge(pv_done, at("pv_done", (br, n)))
                if part == 0:
                    V.tensor_tensor(yh, ob, rb, ALU.mult).then_inc(o_free, tick("o_free", m))
                    dve.wait_ge(o_free, en.mine("o_free"))
                else:
                    t3 = tmp[:, 0:NT * wd].rearrange("p (t d) -> p t d", t=NT)
                    V.tensor_tensor(t3, ob, rb, ALU.mult).then_inc(o_free, tick("o_free", m))
                    dve.wait_ge(o_free, en.mine("o_free"))
                    link(V.tensor_tensor(yh, yh, t3, ALU.add))
                if n == len(units[br]) - 1:
                    dve.sem_inc(f_ready, tick("f_ready", ("y", br)))

            def subln():
                y4 = y.rearrange("p (t h d) -> p t h d", t=NT, h=HEADS)
                for h in range(HEADS):
                    t3 = tmp.rearrange("p (t d) -> p t d", t=NT)
                    link(V.tensor_tensor(t3, y4[:, :, h, :], y4[:, :, h, :], ALU.mult))
                    ins = V.tensor_reduce(fz[:, 32 + 4 * h:36 + 4 * h], t3, AX.X, ALU.add)
                    if h < HEADS - 1:
                        link(ins)
                    else:
                        ins.then_inc(f_ready, tick("f_ready", "subln"))
                dve.wait_ge(act_ready, at("act_ready", "subln"))
                link(V.reciprocal(fz[:, 32:48], fz[:, 32:48]))
                link(V.tensor_scalar(fz[:, 32:48], fz[:, 32:48], neglam[:, bass.ds(en.layer + L, 1)], None, ALU.mult))
                g = vecs_slice(vecs, en.layer, V_SUB, P)
                for h in range(HEADS):
                    r = fz[:, 32 + 4 * h:36 + 4 * h].rearrange("p (t o) -> p t o", o=1).to_broadcast([P, NT, P])
                    link(V.tensor_tensor(y4[:, :, h, :], y4[:, :, h, :], r, ALU.mult))
                    gb = g.rearrange("p (o d) -> p o d", o=1).to_broadcast([P, NT, P])
                    ins = V.tensor_tensor(y4[:, :, h, :], y4[:, :, h, :], gb, ALU.mult)
                    if h < HEADS - 1:
                        link(ins)
                    else:
                        ins.then_inc(f_ready, tick("f_ready", ("y", BR_A)))

            def rotary(raw_t, rot_key, dsts, rows=P):
                link(V.tensor_tensor(SP4[1][0:rows, :], raw_t[0:rows, :], cos[0:rows, :], ALU.mult))
                dve.wait_ge(misc_ready, at("misc_ready", rot_key))
                V.tensor_tensor(SP4[2][0:rows, :], ps[0:rows, bank(en, rot_key), :], sin[0:rows, :], ALU.mult).then_inc(out_free, tick("out_free", rot_key))
                dve.wait_ge(out_free, en.mine("out_free"))
                for d, part in dsts:
                    link(V.tensor_tensor(d, SP4[1][part, :], SP4[2][part, :], ALU.add))

            def add_out(key, k):
                dve.wait_ge(gemm_steps, at("gemm_steps", key))
                xk = xT[:, k * S:(k + 1) * S]
                V.tensor_tensor(xk, ps[:, bank(en, key), :], xk, ALU.add).then_inc(out_free, tick("out_free", key))

            def add_squares(key, k):
                if k >= 2:
                    dve.wait_ge(sq_ready, at("sq_ready", (key, k - 1)))
                    if k >= 3:
                        dve.wait_ge(sq_used, en.mine("sq_used"))
                    V.tensor_tensor(sq_sum, sq_sum, square_of(k - 1), ALU.add).then_inc(sq_used, tick("sq_used", (key, k - 1)))

            def norm(key, root, gain):
                normalise(key, root, KD, lambda k: xT[:, k * S:(k + 1) * S], gain,
                          lambda k: (h_hi[:, k * S:(k + 1) * S], h_lo[:, k * S:(k + 1) * S]))

            dve.sem_inc(out_free, tick("out_free", "credit", 4))
            dve.sem_inc(o_free, tick("o_free", "credit", 2))
            V.memset(epst[:], EPS).then_inc(dve_chain, tick("dve_chain", "eps"))
            dve.wait_ge(dve_chain, en.mine("dve_chain"))
            dve.wait_ge(lam_in, 16)
            dl = y[:, 0:L * 256].rearrange("p (l f d) -> p l f d", l=L, f=4)
            for a in range(2):
                pr = tmp[:, a * 128:(a + 1) * 128].rearrange("p (l d) -> p l d", l=L)
                link(V.tensor_tensor(pr, dl[:, :, 2 * a, :], dl[:, :, 2 * a + 1, :], ALU.mult))
                ins = V.tensor_reduce(neglam[:, 4 + 2 * a:6 + 2 * a], pr, AX.X, ALU.add)
                if a == 0:
                    link(ins)
                else:
                    ins.then_inc(f_ready, tick("f_ready", "lam"))
            for k in range(KD):
                evac(("x", k), xT[:, k * S:(k + 1) * S], ready="misc_ready")
                add_squares("x", k)
            dve.wait_ge(ident_in, 16)
            dve.wait_ge(act_ready, at("act_ready", "lam"))
            link(V.tensor_tensor(neglam[:, 0:2], neglam[:, 6:8], neglam[:, 4:6], ALU.subtract))
            lam0 = cst[:, C_LAM:C_LAM + L]
            link(V.tensor_tensor(neglam[:, 0:2], neglam[:, 0:2], lam0, ALU.subtract))
            link(V.tensor_scalar(neglam[:, 2:4], lam0, -1.0, 1.0, ALU.mult, ALU.add))

            dve.wait_ge(small_in, 16)
            with en.layers(dve):
                nmix = lambda k: col(vecs, en.layer, V_NM + k)
                norm("n1", "x", nmix)
                lo_part(sw_lo[:], vecs_slice(vecs, en.layer, V_SW, KD * SWC), sw_hi[:], "sw")

                def token_scalars():
                    dve.wait_ge(misc_ready, at("misc_ready", "tok"))
                    tok = ps[:, bank(en, "tok"), 0:NT * 28].rearrange("p (t c) -> p t c", t=NT)
                    z4 = fz[:, 0:16].rearrange("p (t h) -> p t h", t=NT)
                    bf = vecs_slice(vecs, en.layer, V_BF, HEADS).rearrange("p (o h) -> p o h", o=1).to_broadcast([P, NT, HEADS])
                    link(V.tensor_tensor(z4, tok[:, :, 0:4], bf, ALU.add))
                    V.tensor_copy(dgate[:].rearrange("p (t c) -> p t c", t=NT), tok[:, :, 4:28]).then_inc(out_free, tick("out_free", "tok"))
                    link(V.tensor_scalar(fz[:, 16:32], fz[:, 0:16], -1.0, None, ALU.mult))
                    V.tensor_tensor(fz[:, 16:32], fz[:, 16:32], fz[:, 0:16], ALU.max).then_inc(f_ready, tick("f_ready", "tok"))

                def fm(br, scale, t):
                    cols = slice(t % 4 * S, (t % 4 + 1) * S)
                    if br == BR_A and t < 4:
                        evac((br, "fm", t), None, scale / slope(br, t), [
                            (q_[0:64, cols], lambda s: s[0:64, :]), (q2_[64:128, cols], lambda s: s[64:128, :])])
                    else:
                        evac((br, "fm", t), (q_ if t < 4 else k_)[:, cols], scale if t < 4 else 1.0)

                V.memset(q_[64:128, :], 0.0).then_inc(dve_chain, tick("dve_chain"))
                V.memset(q2_[0:64, :], 0.0).then_inc(dve_chain, tick("dve_chain"))
                for t in range(7):
                    fm(BR_A, 64 ** -0.5, t)
                dve.wait_ge(const_in, 48)
                evac("kr", None, srcs=[(SP4[0][0:SWC, :], lambda s: s[0:SWC, :])], ready="misc_ready")
                fm(BR_A, 64 ** -0.5, 7)
                dve.wait_ge(out_free, at("out_free", "kr"))
                rotary(SP4[0], "krrot", [(kpe[0:64, :], slice(0, 64))], ROPE)
                token_scalars()
                for t in range(NT):
                    evac((BR_A, "v", t), v_[:, t * S:(t + 1) * S])
                attend_pairs()
                for j, key in enumerate(("cq", "ckv")):
                    for c in range(2):
                        evac((key, c), cfl[:, (2 * j + c) * S:(2 * j + c + 1) * S])
                keep_y(BR_A)
                for t in range(8):
                    fm(BR_C, P ** -0.5, t)
                    if t == 5:
                        dve.wait_ge(act_ready, at("act_ready", "flog"))
                        link(V.tensor_scalar(fz[:, 0:16], fz[:, 0:16], 0.0, None, ALU.min))
                        V.tensor_tensor(fz[:, 0:16], fz[:, 16:32], fz[:, 0:16], ALU.subtract).then_inc(f_ready, tick("f_ready", "logs"))
                    if t < 2:
                        j, key, vg = ((1, "ckv", V_NKV), (0, "cq", V_NQ))[t]
                        normalise(key, key, 2, lambda c: cfl[:, (2 * j + c) * S:(2 * j + c + 1) * S],
                                  lambda c: col(vecs, en.layer, vg + c),
                                  lambda c: (cn_hi[j][:, c * S:(c + 1) * S], cn_lo[j][:, c * S:(c + 1) * S]))
                evac("cum", None, srcs=[(fz[:, 48:64], lambda s: s[:, 0:NT * HEADS])], ready="misc_ready")
                dve.wait_ge(out_free, en.mine("out_free"))

                def diagonals(h):
                    c = fz[:, 48:64].rearrange("p (t h) -> p t h", t=NT)[:, :, h:h + 1].to_broadcast([P, NT, P])
                    V.tensor_tensor(nlfb[h % 2].rearrange("p (t d) -> p t d", t=NT), eye, c, ALU.mult).then_inc(
                        f_ready, tick("f_ready", ("nlf", h)))

                diagonals(0)
                diagonals(1)
                for t in range(NT):
                    evac((BR_C, "v", t), v_[:, t * S:(t + 1) * S])
                for h in range(HEADS):
                    evac(("negc", h), negc[:, h * S:(h + 1) * S], ready="misc_ready")
                    if h + 2 < HEADS:
                        diagonals(h + 2)
                dve.wait_ge(out_free, en.mine("out_free"))
                attend(BR_C)
                scale = (128 + 64) ** -0.5
                for h in range(HEADS):
                    evac(("bq", h), bq[:, h * S:(h + 1) * S], scale)
                keep_y(BR_C)
                for pr in range(2):
                    evac(("bqp", pr), SP4[0] if pr == 0 else SP4[3], scale)
                dve.wait_ge(f_split, en.mine("f_split"))
                dve.wait_ge(out_free, en.mine("out_free"))
                for pr in range(2):
                    rotary(SP4[0] if pr == 0 else SP4[3], ("bqrot", pr),
                           [(bqp[0:64, (2 * pr + e) * S:(2 * pr + e + 1) * S], slice(64 * e, 64 * e + 64)) for e in range(2)])
                for h in range(HEADS):
                    evac(("bk", h), bk[:, h * S:(h + 1) * S])
                for t in range(NT):
                    evac(("bv", t), bv[:, t * S:(t + 1) * S])
                attend(BR_B)
                for j in range(2):
                    key = ("dc", j)
                    dve.wait_ge(gemm_steps, at("gemm_steps", key))
                    pe = vecs_slice(vecs, en.layer, V_PE + 16 * j, 16)
                    zz = z[j].rearrange("p (l g c) -> p l g c", l=16, g=2)
                    for g in range(2):
                        for e in range(2):
                            rows = slice(64 * e, 64 * e + 64)
                            src = ps[64 * g:64 * g + 64, bank(en, key), :]
                            for half in range(2):
                                s3 = src[:, 16 * half:16 * half + 16 * NCMP].rearrange("p (c l e) -> p l e c", l=8, e=2)[:, :, e, :]
                                d3 = zz[rows, 8 * half:8 * half + 8, g, :]
                                pb = pe[rows, 8 * half:8 * half + 8].rearrange("p (l o) -> p l o", o=1).to_broadcast([64, 8, NCMP])
                                ins = V.tensor_tensor(d3, s3, pb, ALU.add)
                                if g + e + half == 3:
                                    ins.then_inc(out_free, tick("out_free", key))
                                else:
                                    ins.then_inc(dve_chain, tick("dve_chain"))
                    dve.wait_ge(dve_chain, en.mine("dve_chain"))
                    dve.wait_ge(out_free, en.mine("out_free"))
                    dve.sem_inc(f_ready, tick("f_ready", ("z", j)))
                evac("dks", dks)
                keep_y(BR_B)
                lo_part(z_lo[0][:], z[0], z_hi[0][:], ("z", 0))
                evac("dkw", dkw)
                lo_part(z_lo[1][:], z[1], z_hi[1][:], ("z", 1))
                V.memset(dq[64:128, 0:4 * S], 0.0).then_inc(dve_chain, tick("dve_chain"))
                V.memset(dq[0:64, 4 * S:8 * S], 0.0).then_inc(dve_chain, tick("dve_chain"))
                link(V.tensor_copy(w2c, vecs_slice(vecs, en.layer, V_W2, P)))

                def queries(t):
                    key = ("dq", t)
                    dve.wait_ge(gemm_steps, at("gemm_steps", key))
                    for g in range(NSA_G):
                        hd, rows = t + 4 * g, slice(64 * g, 64 * g + 64)
                        ins = V.tensor_scalar(dq[rows, hd * S:(hd + 1) * S], ps[rows, bank(en, key), :],
                                              NSA_D ** -0.5 / slope(BR_D, hd), None, ALU.mult)
                    ins.then_inc(out_free, tick("out_free", key))

                for j in range(2):
                    dve.wait_ge(out_free, en.mine("out_free"))
                    dve.wait_ge(act_ready, at("act_ready", ("hid", j)))
                    dve.sem_inc(out_free, tick("out_free", ("hid", j)))
                    queries(2 * j)
                    if j:
                        dve.wait_ge(misc_ready, at("misc_ready", "hidt"))
                        V.tensor_copy(hid, ps[:, bank(en, "hidt"), 0:124]).then_inc(out_free, tick("out_free", "hidt"))
                    queries(2 * j + 1)
                evac("kc", None, srcs=[(kc[:, 0:NCMP], lambda s: s[:, 0:NCMP])], ready="misc_ready")
                evac("vc", None, srcs=[(vc[0:NCMP, :], lambda s: s[0:NCMP, 0:128])], ready="misc_ready")
                for t in range(NT):
                    evac(("dv", t), dv[:, t * 256:(t + 1) * 256], srcs=[(dv[:, t * 256:(t + 1) * 256], lambda s: s[:, 0:256])])
                attend(BR_D)
                keep_y(BR_D)
                dve.wait_ge(out_free, en.mine("out_free"))
                V.memset(merged, 0.0).then_inc(dve_chain, tick("dve_chain", "merged"))
                with en.turns(dve, "gate", 2) as g:
                    for j in range(2):
                        for c in range(4):
                            dve.wait_ge(f_hi, at("f_hi", ("y", j, c)))
                            V.tensor_tensor(y_lo[j][:, c * S:(c + 1) * S], yT[:, bass.ds((g * 2 + j) * 4 * S + c * S, S)],
                                            y_hi[j][:, c * S:(c + 1) * S].bitcast(F32), ALU.subtract).then_inc(
                                f_split, tick("f_split", ("y", j, c)))
                        dve.wait_ge(dve_chain, at("dve_chain", "merged"))
                        for dt in range(8):
                            dve.wait_ge(act_ready, at("act_ready", ("sg", j, dt)))
                            dve.sem_inc(out_free, tick("out_free", ("gate", j, dt, 0)))
                            dve.wait_ge(gemm_steps, at("gemm_steps", ("gate", j, dt, 1)))
                            V.tensor_tensor(tmp, ps[:, bank(en, ("gate", j, dt, 1)), :], sg[dt % 2], ALU.mult).then_inc(
                                f_ready, tick("f_ready", ("mul", j, dt)))
                            dve.wait_ge(f_ready, en.mine("f_ready"))
                            mk = merged[:, dt * S:(dt + 1) * S]
                            V.tensor_tensor(mk, mk, tmp, ALU.add).then_inc(out_free, tick("out_free", ("gate", j, dt, 1)))
                            dve.wait_ge(out_free, en.mine("out_free"))
                for k in range(KD):
                    lo_part(m_lo[:, k * S:(k + 1) * S], merged[:, k * S:(k + 1) * S], m_hi[:, k * S:(k + 1) * S], ("m", k))
                for k in range(KD):
                    add_squares("n2", k)
                    add_out(("wo", k), k)
                dve.wait_ge(out_free, en.mine("out_free"))
                norm("n2", "n2", lambda k: col(vecs, en.layer, V_NF + k))
                for half, (c0, nch) in enumerate(HALVES):
                    with en.turns(dve, ("up", half), nch // 2) as g:
                        for j in range(2):
                            for tap in (1, 0):
                                for part, dst in ((0, ua[j]), (1, ug[j])):
                                    key = ("up", half, j, part)
                                    cv = V_CONV + (part * FFC + c0 + j) * 4
                                    if tap == 1:
                                        dve.wait_ge(act_ready, at("act_ready", key))
                                    else:
                                        dve.wait_ge(dve_chain, at("dve_chain", key))
                                    cols = dst[:, 2 - tap:S]
                                    ins = V.scalar_tensor_tensor(cols, ps[:, bank(en, key), 0:S - 2 + tap],
                                                                 col(vecs, en.layer, cv + tap, g, 8), cols, ALU.mult, ALU.add)
                                    if tap == 1:
                                        ins.then_inc(dve_chain, tick("dve_chain", key))
                                    else:
                                        ins.then_inc(out_free, tick("out_free", key))
                            dve.wait_ge(out_free, en.mine("out_free"))
                            dve.wait_ge(act_ready, at("act_ready", ("silu", half, j)))
                            dve.wait_ge(f_split, at("f_split", ("act", half, j), -2))
                            V.tensor_tensor(uf[j], us[j], ug[j], ALU.mult).then_inc(f_ready, tick("f_ready", ("act", half, j)))
                            dve.wait_ge(f_hi, at("f_hi", ("act", half, j)))
                            V.tensor_tensor(a_lo[:, bass.ds((g * 2 + j) * S, S)], uf[j],
                                            a_hi[:, bass.ds((g * 2 + j) * S, S)].bitcast(F32), ALU.subtract).then_inc(
                                f_split, tick("f_split", ("act", half, j)))
                    for k in range(KD):
                        if half:
                            add_squares("n1", k)
                        add_out(("down", half, k), k)
                dve.wait_ge(act_ready, at("act_ready", ("n1", "root")))
                pad = -counts.now["out_free"] % 4
                if pad:
                    dve.sem_inc(out_free, tick("out_free", "pad", pad))
            dve.wait_ge(act_ready, en.after("act_ready", ("n1", "root")))
            spread_scales("n3")
            for k in range(KD):
                xk = xT[:, k * S:(k + 1) * S]
                V.scalar_tensor_tensor(xk, xk, nf[:, k:k + 1], ps[:, 5, :], ALU.mult, ALU.mult).then_inc(f_ready, tick("f_ready", ("n3", k)))
            for t in range(NT):
                for half in range(2):
                    dve.wait_ge(misc_ready, at("misc_ready", ("o", t, half)))
                    V.tensor_copy(stage[:, t * D + half * S:t * D + (half + 1) * S], ps[:, bank(en, ("o", t, half)), :]).then_inc(
                        out_ready, tick("out_ready", (t, half)))
                    dve.wait_ge(out_ready, en.mine("out_ready"))
                    dve.sem_inc(out_free, tick("out_free", ("o", t, half)))

        @block.tensor
        def _(pe):
            en = Engine(counts)
            tick, at = en.tick, en.at
            MM = nc.tensor.matmul

            def three(dst, a, b, start, stop):
                MM(dst, a[0], b[0], start=start, stop=False)
                MM(dst, a[0], b[1], start=False, stop=False)
                return MM(dst, a[1], b[0], start=False, stop=stop)

            def free_bank(key):
                pe.wait_ge(out_free, at("out_free", key, -4))
                return ps[:, bank(en, key), :]

            def step(ins, key=None, by=1):
                ins.then_inc(gemm_steps, tick("gemm_steps", key, by))

            def enter_block(b):
                n = b + 1
                if en.loop is not None:
                    n = en.turn * en.loop_blocks + n
                pe.wait_ge(lo_done, en.layer * NBLK + n)

            def columns(dsts, weights, x, k, nk, waits):
                if waits is not None:
                    waits(k, "hi")
                for dst, w in zip(dsts, weights):
                    MM(dst, w[0], x[0], start=k == 0, stop=False)
                    MM(dst, w[1], x[0], start=False, stop=False)
                if waits is not None:
                    waits(k, "lo")
                for dst, w in zip(dsts, weights):
                    ins = MM(dst, w[0], x[1], start=False, stop=k == nk - 1)
                return ins

            def parts_of(key):
                def wait(k, part):
                    if part == "hi":
                        pe.wait_ge(f_hi, at("f_hi", key + (k,)))
                    else:
                        pe.wait_ge(f_split, at("f_split", key + (k,)))
                return wait

            def gemm(b, t0, key, rhs, nk, waits=None, padding=0):
                dst = free_bank(key)
                for k in range(nk):
                    t = t0 + k
                    if t % TILES == 0:
                        enter_block(b + t // TILES)
                    ins = columns([dst], [wt(b, t)], rhs(k), k, nk, waits)
                    last = k == nk - 1
                    if t % 2 == 1:
                        step(ins, key if last else None, 1 + (padding if last else 0))

            def gemm_pair(b, keys, waits=None):
                dsts = [free_bank(key) for key in keys]
                for k in range(KD):
                    if k == 0:
                        enter_block(b)
                    ins = columns(dsts, [wt(b, KD * j + k) for j in range(2)], h(k), k, KD, waits)
                    step(ins, keys[1])
                counts.base["gemm_steps", keys[0]] = counts.base["gemm_steps", keys[1]]

            def h(k):
                return h_hi[:, k * S:(k + 1) * S], h_lo[:, k * S:(k + 1) * S]

            def hcols(k, t):
                c = k * S + t * P
                return h_hi[:, c:c + P], h_lo[:, c:c + P]

            def misc(ins, key):
                ins.then_inc(misc_ready, tick("misc_ready", key))

            def sum_squares(key):
                for k, src in ((KD - 2, sq_sum), (KD - 1, square_of(KD - 1))):
                    if k < KD - 1:
                        pe.wait_ge(sq_used, at("sq_used", (key, k)))
                    else:
                        pe.wait_ge(sq_ready, at("sq_ready", (key, k)))
                    for t in range(NT):
                        ins = MM(ps[:, 4, t:t + 1], src[:, t * P:(t + 1) * P], ones[:, 0:1],
                                 start=k == KD - 2 and t == 0, stop=k == KD - 1 and t == NT - 1)
                ins.then_inc(sums_ready, tick("sums_ready", key))

            def spread_scales(key):
                pe.wait_ge(diag_ready, at("diag_ready", key))
                MM(ps[:, 5, :], ones, SP4[2], start=True, stop=True).then_inc(sums_ready, tick("sums_ready", (key, "spread")))

            def onto_residual(b, key, rhs, nk, norm_key=None, waits=None):
                for dt in range(KD):
                    gemm(b, nk * dt, key + (dt,), rhs, nk, waits=waits if dt == 0 else None)
                if norm_key:
                    sum_squares(norm_key)

            def values(b, key, width, nk_block, lhs, nblocks):
                keys = [key + (t,) for t in range(NT)]
                dsts = {}
                total = nblocks * nk_block
                per_step = NT * nk_block // STEPS
                for bb in range(nblocks):
                    enter_block(b + bb)
                    s = (b + bb) % 2
                    for t in range(NT):
                        if bb == 0:
                            dsts[t] = free_bank(keys[t])[:, 0:width]
                        for kk in range(nk_block):
                            k = bb * nk_block + kk
                            w = (w_hi[s][:, kk * width:(kk + 1) * width], w_lo[s][:, kk * width:(kk + 1) * width])
                            ins = three(dsts[t], lhs(k, t), w, k == 0, k == total - 1)
                            g = t * nk_block + kk
                            if (g + 1) % per_step == 0:
                                step(ins, keys[t] if k == total - 1 else None)

            def scores(br, n):
                _, hd, part, i, m = units[br][n]
                w = unit_width(br, part, i)
                dst = ps[:, n % 4, 0:w]
                qs = slice(hd * S + i * P, hd * S + (i + 1) * P)
                if br == BR_A:
                    ins = MM(dst, (q_, q2_)[part][:, qs], k_[:, hd * S:hd * S + w], start=True, stop=True)
                elif br == BR_C:
                    MM(dst, q_[:, qs], k_[:, hd * S:hd * S + w], start=True, stop=False)
                    ins = MM(dst[:, w - P:w], ident, cst[:, C_CM + 3 * P:C_CM + 4 * P], start=False, stop=True)
                elif br == BR_B:
                    MM(dst, bq[:, qs], bk[:, hd * S:hd * S + w], start=True, stop=False)
                    ins = MM(dst, bqp[0:64, qs], kpe[0:64, 0:w], start=False, stop=True)
                else:
                    g = hd // 4
                    if part == 2:
                        for ii in range(NT):
                            ins = MM(dst[:, ii * NCMP:(ii + 1) * NCMP], dq[:, hd * S + ii * P:hd * S + (ii + 1) * P],
                                     kc[:, 0:NCMP], start=True, stop=True)
                    else:
                        kk = dks if part == 0 else dkw
                        e = (i + 1) * P
                        ins = MM(dst, dq[:, qs], kk[:, e - w:e], start=True, stop=True)
                ins.then_inc(s_ready, tick("s_ready", (br, n)))

            def turn(br, n):
                _, hd, part, i, m = units[br][n]
                pe.wait_ge(p_ready, at("p_ready", (br, n)))
                pt = ps[:, 4 + n % 2, :]
                if br == BR_D and part == 2:
                    for ii in range(NT):
                        ins = nc.tensor.transpose(pt[0:NCMP, ii * P:(ii + 1) * P], SP4[n % 4][:, ii * NCMP:(ii + 1) * NCMP], ident)
                else:
                    for j in range(unit_width(br, part, i) // P):
                        ins = nc.tensor.transpose(pt[:, j * P:(j + 1) * P], SP4[n % 4][:, j * P:(j + 1) * P], ident)
                ins.then_inc(t_ready, tick("t_ready", (br, n)))

            def weigh(br, n):
                values_of(br, n, *units[br][n][1:])

            def values_of(br, n, hd, part, i, m):
                pe.wait_ge(pt_ready, at("pt_ready", (br, n)))
                if first_of_map(br, n):
                    pe.wait_ge(o_free, at("o_free", m, -2))
                ob = ps[:, 6 + m % 2, :]
                pt = PT2[n % 2]
                if br == BR_D:
                    g = hd // 4
                    if part == 2:
                        for ii in range(NT):
                            ins = MM(ob[:, ii * NSA_D:(ii + 1) * NSA_D], pt[0:NCMP, ii * P:(ii + 1) * P],
                                     vc[0:NCMP, g * NSA_D:(g + 1) * NSA_D], start=True, stop=True)
                    else:
                        nb = unit_width(br, part, i) // P
                        for jj in range(nb):
                            j = i + 1 - nb + jj
                            c = j * 256 + part * 128 + g * NSA_D
                            ins = MM(ob[:, i * NSA_D:(i + 1) * NSA_D], pt[:, jj * P:(jj + 1) * P], dv[:, c:c + NSA_D],
                                     start=jj == 0, stop=jj == nb - 1)
                else:
                    vv = bv if br == BR_B else v_
                    for j in range(i + 1):
                        ins = MM(ob[:, i * P:(i + 1) * P], pt[:, j * P:(j + 1) * P], vv[:, j * S + hd * P:j * S + (hd + 1) * P],
                                 start=j == 0, stop=j == i)
                ins.then_inc(pv_done, tick("pv_done", (br, n)))

            def attend(br, last_out):
                n_u = len(units[br])
                pe.wait_ge(out_free, at("out_free", last_out))
                for n in range(AHEAD):
                    scores(br, n)
                for n in range(n_u + 1):
                    if n < n_u:
                        turn(br, n)
                    if n + AHEAD < n_u:
                        scores(br, n + AHEAD)
                    if n >= 1:
                        weigh(br, n - 1)

            def attend_pairs(last_out):
                n_g = len(units[BR_A]) // 2
                pe.wait_ge(out_free, at("out_free", last_out))
                for n in range(4):
                    scores(BR_A, n)
                for g in range(n_g + 1):
                    for n in range(2 * g + 4, min(2 * g + 6, 2 * n_g)):
                        pe.wait_ge(sb_ready, at("sb_ready", (BR_A, n - 4)))
                        scores(BR_A, n)
                    if g >= 1:
                        values_of(BR_A, g - 1, *units[BR_A][2 * g - 2][1:])
                    if g < n_g:
                        _, h, _, i, _ = units[BR_A][2 * g]
                        pe.wait_ge(mixed_ready, at("mixed_ready", g))
                        for j in range(i + 1):
                            ins = nc.tensor.transpose(ps[:, 4 + g % 2, j * P:(j + 1) * P], mixed[g % 2][:, j * P:(j + 1) * P], ident)
                        ins.then_inc(t_ready, tick("t_ready", (BR_A, g)))

            def turn_y(br):
                pe.wait_ge(f_ready, at("f_ready", ("y", br)))
                for c in range(4):
                    key = ("yT", br, c)
                    dst = free_bank(key)
                    for t in range(NT):
                        ins = nc.tensor.transpose(dst[:, t * P:(t + 1) * P], y[:, t * S + c * P:t * S + (c + 1) * P], ident)
                    misc(ins, key)

            pe.wait_ge(ident_in, 16)
            for k in range(KD):
                pe.wait_ge(x_part_in[k // 2], 16)
                dst = free_bank(("x", k))
                for t in range(NT):
                    ins = nc.tensor.transpose(dst[:, t * P:(t + 1) * P], stage[:, t * D + k * P:t * D + (k + 1) * P], ident)
                misc(ins, ("x", k))
            sum_squares("x")

            with en.layers(pe):
                spread_scales("n1")
                sw = lambda c, w: (sw_hi[:, c:c + w], sw_lo[:, c:c + w])
                gemm_pair(B_A, [(BR_A, "fm", t) for t in range(2)], parts_of(("n1",)))
                for t in range(2, 7):
                    gemm(B_A, 8 * t, (BR_A, "fm", t), h, KD)
                dst = free_bank("kr")
                pe.wait_ge(f_split, at("f_split", "sw"))
                for k in range(KD):
                    ins = three(dst[0:SWC, :], sw(k * SWC, SWC), h(k), k == 0, k == KD - 1)
                misc(ins, "kr")
                gemm(B_A, 56, (BR_A, "fm", 7), h, KD)
                dst, dst_tok = free_bank("krrot"), free_bank("tok")
                pe.wait_ge(out_free, at("out_free", "kr"))
                misc(MM(dst, rot[0:ROPE, :], SP4[0][0:ROPE, :], start=True, stop=True), "krrot")
                for t in range(NT):
                    ins = nc.tensor.transpose(dst_tok[:, t * 28:(t + 1) * 28], SP4[0][ROPE:SWC, t * P:(t + 1) * P], ident[ROPE:SWC, ROPE:SWC])
                misc(ins, "tok")
                values(B_A + 4, (BR_A, "v"), S, 4, hcols, 2)
                attend_pairs((BR_A, "v", NT - 1))
                for j, key in enumerate(("cq", "ckv")):
                    for c in range(2):
                        gemm(B_LAT + j, 8 * c, (key, c), h, KD)
                turn_y(BR_A)
                for t in range(8):
                    gemm(B_C, 8 * t, (BR_C, "fm", t), h, KD)
                    if t < 2:
                        key = ("ckv", "cq")[t]
                        dst = free_bank((key, "n"))
                        for c in range(2):
                            pe.wait_ge(sq_ready, at("sq_ready", (key, c)))
                            misc(MM(dst, ones, SP4[c], start=c == 0, stop=c == 1), (key, "n", c))
                dst = free_bank("cum")
                pe.wait_ge(f_ready, at("f_ready", "logs"))
                for t in range(NT):
                    for before in range(t + 1):
                        ins = MM(dst[:, t * HEADS:(t + 1) * HEADS], tri if before == t else ones,
                                 fz[:, before * HEADS:(before + 1) * HEADS], start=t == 0, stop=t == before == NT - 1)
                misc(ins, "cum")
                values(B_C + 4, (BR_C, "v"), S, 4, hcols, 2)
                for hd in range(HEADS):
                    dst = free_bank(("negc", hd))
                    pe.wait_ge(f_ready, at("f_ready", ("nlf", hd)))
                    misc(MM(dst, ones, nlfb[hd % 2], start=True, stop=True), ("negc", hd))
                attend(BR_C, ("negc", HEADS - 1))
                lat = lambda j: (lambda c: (cn_hi[j][:, c * S:(c + 1) * S], cn_lo[j][:, c * S:(c + 1) * S]))
                pe.wait_ge(f_split, at("f_split", ("cq", 1)))
                for t in range(6):
                    key = ("bq", t) if t < 4 else ("bqp", t - 4)
                    gemm(B_B, 2 * t, key, lat(0), 2, padding=2 if t == 5 else 0)
                    if t == 3:
                        turn_y(BR_C)
                for pr in range(2):
                    dst = free_bank(("bqrot", pr))
                    pe.wait_ge(out_free, at("out_free", ("bqp", pr)))
                    misc(MM(dst, rot, SP4[0] if pr == 0 else SP4[3], start=True, stop=True), ("bqrot", pr))
                pe.wait_ge(f_split, at("f_split", ("ckv", 1)))
                for t in range(4):
                    gemm(B_B + 1, 2 * t, ("bk", t), lat(1), 2)
                s = (B_B + 1) % 2
                for t in range(NT):
                    dst = free_bank(("bv", t))
                    for k in range(2):
                        c = 8 * P + k * S
                        lhs = (cn_hi[1][:, k * S + t * P:k * S + (t + 1) * P], cn_lo[1][:, k * S + t * P:k * S + (t + 1) * P])
                        ins = three(dst, lhs, (w_hi[s][:, c:c + S], w_lo[s][:, c:c + S]), k == 0, k == 1)
                    step(ins, ("bv", t))
                attend(BR_B, ("bv", NT - 1))
                for t, key in enumerate((("dc", 0), ("dc", 1), "dks", "dkw")):
                    gemm(B_D, 8 * t, key, h, KD)
                    if t == 2:
                        turn_y(BR_B)
                for j in range(2):
                    pe.wait_ge(f_split, at("f_split", ("z", j)))
                    dst = free_bank(("hid", j))[0:2 * NCMP, 0:P]
                    for half in range(2):
                        b = B_D + 2 + 2 * j + half
                        enter_block(b)
                        for k in range(8):
                            kk = 8 * half + k
                            c = slice(kk * 2 * NCMP, (kk + 1) * 2 * NCMP)
                            ins = three(dst, (z_hi[j][:, c], z_lo[j][:, c]), wt(b, k), kk == 0, kk == TILES - 1)
                            if k % 2:
                                step(ins, ("hid", j))
                        if j == half == 1:
                            hid_turned = free_bank("hidt")
                            for e in range(2):
                                pe.wait_ge(act_ready, at("act_ready", ("hid", e)))
                                ins = MM(hid_turned[:, e * 62:(e + 1) * 62], hid_t[0:62, e * P:(e + 1) * P], ident[0:62, 0:62],
                                         start=True, stop=True)
                            misc(ins, "hidt")
                        gemm(b, 8, ("dq", 2 * j + half), h, KD)
                dst = free_bank("kc")
                pe.wait_ge(out_free, at("out_free", "hidt"))
                for g in range(2):
                    ins = MM(dst[64 * g:64 * g + 64, 0:NCMP], w2c[:, 0:64], hid[:, g * NCMP:(g + 1) * NCMP], start=True, stop=True)
                misc(ins, "kc")
                dst = free_bank("vc")
                for g in range(2):
                    ins = MM(dst[0:NCMP, g * 64:(g + 1) * 64], hid[:, 62 + g * NCMP:62 + (g + 1) * NCMP], w2c[:, 64:128], start=True, stop=True)
                misc(ins, "vc")
                values(B_D + 6, ("dv",), 256, 8, hcols, 1)
                attend(BR_D, ("dv", NT - 1))
                turn_y(BR_D)
                en.loop_blocks = 12
                with en.turns(pe, "gate", 2):
                    for j in range(2):
                        ys = lambda c: (y_hi[j][:, c * S:(c + 1) * S], y_lo[j][:, c * S:(c + 1) * S])
                        for dt in range(8):
                            t0 = 96 * j + 12 * dt
                            gemm(B_GATE, t0, ("gate", j, dt, 0), h, KD)
                            gemm(B_GATE, t0 + 8, ("gate", j, dt, 1), ys, 4, parts_of(("y", j)) if dt == 0 else None)
                mm = lambda k: (m_hi[:, k * S:(k + 1) * S], m_lo[:, k * S:(k + 1) * S])
                onto_residual(B_OUT, ("wo",), mm, KD, "n2", parts_of(("m",)))
                spread_scales("n2")
                b = B_MLP
                for half, (c0, nch) in enumerate(HALVES):
                    en.loop_blocks = 2
                    with en.turns(pe, ("up", half), nch // 2):
                        for j in range(2):
                            gemm_pair(b + j, [("up", half, j, part) for part in range(2)],
                                      parts_of(("n2",)) if half == j == 0 else None)
                    b += nch
                    aa = lambda k: (a_hi[:, k * S:(k + 1) * S], a_lo[:, k * S:(k + 1) * S])

                    def gated(k, part, half=half, nch=nch):
                        if k == 0 and part == "hi":
                            pe.wait_ge(f_split, at("f_split", ("act", half, 0), -1))
                        elif k >= nch - 2:
                            parts_of(("act", half))(k - nch + 2, part)
                    onto_residual(b, ("down", half), aa, nch, "n1" if half else None, gated)
                    b += nch // 2
            spread_scales("n3")
            for t in range(NT):
                for half in range(2):
                    dst = free_bank(("o", t, half))
                    for c in range(4):
                        k = half * 4 + c
                        pe.wait_ge(f_ready, at("f_ready", ("n3", k)))
                        ins = nc.tensor.transpose(dst[:, c * P:(c + 1) * P], xT[:, k * S + t * P:k * S + (t + 1) * P], ident)
                    misc(ins, ("o", t, half))

    return counts


def vecs_slice(vecs, layer, c, n):
    return vecs[:, bass.ds(layer * NV + c, n)]


def col(vecs, layer, c, turn=None, per_turn=0):
    at = layer * NV + c
    if turn is not None:
        at = turn * per_turn + at
    return vecs[:, bass.ds(at, 1)]


def slope(br, h):
    return {BR_A: 2.0 ** (-8 * (h + 1) // HEADS), BR_D: 2.0 ** (-8 * (h + 1) // NSA_H)}.get(br, 1.0)


def first_of_map(br, n):
    units = attention_units()[br]
    if br == BR_A:
        n *= 2
    return n == 0 or units[n - 1][4] != units[n][4]


def map_sums(h, part):
    return (h % 2 * 2 + part) * NT


def unit_width(br, part, i):
    if br == BR_D and part == 2:
        return NT * NCMP
    if br == BR_D and part == 1:
        return P * min(i + 1, WIN // P + 1)
    return P * (i + 1)


def _tiles(w):
    k, n = w.shape
    return w.reshape(k // P, P, n // P, P).transpose(2, 0, 1, 3).reshape(-1, P, P)


def _blocks(tiles):
    return tiles.reshape(-1, TILES, P, P).transpose(0, 2, 1, 3).reshape(-1, P, BLK)


def _wide(w, k):
    n = w.shape[1]
    return w.reshape(-1, k, P, n).transpose(0, 2, 1, 3).reshape(-1, P, k * n)


def _hidden_queries(w1, dq):
    w1 = w1.reshape(4, 8, P, P)
    return _blocks(np.concatenate([w1, dq.reshape(4, 8, P, P)], axis=1).reshape(-1, P, P))


def _weights(i, l):
    w = i["w_in"][l]
    cuts = np.cumsum([512, 512, 512, 256, 256, 64, 512, 512, 512, 4, 512, 768, 24])
    aq, ak, av, cq, ckv, kr, fq, fk, fv, cf, dq, dkv, dg, gate = np.split(w, cuts, axis=1)
    fm = lambda *ws: _blocks(_tiles(np.concatenate(ws, axis=1)))
    dq = dq.reshape(D, NSA_G, NSA_H // NSA_G, NSA_D).transpose(0, 2, 1, 3).reshape(D, -1)
    uq = i["mla_w_uq"][l].reshape(256, HEADS, 192)
    ukv = i["mla_w_ukv"][l].reshape(256, HEADS, 256)
    t = _tiles(np.concatenate([uq[:, :, :P].reshape(256, -1), uq[:, :, P:].reshape(256, -1)], axis=1))
    uq = _blocks(np.concatenate([t, np.zeros((4, P, P), np.float32)]))
    kn = _tiles(ukv[:, :, :P].reshape(256, 512)).transpose(1, 0, 2).reshape(P, 8 * P)
    vv = _wide(ukv[:, :, P:].reshape(256, 512), 2)[0]
    ukv = np.concatenate([kn, vv], axis=1)[None]
    k = dkv.reshape(D, 3, 2, P)
    parts = [fm(aq, ak), _wide(av, 4), fm(cq, ckv), fm(fq, fk), _wide(fv, 4), uq, ukv,
             fm(k[:, 0, 0], k[:, 0, 1], k[:, 1, 0], k[:, 2, 0]), _hidden_queries(i["nsa_cmp_w1"][l], _tiles(dq)),
             _wide(np.concatenate([k[:, 1, 1], k[:, 2, 1]], axis=1), 8)]
    tiles = []
    for n in range(4):
        g, b = _tiles(gate[:, n * D:(n + 1) * D]), _tiles(i["w_branch"][l, n])
        for dt in range(8):
            tiles += [g[dt * 8:dt * 8 + 8], b[dt * 4:dt * 4 + 4]]
    parts += [_blocks(np.concatenate(tiles)), fm(i["w_out"][l])]
    up = _tiles(i["w_up"][l]).reshape(2, FFC, 8, P, P).transpose(1, 0, 2, 3, 4)
    for c0, n in HALVES:
        parts.append(_blocks(up[c0:c0 + n].reshape(-1, P, P)))
        parts.append(_blocks(_tiles(i["w_down"][l, c0 * P:(c0 + n) * P])))
    return np.concatenate(parts)


def _small(i, l):
    v = np.zeros((P, NV), np.float32)
    feat = lambda a: np.ascontiguousarray(a.reshape(-1, P).T)
    v[:, V_NM:V_NM + 8] = feat(i["norm_mix"][l])
    v[:, V_NF:V_NF + 8] = feat(i["norm_ffn"][l])
    v[:, V_NQ:V_NQ + 2] = feat(i["mla_norm_q"][l])
    v[:, V_NKV:V_NKV + 2] = feat(i["mla_norm_kv"][l])
    conv = np.concatenate([i["conv_w"][l], i["conv_b"][l][None]])
    v[:, V_CONV:V_SW] = conv.reshape(4, 2 * FFC, P).transpose(2, 1, 0).reshape(P, -1)
    w = i["w_in"][l]
    kr, cf, dg = w[:, 2048:2112], w[:, 3648:3652], w[:, 4932:4956]
    v[:, V_SW:V_W2] = np.concatenate([kr, cf, dg], axis=1).reshape(KD, P, SWC).transpose(1, 0, 2).reshape(P, -1)
    v[:, V_W2:V_PE] = np.concatenate([i["nsa_cmp_w2"][l, 0], i["nsa_cmp_w2"][l, 1]], axis=1)
    v[:, V_PE:V_SUB] = i["nsa_cmp_pe"][l].reshape(2, 16, P).transpose(2, 0, 1).reshape(P, 32)
    v[:, V_SUB:V_BF] = i["diff_subln"][l][None]
    v[:, V_BF:] = i["fox_b_f"][l][None]
    return v


def _constants():
    c = np.zeros((P, NCONST), np.float32)
    p = np.arange(P)[:, None]
    c[:, C_ID:C_ID + P] = np.eye(P)
    c[:, C_TRI:C_TRI + 2 * P] = np.arange(2 * P)[None] >= p
    dist = p - (np.arange(S)[None] - 3 * P)
    c[:, C_ND:C_ND + S] = np.where(dist >= 0, -dist, NEG)
    c[:, C_CM:C_CM + S] = np.where(dist >= 0, 0, NEG)
    dist = p - (np.arange(3 * P)[None] - WIN)
    c[:, C_NDW:C_NDW + 3 * P] = np.where((dist >= 0) & (dist < WIN), -dist, NEG)
    pos = np.arange(NT)[None, :, None] * P + p[:, :, None]
    dist = pos - (np.arange(NCMP)[None, None] * 16 + 31)
    c[:, C_NDC:C_NDC + NT * NCMP] = np.where(dist >= 0, -dist, NEG).reshape(P, -1)
    c[:, C_ROW:C_ROW + NT] = (dist >= 0).any(axis=2)
    f32 = np.float32
    inv = f32(10000.0) ** (-np.arange(0, 64, 2, dtype=f32) / f32(64))
    ang = (np.arange(S, dtype=f32)[None] * inv[:, None]).astype(f32)
    c[:, C_COS:C_COS + S] = np.tile(np.cos(ang.astype(np.float64)), (4, 1))
    c[:, C_SIN:C_SIN + S] = np.tile(np.sin(ang.astype(np.float64)), (4, 1))
    for b in (0, 64):
        for m in range(32):
            c[b + m + 32, C_ROT + b + m] = -1.0
            c[b + m, C_ROT + b + m + 32] = 1.0
    c[:, C_LAM:C_LAM + L] = [0.8 - 0.6 * math.exp(-0.3 * l) for l in range(L)]
    return c


def kernel(**inputs):
    import concourse.bacc as _bacc
    from concourse.bass_utils import run_bass_kernel_spmd as _run

    i = {k: np.asarray(v) for k, v in inputs.items()}
    arrays = {
        "blob": np.concatenate([_weights(i, l) for l in range(L)]),
        "vec": np.stack([_small(i, l) for l in range(L)]),
        "const": _constants(),
        "dlam": np.ascontiguousarray(np.broadcast_to(i["diff_lambda"].reshape(1, -1), (P, L * 256))),
        "nfin": np.ascontiguousarray(i["norm_final"].reshape(KD, P).T),
        "x_in": np.ascontiguousarray(i["x"][0]),
    }

    def program(known):
        nc = _bacc.Bacc("TRN2", target_bir_lowering=False, num_devices=1)
        args = [nc.dram_tensor(n, a.shape, F32, kind="ExternalInput").ap() for n, a in arrays.items()]
        out = nc.dram_tensor("out", (S, D), F32, kind="ExternalOutput").ap()
        return nc, build(nc, *args, out, known)

    _, known = program(None)
    nc, _ = program(known)
    r = _run(nc, [arrays], core_ids=[0])
    return r.results[0]["out"].reshape(1, S, D)
```
